# Optimizing a Trainium2 kernel written in Bass

```python
import jax, jax.numpy as jnp
from jax import lax
import numpy as np

D_MODEL = 1024
BATCH = 1
SEQ = 512
DEPTH = 1

GRID_W = 64
D_CONV = 512
CONV_K = 31
NA_HEADS = 8
NA_HEAD_DIM = 64
D_NA = NA_HEADS * NA_HEAD_DIM
D_IN = 2 * D_CONV + 3 * D_NA
D_MIX = D_CONV + D_NA
WIN_H = 8
WIN_W = 16
QB = WIN_W
KBW = 2 * WIN_W
N_COL_BLOCKS = GRID_W // QB
N_EXPERTS = 32
TOP_K = 4
D_FF = D_MODEL
SWIGLU_LIMIT = 7.0
SWIGLU_ALPHA = 1.702
MOE_BLOCK = 128
EPS = 1e-5

kernel_name = "hybrid_conformer_conv_natten2d_moe_encoder"

def rmsnorm(x, g):
    xf = x.astype(jnp.float32)
    y = xf * lax.rsqrt(jnp.mean(xf * xf, axis=-1, keepdims=True) + EPS) * g.astype(jnp.float32)
    return y.astype(x.dtype)

def conformer_conv(a, g, conv_w, conv_b, ln_g, ln_b):
    u = a * jax.nn.sigmoid(g)
    u = lax.conv_general_dilated(
        u, conv_w[:, None, :].astype(u.dtype), window_strides=(1,),
        padding=[(CONV_K // 2, CONV_K // 2)],
        dimension_numbers=("NWC", "WIO", "NWC"),
        feature_group_count=D_CONV) + conv_b
    uf = u.astype(jnp.float32)
    mu = jnp.mean(uf, axis=-1, keepdims=True)
    var = jnp.mean(jnp.square(uf - mu), axis=-1, keepdims=True)
    un = (uf - mu) * lax.rsqrt(var + EPS) * ln_g.astype(jnp.float32) + ln_b.astype(jnp.float32)
    return jax.nn.silu(un).astype(a.dtype)

def neighbourhood_attention(q, k, v, rpb):
    B, S, H, Dh = q.shape
    rows = S // GRID_W
    kh = min(WIN_H, rows)
    scale = Dh ** -0.5
    qg = q.reshape(B, rows, N_COL_BLOCKS, QB, H, Dh)
    kg = k.reshape(B, rows, GRID_W, H, Dh)
    vg = v.reshape(B, rows, GRID_W, H, Dh)

    col = jnp.arange(GRID_W, dtype=jnp.int32).reshape(N_COL_BLOCKS, QB)
    c0 = jnp.clip(col - WIN_W // 2, 0, GRID_W - WIN_W)
    blk_start = jnp.clip(jnp.arange(N_COL_BLOCKS, dtype=jnp.int32) * QB - WIN_W // 2, 0, GRID_W - KBW)
    key_col = blk_start[:, None] + jnp.arange(KBW, dtype=jnp.int32)[None, :]
    col_valid = (key_col[:, None, :] >= c0[:, :, None]) & (key_col[:, None, :] < c0[:, :, None] + WIN_W)
    dcol_idx = jnp.clip(key_col[:, None, :] - col[:, :, None], -(WIN_W - 1), WIN_W - 1) + (WIN_W - 1)
    valid = col_valid[None, :, None, :, None, :]

    def row_fn(args):
        i, q_row = args
        r0 = jnp.clip(i - kh // 2, 0, rows - kh)
        k_slab = lax.dynamic_slice_in_dim(kg, r0, kh, axis=1)
        v_slab = lax.dynamic_slice_in_dim(vg, r0, kh, axis=1)
        k_blk = k_slab[:, :, key_col]
        v_blk = v_slab[:, :, key_col]
        s = jnp.einsum("bnqhd,brnkhd->bnhqrk", q_row, k_blk,
                       preferred_element_type=jnp.float32) * scale
        drow_idx = r0 + jnp.arange(kh, dtype=jnp.int32) - i + (WIN_H - 1)
        bias = rpb[:, drow_idx[None, None, :, None], dcol_idx[:, :, None, :]]
        s = s + jnp.moveaxis(bias, 0, 1)[None].astype(jnp.float32)
        s = jnp.where(valid, s, jnp.float32(-1e30))
        p = jax.nn.softmax(s.reshape(B, N_COL_BLOCKS, H, QB, kh * KBW), axis=-1)
        p = p.reshape(B, N_COL_BLOCKS, H, QB, kh, KBW).astype(v.dtype)
        return jnp.einsum("bnhqrk,brnkhd->bnqhd", p, v_blk)

    out = lax.map(row_fn, (jnp.arange(rows, dtype=jnp.int32), jnp.moveaxis(qg, 1, 0)))
    return jnp.moveaxis(out, 0, 1).reshape(B, S, H * Dh)

def mixer(xn, w_in, b_in, conv_w, conv_b, ln_g, ln_b, rpb, w_out, b_out):
    B, S, _ = xn.shape
    proj = jnp.einsum("bsd,de->bse", xn, w_in) + b_in
    glu_a, glu_g, q, k, v = jnp.split(
        proj, [D_CONV, 2 * D_CONV, 2 * D_CONV + D_NA, 2 * D_CONV + 2 * D_NA], axis=-1)
    conv_out = conformer_conv(glu_a, glu_g, conv_w, conv_b, ln_g, ln_b)
    na_out = neighbourhood_attention(q.reshape(B, S, NA_HEADS, NA_HEAD_DIM),
                                     k.reshape(B, S, NA_HEADS, NA_HEAD_DIM),
                                     v.reshape(B, S, NA_HEADS, NA_HEAD_DIM), rpb)
    mixed = jnp.concatenate([conv_out, na_out], axis=-1)
    return jnp.einsum("bse,ed->bsd", mixed, w_out) + b_out

def moe(xn, w_router, b_router, w_gate, b_gate, w_up, b_up, w_down, b_down):
    B, S, D = xn.shape
    T = B * S
    xt = xn.reshape(T, D)
    logits = (xt @ w_router + b_router).astype(jnp.float32)
    top_vals, top_idx = lax.top_k(logits, TOP_K)
    gates = jax.nn.softmax(top_vals, axis=-1)
    tk = T * TOP_K
    exp_flat = top_idx.reshape(tk)
    tok_flat = jnp.arange(tk, dtype=jnp.int32) // TOP_K
    gate_flat = gates.reshape(tk)
    order = jnp.argsort(exp_flat)
    s_exp, s_tok, s_gate = exp_flat[order], tok_flat[order], gate_flat[order]
    sizes = jnp.bincount(exp_flat, length=N_EXPERTS).astype(jnp.int32)
    offsets = jnp.cumsum(sizes) - sizes
    padded = (sizes + MOE_BLOCK - 1) // MOE_BLOCK * MOE_BLOCK
    pad_ends = jnp.cumsum(padded)
    pad_offsets = pad_ends - padded
    dest = pad_offsets[s_exp] + jnp.arange(tk, dtype=jnp.int32) - offsets[s_exp]
    cap = tk + N_EXPERTS * MOE_BLOCK
    n_blocks = cap // MOE_BLOCK
    tok_pad = jnp.zeros((cap,), jnp.int32).at[dest].set(s_tok)
    gate_pad = jnp.zeros((cap,), jnp.float32).at[dest].set(s_gate)
    blk_exp = jnp.minimum(
        jnp.searchsorted(pad_ends, jnp.arange(n_blocks, dtype=jnp.int32) * MOE_BLOCK, side="right"),
        N_EXPERTS - 1).astype(jnp.int32)
    x_blocks = xt[tok_pad].reshape(n_blocks, MOE_BLOCK, D)

    def expert_block(args):
        xb, e = args
        gt = jnp.minimum(xb @ w_gate[e] + b_gate[e], SWIGLU_LIMIT)
        up = jnp.clip(xb @ w_up[e] + b_up[e], -SWIGLU_LIMIT, SWIGLU_LIMIT)
        hdn = (up + 1.0) * (gt * jax.nn.sigmoid(SWIGLU_ALPHA * gt))
        return hdn @ w_down[e] + b_down[e]

    y = lax.map(expert_block, (x_blocks, blk_exp)).reshape(cap, D)
    y = y * gate_pad[:, None].astype(y.dtype)
    out = jax.ops.segment_sum(y, tok_pad, num_segments=T)
    return out.reshape(B, S, D)

def setup_inputs(seed: int = 0) -> dict:
    key = jax.random.key(seed)
    ks = jax.random.split(key, 22)

    def nrm(k, shape, scale):
        return jax.random.normal(k, shape, jnp.float32) * scale

    return {
        "x": nrm(ks[0], (BATCH, SEQ, D_MODEL), 1.0),
        "g_mix": 1.0 + nrm(ks[1], (DEPTH, D_MODEL), 0.02),
        "w_in": nrm(ks[2], (DEPTH, D_MODEL, D_IN), D_MODEL ** -0.5),
        "b_in": nrm(ks[3], (DEPTH, D_IN), 0.01),
        "conv_w": nrm(ks[4], (DEPTH, CONV_K, D_CONV), CONV_K ** -0.5),
        "conv_b": nrm(ks[5], (DEPTH, D_CONV), 0.01),
        "ln_g": 1.0 + nrm(ks[6], (DEPTH, D_CONV), 0.02),
        "ln_b": nrm(ks[7], (DEPTH, D_CONV), 0.01),
        "rpb": nrm(ks[8], (DEPTH, NA_HEADS, 2 * WIN_H - 1, 2 * WIN_W - 1), 0.02),
        "w_out": nrm(ks[9], (DEPTH, D_MIX, D_MODEL), D_MIX ** -0.5),
        "b_out": nrm(ks[10], (DEPTH, D_MODEL), 0.01),
        "g_ffn": 1.0 + nrm(ks[11], (DEPTH, D_MODEL), 0.02),
        "w_router": nrm(ks[12], (DEPTH, D_MODEL, N_EXPERTS), D_MODEL ** -0.5),
        "b_router": nrm(ks[13], (DEPTH, N_EXPERTS), 0.01),
        "w_gate": nrm(ks[14], (DEPTH, N_EXPERTS, D_MODEL, D_FF), D_MODEL ** -0.5),
        "b_gate": nrm(ks[15], (DEPTH, N_EXPERTS, D_FF), 0.01),
        "w_up": nrm(ks[16], (DEPTH, N_EXPERTS, D_MODEL, D_FF), D_MODEL ** -0.5),
        "b_up": nrm(ks[17], (DEPTH, N_EXPERTS, D_FF), 0.01),
        "w_down": nrm(ks[18], (DEPTH, N_EXPERTS, D_FF, D_MODEL), D_FF ** -0.5),
        "b_down": nrm(ks[19], (DEPTH, N_EXPERTS, D_MODEL), 0.01),
        "g_final": 1.0 + nrm(ks[20], (D_MODEL,), 0.02),
    }

def reference(x, g_mix, w_in, b_in, conv_w, conv_b, ln_g, ln_b, rpb, w_out, b_out,
              g_ffn, w_router, b_router, w_gate, b_gate, w_up, b_up, w_down, b_down, g_final):
    h = x
    for l in range(DEPTH):
        xn = rmsnorm(h, g_mix[l])
        h = h + mixer(xn, w_in[l], b_in[l], conv_w[l], conv_b[l], ln_g[l], ln_b[l],
                      rpb[l], w_out[l], b_out[l])
        xn = rmsnorm(h, g_ffn[l])
        h = h + moe(xn, w_router[l], b_router[l], w_gate[l], b_gate[l], w_up[l], b_up[l],
                    w_down[l], b_down[l])
    return rmsnorm(h, g_final)


_drawn_inputs = setup_inputs


def setup_inputs(seed=0):
    import zlib

    import numpy as np

    out = dict(_drawn_inputs(seed))
    spreads = {}
    factors = {'ln_b': 4.794,
     'rpb': 4.608,
     'b_gate': 8.0,
     'b_up': 8.0,
     'b_down': 8.0,
     'g_final': 8.702,
     'b_in': 2.667}
    for name, (base, spread) in spreads.items():
        noise = np.random.default_rng([zlib.crc32(name.encode()), seed]).standard_normal(out[name].shape)
        drawn = base * np.exp(spread * noise) if base else spread * noise
        out[name] = __import__('jax').numpy.asarray(drawn.astype(out[name].dtype))
    for name, factor in factors.items():
        out[name] = (out[name] * factor).astype(out[name].dtype)
    return out
```

```python
import numpy as np
import concourse.bass as bass
from concourse import mybir
from contextlib import ExitStack

F32 = mybir.dt.float32
I32 = mybir.dt.int32
U32 = mybir.dt.uint32
ALU = mybir.AluOpType
ACT = mybir.ActivationFunctionType
AX = mybir.AxisListType

P = 128
SEQ, D_MODEL = 512, 1024
GRID_W, N_ROWS = 64, 8
QB = 16
NQ = GRID_W // QB
D_CONV, CONV_K = 512, 31
PAD = CONV_K // 2
HEADS, HEAD_DIM = 8, 64
WIN_H, WIN_W = 8, 16
N_EXPERTS, TOP_K, D_FF = 32, 4, 1024
EPS = 1e-5
SWIGLU_LIMIT, SWIGLU_ALPHA = 7.0, 1.702
NEG = 1e30

KD = D_MODEL // P
CC = D_CONV // P
HALF = D_MODEL // 2
RPB_H, RPB_W = 2 * WIN_H - 1, 2 * WIN_W - 1
RPB_PITCH = 64
RUN = WIN_H * RPB_PITCH

CAP = 100
EXTRA = (SEQ - 1) // CAP
MAX_OVERFLOW = (SEQ * TOP_K - 1) // CAP
N_BLOCKS = N_EXPERTS + MAX_OVERFLOW
COLS = N_BLOCKS + 1
NJ = NQ * TOP_K
UNITS = 6


def encoder_kernel(nc, x, g_mix, w_in, b_in, conv_w, conv_b, ln_g, ln_b, rpb, w_out, b_out,
                   g_ffn, w_router, b_router, w_gate, b_gate, w_up, b_up, w_down, b_down,
                   g_final, out):
    ctx = ExitStack()
    with ctx:
        def sb(name, shape, dt=F32):
            return ctx.enter_context(nc.sbuf_tensor(name, shape, dt))

        def sem(name):
            return ctx.enter_context(nc.semaphore(name))

        rpb_pad = nc.dram_tensor("rpb_pad", [QB, HEADS * RPB_H + 1, RPB_PITCH], F32, kind="Internal").ap()
        xn2_rows = nc.dram_tensor("xn2_rows", [SEQ, D_MODEL], F32, kind="Internal").ap()
        y_rows = nc.dram_tensor("y_rows", [N_BLOCKS * CAP, D_MODEL], F32, kind="Internal").ap()

        h = sb("h", [P, NQ, D_MODEL])
        ring = sb("ring", [P, UNITS, KD * HALF])
        area_a = sb("area_a", [P, 4096])
        area_q = sb("area_q", [P, 2048])
        area_k = sb("area_k", [P, 2048])
        area_v = sb("area_v", [P, 2048])
        area_u = sb("area_u", [P, CC * (SEQ + 2 * PAD)])
        area_m = sb("area_m", [P, 4096])
        area_t = sb("area_t", [P, HEADS * 384])

        def unit(s):
            return ring[:, s, :].rearrange("p (k f) -> p k f", k=KD)

        xnT = area_a[:, :].rearrange("p (k t) -> p k t", k=KD)
        qT = area_q[:, :].rearrange("p (k t) -> p k t", k=4)
        kT = area_k[:, :].rearrange("p (k t) -> p k t", k=4)
        v_sb = area_v[:, :].rearrange("p (n f) -> p n f", n=NQ)
        u_pad = area_u[:, :].rearrange("p (c t) -> p c t", c=CC)
        mixedT = area_m[:, :].rearrange("p (k t) -> p k t", k=KD)
        xn_tile = area_q[:, :].rearrange("p (b d) -> p b d", b=2)
        gmix_row = area_k[:, 0:1024]
        bout_row = area_k[:, 1024:2048]
        sg = area_v[:, 0:1024].rearrange("p (b t) -> p b t", b=2)
        stage = area_m[:, 0:1024].rearrange("p (s q) -> p s q", s=8)
        raw_bias = area_m[:, 2048:3072].rearrange("p (b t) -> p b t", b=2)
        mask = area_m[:, 3072:3072 + 896]
        sq = area_u[:, 0:1024].rearrange("p (b t) -> p b t", b=2)
        ln_rs = area_u[:, 1024:1536]
        silu_sig = area_u[:, 1536:2048]
        convT_out = [area_u[:, 0:512], area_u[:, 512:1024], area_u[:, 1024:1536], area_a[:, 3584:4096]]
        T_mid = area_t[:, :].rearrange("p (h t) -> p h t", h=HEADS)
        T_edge = ring[:, 0, :].rearrange("p (h e t) -> p h e t", h=HEADS, e=2)
        S_sb = area_a[:, 0:1152].rearrange("p (b t) -> p b t", b=3)
        P_sb = area_a[:, 1152:2304].rearrange("p (b t) -> p b t", b=3)
        PT_sb = area_a[:, 2304:3072].rearrange("p (b t) -> p b t", b=2)
        O_sb = area_a[:, 3072:3584]
        xn2 = area_a[:, :].rearrange("p (n d) -> p n d", n=NQ)
        xn2T = [a[:, :].rearrange("p (b k t) -> p b k t", b=2, k=KD) for a in (area_q, area_k)]
        gffn_row = area_v[:, 0:1024]
        gfin_row = area_v[:, 1024:2048]
        xg = area_m[:, 0:1024]
        y_sb = area_m[:, 1024:2048]
        hT = area_m[:, 2048:2048 + 8 * CAP].rearrange("p (k t) -> p k t", k=KD)
        yT = area_m[:, 3072:3072 + 8 * CAP].rearrange("p (k t) -> p k t", k=KD)
        xT = area_t[:, 0:8 * CAP].rearrange("p (k t) -> p k t", k=KD)
        g_lim = area_t[:, 1024:1024 + 4 * CAP].rearrange("p (k t) -> p k t", k=4)
        g_sigm = area_t[:, 1536:1536 + 4 * CAP].rearrange("p (k t) -> p k t", k=4)
        g_silu = area_q[:, 0:8 * CAP].rearrange("p (b k t) -> p b k t", b=2, k=4)
        u_lim = area_q[:, 1024:1024 + 8 * CAP].rearrange("p (b k t) -> p b k t", b=2, k=4)
        pos_1h = area_t[:, 0:NJ * CAP].rearrange("p (i c) -> p i c", i=NJ)
        blk_1h = area_t[:, 1600:1600 + NJ * COLS].rearrange("p (i c) -> p i c", i=NJ)
        exp_1h = area_u[:, 0:512].rearrange("p (i e) -> p i e", i=NJ)
        picked = area_u[:, 512:1024].rearrange("p (i e) -> p i e", i=NJ)
        cmp = area_u[:, 1024:1024 + MAX_OVERFLOW * N_EXPERTS]
        junk_norm = [area_t[:, 0:1024], area_t[:, 1024:2048]]
        junk = area_t[:, 0:1024]
        y_tok = ring[:, :, :].rearrange("p s f -> p (s f)").rearrange("p (i d) -> p i d", d=D_MODEL)

        ident = sb("ident", [P, P])
        zeros = sb("zeros", [P, 256])
        mean_w = sb("mean_w", [P, P])
        ones_w = sb("ones_w", [P, P])
        before = sb("before", [P, P])
        colT = sb("colT", [P, 32])
        convT = sb("convT", [P, CONV_K * CC])
        biasT = sb("biasT", [P, 3, N_EXPERTS * KD])
        bq = sb("bq", [P, 4])
        wr = sb("wr", [P, KD, N_EXPERTS])
        br_row = sb("br_row", [P, N_EXPERTS])
        rpb_tile = sb("rpb_tile", [HEADS * RPB_H + 1, RPB_PITCH])
        iota_i = sb("iota_i", [P, 384], I32)
        iota_u = sb("iota_u", [P, 384])
        p_int = sb("p_int", [P, 2], I32)
        c_flt = sb("c_flt", [P, 1])
        win_lo = sb("win_lo", [P, 3])
        win_hi = sb("win_hi", [P, 3])
        iota_f = sb("iota_f", [P, 128])
        thresholds = sb("thresholds", [P, EXTRA])
        tok_id = sb("tok_id", [P, NQ])
        minus_half = sb("minus_half", [P, 1])
        eps_col = sb("eps_col", [P, 1])
        ss = sb("ss", [P, 3 * NQ])
        ms = sb("ms", [P, 3 * NQ])
        rstd = sb("rstd", [P, 3 * NQ])
        neg_max = sb("neg_max", [P, 32])
        row_max = sb("row_max", [P, 32])
        row_sum = sb("row_sum", [P, 32])
        row_inv = sb("row_inv", [P, 32])
        logits = sb("logits", [P, NQ, N_EXPERTS])
        top_val = sb("top_val", [P, NQ, 8])
        top_idx = sb("top_idx", [P, NQ, 8], U32)
        e_idx = sb("e_idx", [P, NJ])
        chosen = sb("chosen", [P, NQ, N_EXPERTS])
        rank = sb("rank", [P, NJ])
        counts = sb("counts", [P, N_EXPERTS])
        n_extra = sb("n_extra", [P, N_EXPERTS])
        cum = sb("cum", [P, 2, 2 * N_EXPERTS])
        first_extra = sb("first_extra", [P, N_EXPERTS])
        first_j = sb("first_j", [P, NJ])
        extra_j = sb("extra_j", [P, NJ])
        is_extra = sb("is_extra", [P, NJ])
        blk = sb("blk", [P, NJ])
        pos = sb("pos", [P, NJ])
        tmp_j = sb("tmp_j", [P, NJ])
        first_slot = sb("first_slot", [P, NJ], I32)
        pos_i = sb("pos_i", [P, NJ], I32)
        slot = sb("slot", [P, NJ], I32)
        tok_tab = sb("tok_tab", [CAP, COLS], I32)
        tok_now = sb("tok_now", [CAP, 1], I32)
        ovf_exp_f = sb("ovf_exp_f", [1, MAX_OVERFLOW])
        ovf_exp = sb("ovf_exp", [1, MAX_OVERFLOW], I32)
        n_ovf = sb("n_ovf", [1, 1], I32)
        gate_neg = sb("gate_neg", [P, NQ])
        gate_sum = sb("gate_sum", [P, NQ])
        gates = sb("gates", [P, NQ, TOP_K])
        gu_bias = sb("gu_bias", [P, 2, KD])
        d_bias = sb("d_bias", [P, KD])

        bank = [ctx.enter_context(nc.psum_tensor(f"bank{i}", [P, 512], F32)) for i in range(8)]

        x_loaded = [sem(f"x_loaded{n}") for n in range(NQ)]
        win_loaded = [sem(f"win_loaded{i}") for i in range(5)]
        wout_loaded = sem("wout_loaded")
        w_loaded = [sem(f"w_loaded{i}") for i in range(UNITS)]
        rows_loaded = sem("rows_loaded")
        bout_loaded = sem("bout_loaded")
        stage_loaded = sem("stage_loaded")
        router_loaded = sem("router_loaded")
        norm_rows_loaded = sem("norm_rows_loaded")
        rpb_tile_loaded = sem("rpb_tile_loaded")
        rpb_stored = sem("rpb_stored")
        raw_loaded = sem("raw_loaded")
        consts_ready = sem("consts_ready")
        iotas_ready = sem("iotas_ready")
        upad_zeroed = sem("upad_zeroed")
        rpb_zeroed = sem("rpb_zeroed")
        mask_step = sem("mask_step")
        ss_ready = sem("ss_ready")
        ms_ready = sem("ms_ready")
        rstd_ready = sem("rstd_ready")
        xn_ready = sem("xn_ready")
        xn_transposed = sem("xn_transposed")
        xnT_dve = sem("xnT_dve")
        xnT_act = sem("xnT_act")
        stage_transposed = sem("stage_transposed")
        cols_ready = sem("cols_ready")
        bq_ready = sem("bq_ready")
        xb_ready = sem("xb_ready")
        proj_done = sem("proj_done")
        act_evac = sem("act_evac")
        glu_ready = sem("glu_ready")
        conv_tap = sem("conv_tap")
        tables_ready = sem("tables_ready")
        mean_done = sem("mean_done")
        centred = sem("centred")
        squared = sem("squared")
        var_part = sem("var_part")
        std_ready = sem("std_ready")
        ln_rs_ready = sem("ln_rs_ready")
        ln_scaled = sem("ln_scaled")
        ln_affine = sem("ln_affine")
        silu_sig_ready = sem("silu_sig_ready")
        silu_ready = sem("silu_ready")
        qk_done = sem("qk_done")
        s_ready = sem("s_ready")
        neg_max_ready = sem("neg_max_ready")
        exp_ready = sem("exp_ready")
        p_transposed = sem("p_transposed")
        pT_dve = sem("pT_dve")
        pT_act = sem("pT_act")
        pv_done = sem("pv_done")
        inv_ready = sem("inv_ready")
        o_ready = sem("o_ready")
        o_transposed = sem("o_transposed")
        oT_ready = sem("oT_ready")
        wout_done = sem("wout_done")
        h_ready = sem("h_ready")
        ss2_ready = sem("ss2_ready")
        xn2_ready = sem("xn2_ready")
        xn2_stored = sem("xn2_stored")
        xn2_transposed = sem("xn2_transposed")
        xn2T_act = sem("xn2T_act")
        xn2T_dve = sem("xn2T_dve")
        logits_done = sem("logits_done")
        logits_ready = sem("logits_ready")
        top_ready = sem("top_ready")
        gate_exp = sem("gate_exp")
        gates_ready = sem("gates_ready")
        route_step = sem("route_step")
        chosen_ready = sem("chosen_ready")
        rank_done = sem("rank_done")
        onehots_ready = sem("onehots_ready")
        table_done = sem("table_done")
        table_ready = sem("table_ready")
        slot_ready = sem("slot_ready")
        zeros_ready = sem("zeros_ready")
        spare_zeroed = sem("spare_zeroed")
        overflow_ready = sem("overflow_ready")
        xg_loaded = sem("xg_loaded")
        xg_transposed = sem("xg_transposed")
        xT_ready = sem("xT_ready")
        gu_done = sem("gu_done")
        gu_bias_ready = sem("gu_bias_ready")
        g_limited = sem("g_limited")
        u_limited = sem("u_limited")
        g_sig_ready = sem("g_sig_ready")
        g_silu_ready = sem("g_silu_ready")
        hT_ready = sem("hT_ready")
        down_done = sem("down_done")
        d_bias_ready = sem("d_bias_ready")
        yT_ready = sem("yT_ready")
        y_transposed = sem("y_transposed")
        y_ready = sem("y_ready")
        y_stored = sem("y_stored")
        y_back = [sem(f"y_back{n}") for n in range(NQ)]
        combined = sem("combined")
        ss3_ready = sem("ss3_ready")
        final_ready = sem("final_ready")
        out_stored = sem("out_stored")

        def row_bcast(ap, n, offset=0):
            return bass.AP(ap.tensor, ap.offset + offset, [[0, P], [1, n]])

        def by_block(ap):
            return ap[0].rearrange("(r n c) d -> n r c d", r=N_ROWS, c=QB)

        x_blocks, out_blocks = by_block(x), by_block(out)
        win_v = w_in[0].rearrange("(k p) f -> p k f", p=P)
        wout_v = w_out[0].rearrange("(k p) f -> p k f", p=P)
        wg_v, wu_v, wd_v = (w[0].rearrange("e (k p) f -> e p k f", p=P) for w in (w_gate, w_up, w_down))

        unit_src = [(wg_v, 0), (wu_v, 0), (wg_v, 1), (wu_v, 1), (wd_v, 0), (wd_v, 1)]

        def keys_of(n):
            return max(n - 1, 0), min(n + 2, NQ)

        def table_of(n, hd):
            if n == 0:
                return T_edge[:, hd, 0, :]
            if n == NQ - 1:
                return T_edge[:, hd, 1, :]
            return T_mid[:, hd, :]

        steps = [(n, hd) for n in range(NQ) for hd in range(HEADS)]
        NS = len(steps)

        block = ctx.enter_context(nc.Block())

        @block.sync
        def _(sp):
            for n in range(NQ):
                for r in range(N_ROWS):
                    sp.dma_start(h[r * QB:(r + 1) * QB, n, :], x_blocks[n, r]).then_inc(x_loaded[n], 16)
            for i, col in enumerate((1, 0, 2, 3, 4)):
                sp.dma_start(unit(1 + i), win_v[:, :, col * HALF:(col + 1) * HALF]).then_inc(win_loaded[i], 16)
            sp.wait_ge(rpb_tile_loaded, 16)
            for c in range(QB):
                sp.dma_start(rpb_pad[c], rpb_tile[:, :]).then_inc(rpb_stored, 16)
            sp.wait_ge(rpb_stored, 16 * QB)
            copy_size = (HEADS * RPB_H + 1) * RPB_PITCH
            for pair in range(HEADS // 2):
                if pair:
                    sp.wait_ge(tables_ready, 6 * pair)
                for r in range(N_ROWS):
                    start = (2 * pair * RPB_H + WIN_H - 1 - r) * RPB_PITCH + QB - 1
                    src = bass.AP(rpb_pad.tensor, rpb_pad.offset + start,
                                  [[copy_size - 1, QB], [RPB_H * RPB_PITCH, 2], [1, RUN]])
                    sp.dma_start(raw_bias[r * QB:(r + 1) * QB, :, :], src).then_inc(raw_loaded, 16)
            spare = y_rows[N_EXPERTS * CAP:, :].rearrange("(p i) (j f) -> p (i j) f", p=CAP, f=zeros.shape[1])
            sp.wait_ge(zeros_ready, 1)
            sp.dma_start(spare, zeros[0:CAP, :].unsqueeze(1).to_broadcast([CAP, spare.shape[1], spare.shape[2]])).then_inc(spare_zeroed, 16)
            sp.wait_ge(proj_done, 8)
            for i in range(2):
                sp.dma_start(unit(1 + i), wout_v[:, :, i * HALF:(i + 1) * HALF]).then_inc(wout_loaded, 16)

            def load(i, e):
                src, half = unit_src[i]
                sp.dma_start(unit(i), src[e, :, :, half * HALF:(half + 1) * HALF]).then_inc(w_loaded[i], 16)

            for i, groups in ((3, 12), (4, 16), (5, 20)):
                sp.wait_ge(proj_done, groups)
                load(i, 0)
            sp.wait_ge(s_ready, NS)
            load(0, 0)
            sp.wait_ge(wout_done, 2 * NQ)
            load(1, 0)
            load(2, 0)

            def weights(b, e):
                for i in range(UNITS):
                    if i < 4:
                        sp.wait_ge(gu_done, 4 * (b - 1) + i + 1)
                    else:
                        sp.wait_ge(down_done, 2 * (b - 1) + i - 3)
                    load(i, e)

            with sp.Fori(1, N_EXPERTS) as b:
                weights(b, b)
            sp.wait_ge(overflow_ready, 2)
            trips = sp.value_load(n_ovf[0:1, 0:1], min_val=0, max_val=MAX_OVERFLOW)
            with sp.If(trips > 0):
                with sp.Fori(N_EXPERTS, trips + N_EXPERTS) as b:
                    e = sp.value_load(ovf_exp[0:1, bass.ds(b - N_EXPERTS, 1)], min_val=0, max_val=N_EXPERTS - 1)
                    weights(b, e)
            for n in range(NQ):
                sp.wait_ge(final_ready, n + 1)
                for r in range(N_ROWS):
                    sp.dma_start(out_blocks[n, r], y_tok[r * QB:(r + 1) * QB, n * TOP_K, :]).then_inc(out_stored, 16)
            sp.wait_ge(out_stored, 16 * NQ * N_ROWS)

        @block.gpsimd
        def _(pool):
            g = nc.gpsimd
            g.memset(minus_half[:, :], -0.5).then_inc(consts_ready, 1)
            g.memset(ident[:, :], 0.0).then_inc(consts_ready, 1)
            g.memset(ones_w[:, :], 1.0).then_inc(consts_ready, 1)
            g.memset(before[:, :], 1.0).then_inc(consts_ready, 1)
            g.memset(mean_w[:, :], 1.0 / D_CONV).then_inc(consts_ready, 1)
            g.memset(eps_col[:, :], EPS).then_inc(consts_ready, 1)
            pool.wait_ge(consts_ready, 6)
            g.affine_select(out=ident[:, :], in_=ident[:, :], compare_op=ALU.not_equal, fill=1.0,
                            base=0, pattern=[[-1, P]], channel_multiplier=1).then_inc(consts_ready, 1)
            g.affine_select(out=before[:, :], in_=before[:, :], compare_op=ALU.is_gt, fill=0.0,
                            base=0, pattern=[[1, P]], channel_multiplier=-1).then_inc(consts_ready, 1)
            g.memset(zeros[:, :], 0.0).then_inc(zeros_ready, 1)
            g.memset(rpb_tile[:, :], 0.0).then_inc(rpb_zeroed, 1)
            g.iota(iota_i[:, :], [[QB, 3], [0, N_ROWS], [1, QB]], base=0, channel_multiplier=0).then_inc(iotas_ready, 1)
            g.iota(p_int[:, 0:1], [[0, 1]], base=0, channel_multiplier=1).then_inc(iotas_ready, 1)
            g.iota(iota_f[:, :], [[1, 128]], base=0, channel_multiplier=0,
                   allow_small_or_imprecise_dtypes=True).then_inc(iotas_ready, 1)
            g.iota(tok_id[:, :], [[P, NQ]], base=0, channel_multiplier=1,
                   allow_small_or_imprecise_dtypes=True).then_inc(iotas_ready, 1)
            g.iota(thresholds[:, :], [[CAP, EXTRA]], base=CAP, channel_multiplier=0,
                   allow_small_or_imprecise_dtypes=True).then_inc(iotas_ready, 1)
            g.memset(area_u[:, :], 0.0).then_inc(upad_zeroed, 1)
            g.memset(cum[:, :, :], 0.0).then_inc(upad_zeroed, 1)
            pool.wait_ge(rpb_zeroed, 1)
            pool.dma_start(rpb_tile[0:HEADS * RPB_H, QB:QB + RPB_W],
                           rpb[0].rearrange("h a b -> (h a) b")).then_inc(rpb_tile_loaded, 16)

            def rstd_of(i, ready):
                g.tensor_scalar(ms[:, i:i + 1], ss[:, i:i + 1], 1.0 / D_MODEL, EPS, ALU.mult, ALU.add).then_inc(ms_ready, 1)
                pool.wait_ge(ms_ready, i + 1)
                g.tensor_tensor(rstd[:, i:i + 1], ms[:, i:i + 1], minus_half[:, :], ALU.pow).then_inc(rstd_ready, 1)

            for n in range(NQ):
                pool.wait_ge(ss_ready, n + 1)
                rstd_of(n, ss_ready)
            pool.wait_ge(bout_loaded, 16)
            for n in range(NQ):
                pool.wait_ge(xn_ready, n + 1)
                g.tensor_tensor(h[:, n, :], h[:, n, :], bout_row, ALU.add).then_inc(xb_ready, 1)
            pool.wait_ge(mask_step, 13)

            for hd in range(HEADS):
                pool.wait_ge(raw_loaded, 16 * N_ROWS * (hd // 2 + 1))
                raw = raw_bias[:, hd % 2, :].rearrange("p (r w) -> p r w", r=N_ROWS)
                for kind, (dst, m0, m1, o) in enumerate(((T_mid[:, hd, :], 0, 3, 0), (T_edge[:, hd, 0, :], 1, 3, 384),
                                                         (T_edge[:, hd, 1, :], 0, 2, 640))):
                    w = (m1 - m0) * P
                    src = raw[:, :, m0 * QB:m1 * QB].rearrange("p r (m c) -> p m r c", c=QB)
                    g.tensor_tensor(dst.rearrange("p (m r c) -> p m r c", r=N_ROWS, c=QB), src,
                                    mask[:, o:o + w].rearrange("p (m r c) -> p m r c", r=N_ROWS, c=QB),
                                    ALU.add).then_inc(tables_ready, 1)
            for c in range(CC):
                pool.wait_ge(ln_rs_ready, 1)
                g.tensor_tensor(mixedT[:, c, :], mixedT[:, c, :], ln_rs, ALU.mult).then_inc(ln_scaled, 1)
            for c in range(CC):
                pool.wait_ge(silu_sig_ready, c + 1)
                g.tensor_scalar(mixedT[:, c, :], mixedT[:, c, :], colT[:, 24 + c:25 + c], colT[:, 28 + c:29 + c],
                                ALU.mult, ALU.add).then_inc(ln_affine, 1)
                pool.wait_ge(ln_affine, c + 1)
                natural = [a.rearrange("p (r n q) -> p n r q", n=NQ, q=QB) for a in (mixedT[:, c, :], silu_sig)]
                g.tensor_tensor(convT_out[c].rearrange("p (n r q) -> p n r q", n=NQ, q=QB), *natural, ALU.mult).then_inc(silu_ready, 1)
            for n in range(NQ):
                pool.wait_ge(ss2_ready, n + 1)
                rstd_of(NQ + n, ss2_ready)

            def gather(b):
                g.tensor_copy(tok_now[:, :], tok_tab[:, bass.ds(b, 1)])
                pool.drain()
                g.indirect_dma_start(out=xg[0:CAP, :], out_offset=None, in_=xn2_rows,
                                     in_offset=bass.IndirectOffsetOnAxis(ap=tok_now[:, 0:1], axis=0)).then_inc(xg_loaded, 16)

            pool.wait_ge(table_ready, 1)
            pool.wait_ge(xn2_stored, 16 * NQ)
            pool.wait_ge(wout_done, 2 * NQ)
            gather(0)

            def pool_block(b):
                pool.wait_ge(xg_loaded, 16 * (b + 1))
                pool.wait_ge(xg_transposed, b + 1)
                gather(b + 1)
                for half in range(2):
                    pool.wait_ge(g_sig_ready, 2 * b + half + 1)
                    g.tensor_tensor(g_silu[:, half], g_lim[:, :, :], g_sigm[:, :, :], ALU.mult).then_inc(g_silu_ready, 1)

            with pool.Fori(0, N_EXPERTS) as b:
                pool_block(b)
            pool.wait_ge(overflow_ready, 2)
            trips = pool.value_load(n_ovf[0:1, 0:1], min_val=0, max_val=MAX_OVERFLOW)
            with pool.If(trips > 0):
                with pool.Fori(N_EXPERTS, trips + N_EXPERTS) as b:
                    pool_block(b)
            pool.wait_ge(spare_zeroed, 16)
            pool.wait_ge(slot_ready, 1)
            pool.wait_ge(y_stored, 16 * (trips + N_EXPERTS))
            g.tensor_tensor(slot[:, :], first_slot[:, :], pos_i[:, :], ALU.add).then_inc(slot_ready, 1)
            pool.wait_ge(slot_ready, 2)
            for i in range(NJ):
                g.indirect_dma_start(out=y_tok[:, i, :], out_offset=None, in_=y_rows,
                                     in_offset=bass.IndirectOffsetOnAxis(ap=slot[:, i:i + 1], axis=0)).then_inc(y_back[i // TOP_K], 16)
            for n in range(NQ):
                pool.wait_ge(ss3_ready, n + 1)
                rstd_of(2 * NQ + n, ss3_ready)

        @block.scalar
        def _(act):
            s = nc.scalar
            act.dma_start(gmix_row, row_bcast(g_mix, D_MODEL)).then_inc(rows_loaded, 16)
            act.dma_start(stage[0:20, 0, :], b_in[0].rearrange("(c p) -> c p", p=P)).then_inc(stage_loaded, 16)
            for i, vec in enumerate((conv_b, ln_g, ln_b)):
                act.dma_start(stage[20 + CC * i:20 + CC * (i + 1), 0, :],
                              vec[0].rearrange("(c p) -> c p", p=P)).then_inc(stage_loaded, 16)
            act.dma_start(stage[0:CONV_K * CC, 1, :],
                          conv_w[0].rearrange("k (c p) -> (k c) p", p=P)).then_inc(stage_loaded, 16)
            for i, mat in enumerate((b_gate, b_up, b_down)):
                rows = mat[0].rearrange("e (c p) -> (e c) p", p=P)
                for j in range(2):
                    act.dma_start(stage[:, 2 + 2 * i + j, :], rows[j * P:(j + 1) * P, :]).then_inc(stage_loaded, 16)
            act.dma_start(bout_row, row_bcast(b_out, D_MODEL)).then_inc(bout_loaded, 16)
            act.dma_start(br_row[:, :], row_bcast(b_router, N_EXPERTS)).then_inc(router_loaded, 16)
            act.dma_start(wr[:, :, :], w_router[0].rearrange("(k p) e -> p k e", p=P)).then_inc(router_loaded, 16)

            def xnT_half(n):
                act.wait_ge(xn_transposed, 2 * n + 2)
                s.copy(xnT[:, 4:8, n * P:(n + 1) * P],
                       bank[4 + (2 * n + 1) % 4][:, :].rearrange("p (k t) -> p k t", k=4)).then_inc(xnT_act, 1)

            def pT_out(j):
                m0, m1 = keys_of(steps[j][0])
                w = (m1 - m0) * P
                act.wait_ge(p_transposed, j + 1)
                s.copy(PT_sb[:, 1, 0:w], bank[6][:, 0:w]).then_inc(pT_act, 1)

            for n in range(NQ):
                act.wait_ge(x_loaded[n], 16 * N_ROWS)
                if n:
                    act.wait_ge(ss_ready, n)
                s.activation(junk_norm[n % 2], h[:, n, :], ACT.Square, accum_out=ss[:, n:n + 1]).then_inc(ss_ready, 1)
            for n in range(NQ):
                xnT_half(n)
            act.wait_ge(cols_ready, 4)
            for c in range(CC):
                act.wait_ge(proj_done, 2 * c + 1)
                if c >= 2:
                    act.wait_ge(glu_ready, 4 * (c - 1))
                s.activation(sg[:, c % 2, :], bank[2 * c % 4][:, :], ACT.Sigmoid, bias=colT[:, 4 + c:5 + c]).then_inc(act_evac, 1)
            act.wait_ge(bq_ready, 1)
            for i in range(4):
                act.wait_ge(proj_done, 8 + i + 1)
                s.activation(qT[:, i, :], bank[i][:, :], ACT.Identity, bias=bq[:, i:i + 1], scale=HEAD_DIM ** -0.5).then_inc(act_evac, 1)
            act.wait_ge(xb_ready, NQ)
            for i in range(4):
                act.wait_ge(proj_done, 12 + i + 1)
                s.activation(kT[:, i, :], bank[i][:, :], ACT.Identity, bias=colT[:, 12 + i:13 + i]).then_inc(act_evac, 1)
            act.wait_ge(glu_ready, 16)
            for n in range(NQ):
                act.wait_ge(proj_done, 16 + n + 1)
                s.copy(v_sb[:, n, :], bank[n][:, :]).then_inc(act_evac, 1)
            for c in range(CC):
                act.wait_ge(centred, c + 1)
                if c >= 2:
                    act.wait_ge(var_part, c - 1)
                s.activation(sq[:, c % 2, :], mixedT[:, c, :], ACT.Square).then_inc(squared, 1)
            act.wait_ge(var_part, CC)
            s.activation(ln_rs, bank[5][:, :], ACT.Sqrt, bias=eps_col[:, :]).then_inc(std_ready, 1)
            for i in range(NS):
                n, hd = steps[i]
                m0, m1 = keys_of(n)
                w = (m1 - m0) * P
                act.wait_ge(neg_max_ready, i + 1)
                if i >= 3:
                    act.wait_ge(p_transposed, i - 2)
                s.activation(P_sb[:, i % 3, 0:w], S_sb[:, i % 3, 0:w], ACT.Exp, bias=neg_max[:, i:i + 1],
                             accum_out=row_sum[:, i:i + 1]).then_inc(exp_ready, 1)
                j = i - 1
                if j >= 1 and j % 2:
                    pT_out(j)
                if i == 8:
                    for c in range(CC):
                        act.wait_ge(ln_scaled, c + 1)
                        if c >= 1:
                            act.wait_ge(silu_ready, c)
                        s.activation(silu_sig, mixedT[:, c, :], ACT.Sigmoid, bias=colT[:, 28 + c:29 + c],
                                     scale=colT[:, 24 + c:25 + c]).then_inc(silu_sig_ready, 1)
            pT_out(NS - 1)

            act.wait_ge(pv_done, NS)
            act.dma_start(gffn_row, row_bcast(g_ffn, D_MODEL)).then_inc(norm_rows_loaded, 16)
            act.dma_start(gfin_row, row_bcast(g_final, D_MODEL)).then_inc(norm_rows_loaded, 16)

            def square2(n):
                act.wait_ge(h_ready, 2 * n + 2)
                if n:
                    act.wait_ge(ss2_ready, n)
                s.activation(junk, h[:, n, :], ACT.Square, accum_out=ss[:, NQ + n:NQ + n + 1]).then_inc(ss2_ready, 1)

            def xn2T_half(n):
                act.wait_ge(xn2_ready, n + 1)
                act.dma_start(xn2_rows[n * P:(n + 1) * P, :], xn2[:, n, :]).then_inc(xn2_stored, 16)
                act.wait_ge(xn2_transposed, 2 * n + 2)
                s.copy(xn2T[n // 2][:, n % 2, 4:8, :],
                       bank[4 + (2 * n + 1) % 3][:, :].rearrange("p (k t) -> p k t", k=4)).then_inc(xn2T_act, 1)

            square2(0)
            square2(1)
            xn2T_half(0)
            square2(2)
            xn2T_half(1)
            square2(3)
            xn2T_half(2)
            xn2T_half(3)
            for n in range(NQ):
                act.wait_ge(top_ready, n + 1)
                s.mul(gate_neg[:, n:n + 1], top_val[:, n, 0:1], -1.0).then_inc(gate_exp, 1)
                act.wait_ge(gate_exp, 2 * n + 1)
                s.activation(gates[:, n, :], top_val[:, n, 0:TOP_K], ACT.Exp, bias=gate_neg[:, n:n + 1],
                             accum_out=gate_sum[:, n:n + 1]).then_inc(gate_exp, 1)

            def rows_out(b):
                for half in range(2):
                    act.wait_ge(y_transposed, 2 * b + half + 1)
                    s.copy(y_sb[0:CAP, half * HALF:(half + 1) * HALF], bank[6 + half][0:CAP, :]).then_inc(y_ready, 1)
                act.wait_ge(y_ready, 2 * b + 2)
                act.dma_start(y_rows[bass.ds(b * CAP, CAP), :], y_sb[0:CAP, :]).then_inc(y_stored, 16)

            def sigmoid(b, half):
                act.wait_ge(g_limited, 8 * b + 4 * (half + 1))
                s.activation(g_sigm[:, :, :], g_lim[:, :, :], ACT.Sigmoid, scale=SWIGLU_ALPHA).then_inc(g_sig_ready, 1)

            def act_block(b, e, first=False):
                if not first:
                    act.wait_ge(yT_ready, 8 * b)
                s.copy(d_bias[:, :], biasT[:, 2, bass.ds(e * KD, KD)]).then_inc(d_bias_ready, 1)
                sigmoid(b, 0)
                if not first:
                    act.wait_ge(y_stored, 16 * (b - 1))
                    rows_out(b - 1)
                sigmoid(b, 1)
                act.wait_ge(d_bias_ready, b + 1)
                for half in range(2):
                    act.wait_ge(down_done, 2 * b + half + 1)
                    for c in range(4):
                        k = 4 * half + c
                        s.activation(yT[:, k, :], bank[4 + half][:, c * CAP:(c + 1) * CAP], ACT.Identity,
                                     bias=d_bias[:, k:k + 1]).then_inc(yT_ready, 1)

            act_block(0, 0, first=True)
            with act.Fori(1, N_EXPERTS) as b:
                act_block(b, b)
            act.wait_ge(overflow_ready, 2)
            trips = act.value_load(n_ovf[0:1, 0:1], min_val=0, max_val=MAX_OVERFLOW)
            with act.If(trips > 0):
                with act.Fori(N_EXPERTS, trips + N_EXPERTS) as b:
                    e = act.value_load(ovf_exp[0:1, bass.ds(b - N_EXPERTS, 1)], min_val=0, max_val=N_EXPERTS - 1)
                    act_block(b, e)
            act.wait_ge(y_stored, 16 * (trips + N_EXPERTS - 1))
            rows_out(trips + N_EXPERTS - 1)
            for n in range(NQ):
                act.wait_ge(combined, TOP_K * (n + 1))
                if n:
                    act.wait_ge(ss3_ready, n)
                s.activation(junk, h[:, n, :], ACT.Square, accum_out=ss[:, 2 * NQ + n:2 * NQ + n + 1]).then_inc(ss3_ready, 1)

        @block.vector
        def _(dve):
            v = nc.vector
            dve.wait_ge(iotas_ready, 5)
            v.tensor_scalar(p_int[:, 1:2], p_int[:, 0:1], QB - 1, None, ALU.bitwise_and).then_inc(mask_step, 1)
            v.tensor_copy(iota_u[:, :], iota_i[:, :]).then_inc(mask_step, 1)
            dve.wait_ge(mask_step, 2)
            v.tensor_copy(c_flt[:, :], p_int[:, 1:2]).then_inc(mask_step, 1)
            dve.wait_ge(mask_step, 3)
            v.tensor_scalar(win_lo[:, 0:1], c_flt[:, :], WIN_W / 2, None, ALU.add)
            v.tensor_scalar(win_lo[:, 1:2], c_flt[:, :], WIN_W / 2, float(QB), ALU.add, ALU.max)
            v.tensor_scalar(win_lo[:, 2:3], c_flt[:, :], WIN_W / 2, float(QB), ALU.add, ALU.min).then_inc(mask_step, 3)
            dve.wait_ge(mask_step, 6)
            v.tensor_scalar(win_hi[:, :], win_lo[:, :], WIN_W - 1.0, None, ALU.add)
            for kind, (o, a, w) in enumerate(((0, 0, 384), (384, 128, 256), (640, 0, 256))):
                v.tensor_scalar(mask[:, o:o + w], iota_u[:, a:a + w], win_lo[:, kind:kind + 1], None, ALU.is_ge).then_inc(mask_step, 1)
            dve.wait_ge(mask_step, 9)
            for kind, (o, a, w) in enumerate(((0, 0, 384), (384, 128, 256), (640, 0, 256))):
                v.scalar_tensor_tensor(mask[:, o:o + w], iota_u[:, a:a + w], win_hi[:, kind:kind + 1],
                                       mask[:, o:o + w], ALU.is_le, ALU.mult).then_inc(mask_step, 1)
            dve.wait_ge(mask_step, 12)
            v.tensor_scalar(mask, mask, -1.0, NEG, ALU.add, ALU.mult).then_inc(mask_step, 1)

            dve.wait_ge(rows_loaded, 16)
            for n in range(NQ + 1):
                if n < NQ:
                    dve.wait_ge(rstd_ready, n + 1)
                    if n >= 2:
                        dve.wait_ge(xn_transposed, 2 * (n - 1))
                    v.scalar_tensor_tensor(xn_tile[:, n % 2, :], h[:, n, :], rstd[:, n:n + 1], gmix_row,
                                           ALU.mult, ALU.mult).then_inc(xn_ready, 1)
                if n:
                    dve.wait_ge(xn_transposed, 2 * (n - 1) + 1)
                    v.tensor_copy(xnT[:, 0:4, (n - 1) * P:n * P],
                                  bank[4 + 2 * (n - 1) % 4][:, :].rearrange("p (k t) -> p k t", k=4)).then_inc(xnT_dve, 1)
            dve.wait_ge(stage_transposed, 1)
            v.tensor_copy(colT[:, :], bank[0][:, 0:32])
            v.tensor_copy(convT[:, :], bank[0][:, 32:32 + CONV_K * CC]).then_inc(cols_ready, 1)
            v.tensor_copy(biasT[:, 0, :], bank[1][:, 0:256]).then_inc(cols_ready, 1)
            v.tensor_scalar(biasT[:, 1, :], bank[2][:, 0:256], 1.0, None, ALU.add).then_inc(cols_ready, 1)
            v.tensor_copy(biasT[:, 2, :], bank[3][:, 0:256]).then_inc(cols_ready, 1)
            dve.wait_ge(cols_ready, 4)
            v.tensor_scalar(bq[:, :], colT[:, 8:12], HEAD_DIM ** -0.5, None, ALU.mult).then_inc(bq_ready, 1)
            dve.wait_ge(upad_zeroed, 2)
            for c in range(CC):
                dve.wait_ge(proj_done, 2 * c + 2)
                dve.wait_ge(act_evac, c + 1)
                dst = u_pad[:, c, PAD:PAD + SEQ].rearrange("p (r n q) -> p n r q", n=NQ, q=QB)
                for n in range(NQ):
                    v.scalar_tensor_tensor(dst[:, n], bank[(2 * c + 1) % 4][:, n * P:(n + 1) * P].rearrange("p (r q) -> p r q", q=QB),
                                           colT[:, c:c + 1],
                                           sg[:, c % 2, n * P:(n + 1) * P].rearrange("p (r q) -> p r q", q=QB),
                                           ALU.add, ALU.mult).then_inc(glu_ready, 1)
            dve.wait_ge(glu_ready, 16)
            for c in range(CC):
                v.tensor_scalar(mixedT[:, c, :], u_pad[:, c, 0:SEQ], convT[:, c:c + 1], colT[:, 20 + c:21 + c],
                                ALU.mult, ALU.add).then_inc(conv_tap, 1)
            with dve.Fori(1, CONV_K) as k:
                for c in range(CC):
                    dve.wait_ge(conv_tap, k * CC + c - (CC - 1))
                    v.scalar_tensor_tensor(mixedT[:, c, :], u_pad[:, c, bass.ds(k, SEQ)], convT[:, bass.ds(k * CC + c, 1)],
                                           mixedT[:, c, :], ALU.mult, ALU.add).then_inc(conv_tap, 1)
            dve.wait_ge(mean_done, 1)
            dve.wait_ge(conv_tap, CONV_K * CC)
            for c in range(CC):
                v.tensor_tensor(mixedT[:, c, :], mixedT[:, c, :], bank[4][:, :], ALU.subtract).then_inc(centred, 1)

            def scores(i):
                n, hd = steps[i]
                m0, m1 = keys_of(n)
                w = (m1 - m0) * P
                dve.wait_ge(qk_done, i + 1)
                if i >= 3:
                    dve.wait_ge(exp_ready, i - 2)
                v.tensor_tensor_reduce(out=S_sb[:, i % 3, 0:w], in0=bank[i % 3][:, 0:w], in1=table_of(n, hd),
                                       scale=1.0, scalar=-3.0e38, op0=ALU.add, op1=ALU.max,
                                       accum_out=row_max[:, i:i + 1]).then_inc(s_ready, 1)
                dve.wait_ge(s_ready, i + 1)
                v.tensor_scalar(neg_max[:, i:i + 1], row_max[:, i:i + 1], -1.0, None, ALU.mult).then_inc(neg_max_ready, 1)

            dve.wait_ge(tables_ready, 3 * HEADS)
            for i in range(NS + 3):
                if i < NS:
                    scores(i)
                if i == 1:
                    dve.wait_ge(std_ready, 1)
                    v.reciprocal(ln_rs, ln_rs).then_inc(ln_rs_ready, 1)
                j = i - 2
                if 0 <= j < NS and j % 2 == 0:
                    m0, m1 = keys_of(steps[j][0])
                    w = (m1 - m0) * P
                    dve.wait_ge(p_transposed, j + 1)
                    v.tensor_copy(PT_sb[:, 0, 0:w], bank[3][:, 0:w]).then_inc(pT_dve, 1)
                if i >= 10 and (i - 10) % HEADS == 0:
                    n = (i - 10) // HEADS
                    dve.wait_ge(exp_ready, HEADS * (n + 1))
                    v.reciprocal(row_inv[:, n * HEADS:(n + 1) * HEADS], row_sum[:, n * HEADS:(n + 1) * HEADS]).then_inc(inv_ready, 1)
                    dve.wait_ge(inv_ready, n + 1)
                    dve.wait_ge(pv_done, HEADS * (n + 1))
                    if n:
                        dve.wait_ge(o_transposed, n)
                    v.tensor_tensor(O_sb.rearrange("p (h d) -> p h d", d=HEAD_DIM),
                                    bank[7 if n % 2 == 0 else 4][:, :].rearrange("p (h d) -> p h d", d=HEAD_DIM),
                                    row_inv[:, n * HEADS:(n + 1) * HEADS].unsqueeze(2).to_broadcast([P, HEADS, HEAD_DIM]),
                                    ALU.mult).then_inc(o_ready, 1)
                    dve.wait_ge(o_transposed, n + 1)
                    v.tensor_tensor(mixedT[:, 4:8, n * P:(n + 1) * P], bank[5][:, :].rearrange("p (k t) -> p k t", k=4),
                                    colT[:, 16:20].unsqueeze(2).to_broadcast([P, 4, P]), ALU.add).then_inc(oT_ready, 1)

            def residual(n):
                for half in range(2):
                    dve.wait_ge(wout_done, 2 * n + half + 1)
                    v.tensor_tensor(h[:, n, half * HALF:(half + 1) * HALF], h[:, n, half * HALF:(half + 1) * HALF],
                                    bank[(2 * n + half) % 4][:, :], ALU.add).then_inc(h_ready, 1)

            def norm2(n):
                dve.wait_ge(rstd_ready, NQ + n + 1)
                v.scalar_tensor_tensor(xn2[:, n, :], h[:, n, :], rstd[:, NQ + n:NQ + n + 1], gffn_row,
                                       ALU.mult, ALU.mult).then_inc(xn2_ready, 1)
                dve.wait_ge(xn2_transposed, 2 * n + 1)
                v.tensor_copy(xn2T[n // 2][:, n % 2, 0:4, :],
                              bank[4 + 2 * n % 3][:, :].rearrange("p (k t) -> p k t", k=4)).then_inc(xn2T_dve, 1)

            def top(n):
                dve.wait_ge(logits_done, n + 1)
                v.tensor_tensor(logits[:, n, :], bank[7][:, n * 32:(n + 1) * 32], br_row[:, :], ALU.add).then_inc(logits_ready, 1)
                dve.wait_ge(logits_ready, n + 1)
                v.max(top_val[:, n, :], logits[:, n, :]).then_inc(top_ready, 1)
                dve.wait_ge(top_ready, n + 1)
                v.max_index(top_idx[:, n, :], top_val[:, n, :], logits[:, n, :]).then_inc(route_step, 1)

            dve.wait_ge(norm_rows_loaded, 32)
            dve.wait_ge(router_loaded, 32)
            residual(0)
            residual(1)
            norm2(0)
            residual(2)
            norm2(1)
            top(0)
            residual(3)
            norm2(2)
            top(1)
            norm2(3)
            top(2)
            top(3)

            n_steps = [NQ]

            def then(ins):
                n_steps[0] += 1
                ins.then_inc(route_step, 1)
                dve.wait_ge(route_step, n_steps[0])

            def wide(ap, n):
                return ap.unsqueeze(2).to_broadcast([ap.shape[0], ap.shape[1], n])

            def across(ap, n):
                return ap.unsqueeze(1).to_broadcast([ap.shape[0], n, ap.shape[1]])

            dve.wait_ge(route_step, NQ)
            dve.wait_ge(ss2_ready, NQ)
            then(v.tensor_copy(e_idx[:, :].rearrange("p (n j) -> p n j", j=TOP_K), top_idx[:, :, 0:TOP_K]))
            then(v.tensor_tensor(exp_1h, across(iota_f[:, 0:N_EXPERTS], NJ), wide(e_idx[:, :], N_EXPERTS), ALU.is_equal))
            v.tensor_reduce(chosen[:, :, :], exp_1h.rearrange("p (n j) e -> p n e j", j=TOP_K), AX.X, ALU.add).then_inc(chosen_ready, 1)
            dve.wait_ge(rank_done, 1)
            then(v.tensor_copy(counts[:, :], bank[0][:, NQ * 32:NQ * 32 + 32]))
            then(v.tensor_tensor(picked.rearrange("p (n j) e -> p n j e", j=TOP_K),
                                 exp_1h.rearrange("p (n j) e -> p n j e", j=TOP_K),
                                 bank[0][:, 0:NQ * 32].rearrange("p (n e) -> p n e", n=NQ).unsqueeze(2).to_broadcast([P, NQ, TOP_K, N_EXPERTS]),
                                 ALU.mult))
            then(v.tensor_reduce(rank[:, :], picked, AX.X, ALU.add))
            over = cmp[:, 0:EXTRA * N_EXPERTS].rearrange("p (i e) -> p i e", i=EXTRA)
            then(v.tensor_tensor(over, across(counts[:, :], EXTRA), wide(thresholds[:, :], N_EXPERTS), ALU.is_gt))
            then(v.tensor_reduce(n_extra[:, :], over.rearrange("p i e -> p e i"), AX.X, ALU.add))
            then(v.tensor_copy(cum[:, 0, N_EXPERTS:], n_extra[:, :]))
            cur, shift = 0, 1
            while shift < N_EXPERTS:
                then(v.tensor_tensor(cum[:, 1 - cur, N_EXPERTS:], cum[:, cur, N_EXPERTS:],
                                     cum[:, cur, N_EXPERTS - shift:2 * N_EXPERTS - shift], ALU.add))
                cur, shift = 1 - cur, 2 * shift
            upto = cum[:, cur, N_EXPERTS:]
            then(v.tensor_tensor(first_extra[:, :], upto, n_extra[:, :], ALU.subtract))
            then(v.tensor_tensor(picked, exp_1h, across(first_extra[:, :], NJ), ALU.mult))
            then(v.tensor_reduce(first_j[:, :], picked, AX.X, ALU.add))
            past = cmp[:, 0:NJ * EXTRA].rearrange("p (i t) -> p i t", i=NJ)
            then(v.tensor_tensor(past, wide(rank[:, :], EXTRA), across(thresholds[:, :], NJ), ALU.is_ge))
            then(v.tensor_reduce(extra_j[:, :], past, AX.X, ALU.add))
            then(v.scalar_tensor_tensor(pos[:, :], extra_j[:, :], -float(CAP), rank[:, :], ALU.mult, ALU.add))
            v.tensor_tensor(pos_1h[:, :, :], across(iota_f[:, 0:CAP], NJ), wide(pos[:, :], CAP), ALU.is_equal).then_inc(onehots_ready, 1)
            then(v.tensor_scalar(is_extra[:, :], extra_j[:, :], 1.0, None, ALU.min))
            then(v.tensor_tensor(tmp_j[:, :], first_j[:, :], extra_j[:, :], ALU.add))
            then(v.scalar_tensor_tensor(tmp_j[:, :], tmp_j[:, :], N_EXPERTS - 1.0, e_idx[:, :], ALU.add, ALU.subtract))
            then(v.tensor_tensor(tmp_j[:, :], tmp_j[:, :], is_extra[:, :], ALU.mult))
            then(v.tensor_tensor(blk[:, :], tmp_j[:, :], e_idx[:, :], ALU.add))
            then(v.tensor_tensor(blk_1h, across(iota_f[:, 0:COLS], NJ), wide(blk[:, :], COLS), ALU.is_equal))
            blk_n = blk_1h.rearrange("p (n j) c -> p n (j c)", j=TOP_K)
            v.tensor_tensor(blk_n, blk_n, wide(tok_id[:, :], TOP_K * COLS), ALU.mult).then_inc(onehots_ready, 1)
            dve.wait_ge(table_done, 1)
            v.tensor_copy(tok_tab[:, :], bank[1][0:CAP, 0:COLS]).then_inc(table_ready, 1)
            v.tensor_scalar(first_slot[:, :], blk[:, :], float(CAP), None, ALU.mult)
            v.tensor_copy(pos_i[:, :], pos[:, :]).then_inc(slot_ready, 1)
            v.tensor_copy(n_ovf[:, :], cum[0:1, cur, 2 * N_EXPERTS - 1:]).then_inc(overflow_ready, 1)
            seen = cmp[0:1, :].rearrange("p (b e) -> p b e", e=N_EXPERTS)
            then(v.tensor_tensor(seen, wide(iota_f[0:1, 0:MAX_OVERFLOW], N_EXPERTS), across(cum[0:1, cur, N_EXPERTS:], MAX_OVERFLOW), ALU.is_ge))
            then(v.tensor_reduce(ovf_exp_f[:, :], seen, AX.X, ALU.add))
            v.tensor_scalar(ovf_exp[:, :], ovf_exp_f[:, :], N_EXPERTS - 1.0, None, ALU.min).then_inc(overflow_ready, 1)
            dve.wait_ge(gate_exp, 2 * NQ)
            then(v.reciprocal(gate_sum[:, :], gate_sum[:, :]))
            v.tensor_tensor(gates[:, :, :], gates[:, :, :], wide(gate_sum[:, :], TOP_K), ALU.mult).then_inc(gates_ready, 1)

            def tokens_in(b):
                dve.wait_ge(xg_transposed, b + 1)
                for half in range(2):
                    v.tensor_copy(xT[:, 4 * half:4 * half + 4, :],
                                  bank[6 + half][:, 0:4 * CAP].rearrange("p (k t) -> p k t", k=4)).then_inc(xT_ready, 1)

            tokens_in(0)

            def dve_block(b, e):
                v.tensor_copy(gu_bias[:, :, :], biasT[:, 0:2, bass.ds(e * KD, KD)]).then_inc(gu_bias_ready, 1)
                dve.wait_ge(gu_bias_ready, b + 1)
                for half in range(2):
                    dve.wait_ge(gu_done, 4 * b + 2 * half + 1)
                    for c in range(4):
                        k = 4 * half + c
                        v.tensor_scalar(g_lim[:, c, :], bank[2 * half][:, c * CAP:(c + 1) * CAP], gu_bias[:, 0, k:k + 1],
                                        SWIGLU_LIMIT, ALU.add, ALU.min).then_inc(g_limited, 1)
                    dve.wait_ge(gu_done, 4 * b + 2 * half + 2)
                    for c in range(4):
                        k = 4 * half + c
                        v.tensor_scalar(u_lim[:, half, c, :], bank[2 * half + 1][:, c * CAP:(c + 1) * CAP], gu_bias[:, 1, k:k + 1],
                                        1.0 + SWIGLU_LIMIT, ALU.add, ALU.min).then_inc(u_limited, 1)
                    dve.wait_ge(u_limited, 8 * b + 4 * (half + 1))
                    dve.wait_ge(g_silu_ready, 2 * b + half + 1)
                    v.scalar_tensor_tensor(hT[:, 4 * half:4 * half + 4, :], u_lim[:, half], 1.0 - SWIGLU_LIMIT,
                                           g_silu[:, half], ALU.max, ALU.mult).then_inc(hT_ready, 1)
                tokens_in(b + 1)

            with dve.Fori(0, N_EXPERTS) as b:
                dve_block(b, b)
            trips = dve.value_load(n_ovf[0:1, 0:1], min_val=0, max_val=MAX_OVERFLOW)
            with dve.If(trips > 0):
                with dve.Fori(N_EXPERTS, trips + N_EXPERTS) as b:
                    e = dve.value_load(ovf_exp[0:1, bass.ds(b - N_EXPERTS, 1)], min_val=0, max_val=N_EXPERTS - 1)
                    dve_block(b, e)
            dve.wait_ge(gates_ready, 1)
            for n in range(NQ + 1):
                if n < NQ:
                    dve.wait_ge(y_back[n], 16 * TOP_K)
                    for j in range(TOP_K):
                        if j:
                            dve.wait_ge(combined, TOP_K * n + j)
                        v.scalar_tensor_tensor(h[:, n, :], y_tok[:, n * TOP_K + j, :], gates[:, n, j:j + 1], h[:, n, :],
                                               ALU.mult, ALU.add).then_inc(combined, 1)
                if n:
                    m = n - 1
                    dve.wait_ge(rstd_ready, 2 * NQ + m + 1)
                    v.scalar_tensor_tensor(y_tok[:, m * TOP_K, :], h[:, m, :], rstd[:, 2 * NQ + m:2 * NQ + m + 1], gfin_row,
                                           ALU.mult, ALU.mult).then_inc(final_ready, 1)

        @block.tensor
        def _(pe):
            t = nc.tensor
            pe.wait_ge(consts_ready, 8)
            for n in range(NQ):
                pe.wait_ge(xn_ready, n + 1)
                for half in range(2):
                    i = 2 * n + half
                    if i >= 4:
                        pe.wait_ge(xnT_act if half else xnT_dve, n - 1)
                    for c in range(4):
                        k = 4 * half + c
                        last = t.transpose(bank[4 + i % 4][:, c * P:(c + 1) * P], xn_tile[:, n % 2, k * P:(k + 1) * P], ident[:, :])
                    last.then_inc(xn_transposed, 1)
                if n == 0:
                    pe.wait_ge(stage_loaded, 16 * 11)
                    t.transpose(bank[0][:, 0:32], stage[0:32, 0, :], ident[0:32, 0:32])
                    rows = CONV_K * CC
                    t.transpose(bank[0][:, 32:32 + rows], stage[0:rows, 1, :], ident[0:rows, 0:rows])
                    for i in range(6):
                        last = t.transpose(bank[1 + i // 2][:, (i % 2) * P:(i % 2 + 1) * P], stage[:, 2 + i, :], ident[:, :])
                    last.then_inc(stage_transposed, 1)
            pe.wait_ge(xnT_dve, NQ)
            pe.wait_ge(xnT_act, NQ)
            pe.wait_ge(cols_ready, 4)

            groups = [(1 + i % 2, i // 2) for i in range(8)] + [(3, c) for c in range(4)] + [(4, c) for c in range(4)]
            for g, (s, c) in enumerate(groups):
                pe.wait_ge(win_loaded[s - 1], 16)
                if 4 <= g < 12 and g % 2:
                    pe.wait_ge(glu_ready, 4 * ((g - 4) // 2 + 1))
                elif 4 <= g < 12:
                    pe.wait_ge(act_evac, (g - 4) // 2 + 1)
                elif g >= 12:
                    pe.wait_ge(act_evac, 4 + g - 12 + 1)
                for k in range(KD):
                    last = t.matmul(bank[g % 4][:, :], unit(s)[:, k, c * P:(c + 1) * P], xnT[:, k, :],
                                    start=(k == 0), stop=(k == KD - 1))
                last.then_inc(proj_done, 1)
            pe.wait_ge(win_loaded[4], 16)
            for n in range(NQ):
                pe.wait_ge(act_evac, 8 + n + 1)
                for k in range(KD):
                    last = t.matmul(bank[n][:, :], xnT[:, k, n * P:(n + 1) * P], unit(5)[:, k, :],
                                    start=(k == 0), stop=(k == KD - 1))
                last.then_inc(proj_done, 1)
            pe.wait_ge(conv_tap, CONV_K * CC)
            for c in range(CC):
                last = t.matmul(bank[4][:, :], mean_w[:, :], mixedT[:, c, :], start=(c == 0), stop=(c == CC - 1))
            last.then_inc(mean_done, 1)

            def qk(i):
                n, hd = steps[i]
                m0, m1 = keys_of(n)
                p0 = (hd % 2) * HEAD_DIM
                if i >= 3:
                    pe.wait_ge(s_ready, i - 2)
                t.matmul(bank[i % 3][:, 0:(m1 - m0) * P], qT[p0:p0 + HEAD_DIM, hd // 2, n * P:(n + 1) * P],
                         kT[p0:p0 + HEAD_DIM, hd // 2, m0 * P:m1 * P], start=True, stop=True).then_inc(qk_done, 1)

            def transpose_p(i):
                m0, m1 = keys_of(steps[i][0])
                pe.wait_ge(exp_ready, i + 1)
                if i >= 2:
                    pe.wait_ge(pT_act if i % 2 else pT_dve, i // 2)
                for m in range(m1 - m0):
                    last = t.transpose(bank[6 if i % 2 else 3][:, m * P:(m + 1) * P], P_sb[:, i % 3, m * P:(m + 1) * P], ident[:, :])
                last.then_inc(p_transposed, 1)

            def pv(i):
                n, hd = steps[i]
                m0, m1 = keys_of(n)
                pe.wait_ge(pT_act if i % 2 else pT_dve, i // 2 + 1)
                if hd == 0 and n >= 2:
                    pe.wait_ge(o_ready, n - 1)
                for m in range(m0, m1):
                    last = t.matmul(bank[7 if n % 2 == 0 else 4][:, hd * HEAD_DIM:(hd + 1) * HEAD_DIM],
                                    PT_sb[:, i % 2, (m - m0) * P:(m - m0 + 1) * P],
                                    v_sb[:, m, hd * HEAD_DIM:(hd + 1) * HEAD_DIM], start=(m == m0), stop=(m == m1 - 1))
                last.then_inc(pv_done, 1)

            def transpose_o(n):
                pe.wait_ge(o_ready, n + 1)
                if n:
                    pe.wait_ge(oT_ready, n)
                for c in range(4):
                    last = t.transpose(bank[5][:, c * P:(c + 1) * P], O_sb[:, c * P:(c + 1) * P], ident[:, :])
                last.then_inc(o_transposed, 1)

            pe.wait_ge(act_evac, 16)
            for i in range(NS + 3):
                if i < NS:
                    qk(i)
                if i == 1:
                    for c in range(CC):
                        pe.wait_ge(squared, c + 1)
                        t.matmul(bank[5][:, :], mean_w[:, :], sq[:, c % 2, :], start=(c == 0),
                                 stop=(c == CC - 1)).then_inc(var_part, 1)
                if 0 <= i - 1 < NS:
                    transpose_p(i - 1)
                if 0 <= i - 2 < NS:
                    pv(i - 2)
                if i >= 10 and (i - 10) % HEADS == 0:
                    transpose_o((i - 10) // HEADS)

            def project_out(n):
                for half in range(2):
                    i = 2 * n + half
                    if i >= 4:
                        pe.wait_ge(h_ready, i - 3)
                    for k in range(KD):
                        if k < 4:
                            lhsT = convT_out[k][:, n * P:(n + 1) * P]
                        else:
                            lhsT = mixedT[:, k, n * P:(n + 1) * P]
                        last = t.matmul(bank[i % 4][:, :], lhsT, unit(1 + half)[:, k, :], start=(k == 0), stop=(k == KD - 1))
                    last.then_inc(wout_done, 1)

            def route(n):
                pe.wait_ge(xn2_ready, n + 1)
                for half in range(2):
                    i = 2 * n + half
                    if i >= 3:
                        j = i - 3
                        pe.wait_ge(xn2T_act if j % 2 else xn2T_dve, j // 2 + 1)
                    for c in range(4):
                        k = 4 * half + c
                        last = t.transpose(bank[4 + i % 3][:, c * P:(c + 1) * P], xn2[:, n, k * P:(k + 1) * P], ident[:, :])
                    last.then_inc(xn2_transposed, 1)
                if n:
                    pe.wait_ge(logits_ready, n)
                pe.wait_ge(xn2T_act, n + 1)
                pe.wait_ge(xn2T_dve, n + 1)
                for k in range(KD):
                    last = t.matmul(bank[7][:, n * 32:(n + 1) * 32], xn2T[n // 2][:, n % 2, k, :], wr[:, k, :],
                                    start=(k == 0), stop=(k == KD - 1))
                last.then_inc(logits_done, 1)

            pe.wait_ge(silu_ready, CC)
            pe.wait_ge(oT_ready, NQ)
            pe.wait_ge(wout_loaded, 32)
            pe.wait_ge(router_loaded, 32)
            project_out(0)
            project_out(1)
            route(0)
            project_out(2)
            route(1)
            project_out(3)
            route(2)
            route(3)
            pe.wait_ge(chosen_ready, 1)
            for n in range(NQ):
                for m in range(n + 1):
                    last = t.matmul(bank[0][:, n * 32:(n + 1) * 32], (before if m == n else ones_w)[:, :], chosen[:, m, :],
                                    start=(m == 0), stop=(m == n))
            for m in range(NQ):
                last = t.matmul(bank[0][:, NQ * 32:NQ * 32 + 32], ones_w[:, :], chosen[:, m, :], start=(m == 0), stop=(m == NQ - 1))
            last.then_inc(rank_done, 1)
            pe.wait_ge(onehots_ready, 2)
            for i in range(NJ):
                last = t.matmul(bank[1][0:CAP, 0:COLS], pos_1h[:, i, :], blk_1h[:, i, :], start=(i == 0), stop=(i == NJ - 1))
            last.then_inc(table_done, 1)

            def transpose_x(b):
                pe.wait_ge(xg_loaded, 16 * (b + 1))
                for k in range(KD):
                    last = t.transpose(bank[6 + k // 4][:, (k % 4) * CAP:(k % 4 + 1) * CAP], xg[0:CAP, k * P:(k + 1) * P],
                                       ident[0:CAP, 0:CAP])
                last.then_inc(xg_transposed, 1)

            def transpose_y(b):
                pe.wait_ge(yT_ready, 8 * (b + 1))
                for half in range(2):
                    for c in range(4):
                        last = t.transpose(bank[6 + half][0:CAP, c * P:(c + 1) * P], yT[:, 4 * half + c, :], ident[:, :])
                    last.then_inc(y_transposed, 1)

            def pe_block(b, first=False):
                for i in range(4):
                    pe.wait_ge(w_loaded[i], 16 * (b + 1))
                    if i == 0:
                        pe.wait_ge(xT_ready, 2 * (b + 1))
                    for c in range(4):
                        for k in range(KD):
                            last = t.matmul(bank[i][:, c * CAP:(c + 1) * CAP], unit(i)[:, k, c * P:(c + 1) * P], xT[:, k, :],
                                            start=(k == 0), stop=(k == KD - 1))
                    last.then_inc(gu_done, 1)
                    if i == 0 and not first:
                        transpose_y(b - 1)
                if not first:
                    pe.wait_ge(y_ready, 2 * b)
                transpose_x(b + 1)
                for half in range(2):
                    pe.wait_ge(w_loaded[4 + half], 16 * (b + 1))
                    if half == 0:
                        for k in range(KD):
                            if k % 4 == 0:
                                pe.wait_ge(hT_ready, 2 * b + k // 4 + 1)
                            for c in range(4):
                                last = t.matmul(bank[4][:, c * CAP:(c + 1) * CAP], unit(4)[:, k, c * P:(c + 1) * P], hT[:, k, :],
                                                start=(k == 0 and c == 0), stop=(k == KD - 1), skip_group_check=True)
                    else:
                        for c in range(4):
                            for k in range(KD):
                                last = t.matmul(bank[5][:, c * CAP:(c + 1) * CAP], unit(5)[:, k, c * P:(c + 1) * P], hT[:, k, :],
                                                start=(k == 0), stop=(k == KD - 1))
                    last.then_inc(down_done, 1)

            transpose_x(0)
            pe_block(0, first=True)
            with pe.Fori(1, N_EXPERTS) as b:
                pe_block(b)
            pe.wait_ge(overflow_ready, 2)
            trips = pe.value_load(n_ovf[0:1, 0:1], min_val=0, max_val=MAX_OVERFLOW)
            with pe.If(trips > 0):
                with pe.Fori(N_EXPERTS, trips + N_EXPERTS) as b:
                    pe_block(b)
            pe.wait_ge(xT_ready, 2 * (trips + N_EXPERTS + 1))
            transpose_y(trips + N_EXPERTS - 1)


_INS = ['x', 'g_mix', 'w_in', 'b_in', 'conv_w', 'conv_b', 'ln_g', 'ln_b', 'rpb', 'w_out', 'b_out', 'g_ffn',
        'w_router', 'b_router', 'w_gate', 'b_gate', 'w_up', 'b_up', 'w_down', 'b_down', 'g_final']


def kernel(**inputs):
    import numpy as _np
    import concourse.bacc as _bacc
    from concourse import mybir as _mybir
    from concourse.bass_utils import run_bass_kernel_spmd as _run

    nc = _bacc.Bacc("TRN2", target_bir_lowering=False, num_devices=1)
    arrays, args = {}, []
    for name in _INS:
        a = _np.ascontiguousarray(inputs[name])
        arrays[f"in_{name}"] = a
        args.append(nc.dram_tensor(f"in_{name}", a.shape, _mybir.dt.from_np(a.dtype), kind="ExternalInput").ap())
    args.append(nc.dram_tensor("out_0", (1, SEQ, D_MODEL), F32, kind="ExternalOutput").ap())
    encoder_kernel(nc, *args)
    r = _run(nc, [arrays], core_ids=[0])
    return r.results[0]["out_0"]
```

```python
import numpy as np
import concourse.bass as bass
from concourse import mybir
from contextlib import ExitStack

F32 = mybir.dt.float32
F32R = mybir.dt.float32r
BF16 = mybir.dt.bfloat16
I32 = mybir.dt.int32
U32 = mybir.dt.uint32
ALU = mybir.AluOpType
ACT = mybir.ActivationFunctionType
AX = mybir.AxisListType

P = 128
SEQ, D_MODEL = 512, 1024
GRID_W, N_ROWS = 64, 8
QB = 16
NQ = GRID_W // QB
D_CONV, CONV_K = 512, 31
PAD = CONV_K // 2
HEADS, HEAD_DIM = 8, 64
WIN_H, WIN_W = 8, 16
N_EXPERTS, TOP_K, D_FF = 32, 4, 1024
EPS = 1e-5
SWIGLU_LIMIT, SWIGLU_ALPHA = 7.0, 1.702
NEG = 1e30

KD = D_MODEL // P
CC = D_CONV // P
HALF = D_MODEL // 2
RPB_H, RPB_W = 2 * WIN_H - 1, 2 * WIN_W - 1
RPB_PITCH = 64
RUN = WIN_H * RPB_PITCH

CAP = 112
EXTRA = (SEQ - 1) // CAP
MAX_OVERFLOW = (SEQ * TOP_K - 1) // CAP
N_BLOCKS = N_EXPERTS + MAX_OVERFLOW
COLS = N_BLOCKS + 2 - N_BLOCKS % 2
NJ = NQ * TOP_K
UNITS = 7
PIECES, PIECE = 12, 2048
HIGH_RING = 4
AHEAD = HIGH_RING - 1
POOL_PIECES = (11,)
DVE_PIECES = [i for i in range(PIECES) if i not in POOL_PIECES]


def encoder_kernel(nc, x, g_mix, w_in, b_in, conv_w, conv_b, ln_g, ln_b, rpb, w_out, b_out,
                   g_ffn, w_router, b_router, w_gate, b_gate, w_up, b_up, w_down, b_down,
                   g_final, out):
    ctx = ExitStack()
    with ctx:
        def sb(name, shape, dt=F32):
            return ctx.enter_context(nc.sbuf_tensor(name, shape, dt))

        def sem(name):
            return ctx.enter_context(nc.semaphore(name))

        rpb_pad = nc.dram_tensor("rpb_pad", [QB, HEADS * RPB_H + 1, RPB_PITCH], F32, kind="Internal").ap()
        xn2_rows = nc.dram_tensor("xn2_rows", [SEQ, D_MODEL], F32, kind="Internal").ap()
        y_rows = nc.dram_tensor("y_rows", [N_BLOCKS * CAP, D_MODEL], F32, kind="Internal").ap()

        free = [-(-nc.sbuf_base // 64) * 64]

        def area(name, shape, dt=F32):
            at = free[0]
            align = 32
            size = int(np.prod(shape[1:])) * (2 if dt == BF16 else 4)
            free[0] = at + -(-size // align) * align
            return nc.alloc_sbuf_tensor_at(name, shape, dt, offset=at), at

        def sb(name, shape, dt=F32):
            return area(name, shape, dt)[0]

        def over(name, at, word, shape, dt=F32R):
            return nc.alloc_sbuf_tensor_at(name, shape, dt, offset=at + 4 * word)

        h = sb("h", [P, NQ, D_MODEL])
        ring, ring_at = area("ring", [P, UNITS, KD * HALF])
        area_a, a_at = area("area_a", [P, 4096])
        area_q, q_at = area("area_q", [P, 2048])
        area_k, k_at = area("area_k", [P, 2048])
        area_v, v_at = area("area_v", [P, 2048])
        area_u, u_at = area("area_u", [P, CC * (SEQ + 2 * PAD)])
        area_m, m_at = area("area_m", [P, 4096])
        area_t, t_at = area("area_t", [P, HEADS * 384])
        w_high = over("w_high", ring_at, 0, [P, HIGH_RING, PIECE])
        piece_at = [(ring_at, 2 * 4096 + i * PIECE) for i in range(10)] + [(u_at, 0), (a_at, 2048)]
        w_raw = [over(f"w_raw{i}", *piece_at[i], [P, PIECE], F32) for i in range(PIECES)]
        w_low = [over(f"w_low{i}", *piece_at[i], [P, PIECE]) for i in range(PIECES)]
        bias_gu = over("bias_gu", a_at, 0, [P, D_MODEL])
        bias_d = over("bias_d", a_at, 1024, [P, D_MODEL])
        xT_high = over("xT_high", k_at, 0, [P, KD, CAP])
        xT_low = over("xT_low", k_at, 1024, [P, KD, CAP])
        hT_high = over("hT_high", m_at, 2048, [P, KD, CAP])
        hT_low = over("hT_low", m_at, 3072, [P, KD, CAP])
        pos_1h = over("pos_1h", t_at, 0, [P, NJ, CAP])
        blk_1h = over("blk_1h", t_at, NJ * CAP, [P, NJ, COLS])

        iota_i = over("iota_i", m_at, 1024, [P, 384], I32)
        iota_u = area_m[:, 1408:1792]
        before = area_m[:, 1792:1920]

        def unit(s):
            return ring[:, s, :].rearrange("p (k f) -> p k f", k=KD)

        xnT = area_a[:, :].rearrange("p (k t) -> p k t", k=KD)
        qT = area_q[:, :].rearrange("p (k t) -> p k t", k=4)
        kT = area_k[:, :].rearrange("p (k t) -> p k t", k=4)
        v_sb = area_v[:, :].rearrange("p (n f) -> p n f", n=NQ)
        u_pad = area_u[:, :].rearrange("p (c t) -> p c t", c=CC)
        mixedT = area_m[:, :].rearrange("p (k t) -> p k t", k=KD)
        xn_tile = area_q[:, :].rearrange("p (b d) -> p b d", b=2)
        gmix_row = area_k[:, 0:1024]
        bout_row = area_k[:, 1024:2048]
        zeros = ring[:, 6, 0:D_MODEL]
        sg = area_v[:, 0:1024].rearrange("p (b t) -> p b t", b=2)
        stage = area_m[:, 0:1024].rearrange("p (s q) -> p s q", s=8)
        raw_bias = area_m[:, 2048:3072].rearrange("p (b t) -> p b t", b=2)
        mask = area_m[:, 3072:3072 + 896]
        sq = area_u[:, 0:1024].rearrange("p (b t) -> p b t", b=2)
        ln_rs = area_u[:, 1024:1536]
        silu_sig = area_u[:, 1536:2048]
        convT_out = [area_u[:, 0:512], area_u[:, 512:1024], area_u[:, 1024:1536], area_a[:, 3584:4096]]
        T_mid = area_t[:, :].rearrange("p (h t) -> p h t", h=HEADS)
        T_edge = ring[:, 0, :].rearrange("p (h e t) -> p h e t", h=HEADS, e=2)
        S_sb = area_a[:, 0:1152].rearrange("p (b t) -> p b t", b=3)
        P_sb = area_a[:, 1152:2304].rearrange("p (b t) -> p b t", b=3)
        PT_sb = area_a[:, 2304:3072].rearrange("p (b t) -> p b t", b=2)
        O_sb = area_a[:, 3072:3584]
        wr = area_t[:, 2048:2304].rearrange("p (k e) -> p k e", k=KD)
        br_row = area_t[:, 2304:2336]
        xn2 = area_a[:, :].rearrange("p (n d) -> p n d", n=NQ)
        xn2T = [a[:, :].rearrange("p (b k t) -> p b k t", b=2, k=KD) for a in (area_q, area_k)]
        gffn_row = area_v[:, 0:1024]
        gfin_row = area_v[:, 1024:2048]
        xg = area_m[:, 0:1024]
        y_sb = area_m[:, 1024:2048]
        bias_stage = area_v[:, 0:1024]
        g_lim = area_t[0:CAP, 0:1024].rearrange("p (b f) -> p b f", b=2)
        g_silu = area_t[0:CAP, 1024:2048].rearrange("p (b f) -> p b f", b=2)
        u_lim = area_q[0:CAP, 0:1024].rearrange("p (b f) -> p b f", b=2)
        h_tok = area_q[0:CAP, 1024:2048].rearrange("p (b f) -> p b f", b=2)
        exp_1h = area_u[:, 0:512].rearrange("p (i e) -> p i e", i=NJ)
        picked = area_u[:, 512:1024].rearrange("p (i e) -> p i e", i=NJ)
        cmp = area_u[:, 1024:1024 + MAX_OVERFLOW * N_EXPERTS]
        junk_norm = [area_t[:, 0:1024], area_t[:, 1024:2048]]
        junk = area_t[:, 0:1024]
        y_tok = ring[:, :, :].rearrange("p s f -> p (s f)").rearrange("p (i d) -> p i d", d=D_MODEL)

        rpb_tile = area_t[0:HEADS * RPB_H + 1, 2048:2048 + RPB_PITCH]
        neg_max, row_max, row_sum = (area_u[:, 2048 + 32 * i:2080 + 32 * i] for i in range(3))
        late_at = NJ * (CAP + COLS)
        top_val = area_t[:, late_at:late_at + 32].rearrange("p (n j) -> p n j", n=NQ)
        top_idx = over("top_idx", t_at, late_at + 32, [P, NQ, 8], U32)
        chosen = over("chosen", t_at, late_at + 64, [P, NQ, N_EXPERTS], BF16)
        tok_tab = over("tok_tab", t_at, late_at + 128, [CAP, COLS], I32)
        gates = area_t[:, late_at + 128 + COLS:late_at + 144 + COLS].rearrange("p (n j) -> p n j", n=NQ)
        gate_neg, gate_sum = (area_t[:, late_at + 144 + COLS + NQ * i:late_at + 148 + COLS + NQ * i] for i in range(2))
        first_slot, pos_i, slot = (over(name, t_at, 2048 + NJ * i, [P, NJ], I32)
                                   for i, name in enumerate(("first_slot", "pos_i", "slot")))
        ovf_exp = over("ovf_exp", t_at, 2048 + 3 * NJ, [1, MAX_OVERFLOW], I32)
        e_idx, rank, first_j, extra_j, is_extra, blk, pos, tmp_j = (area_q[:, NJ * i:NJ * (i + 1)] for i in range(8))
        counts, n_extra, first_extra, ovf_exp_f = (area_q[:, 128 + 32 * i:160 + 32 * i] for i in range(4))
        ovf_exp_f = ovf_exp_f[0:1, 0:MAX_OVERFLOW]
        cum = area_q[:, 256:256 + 4 * N_EXPERTS].rearrange("p (b e) -> p b e", b=2)

        ident = sb("ident", [P, P])
        mean_w, mean_at = area("mean_w", [P, P])
        selector = over("selector", mean_at, 0, [P, CAP])
        is_expert = sb("is_expert", [P, N_EXPERTS])
        ones_b = sb("ones_b", [P, P], BF16)
        before_b = sb("before_b", [P, P], BF16)
        colT = sb("colT", [P, 32])
        convT = sb("convT", [P, P])
        logits = convT[:, :].rearrange("p (n e) -> p n e", n=NQ)
        bq = sb("bq", [P, 4])
        p_int = sb("p_int", [P, 3], I32)
        c_flt = sb("c_flt", [P, 2])
        win_lo = sb("win_lo", [P, 3])
        win_hi = sb("win_hi", [P, 3])
        iota_f = sb("iota_f", [P, 128])
        thresholds = sb("thresholds", [P, EXTRA])
        tok_id = sb("tok_id", [P, NQ])
        minus_half = sb("minus_half", [P, 1])
        eps_col = sb("eps_col", [P, 1])
        ss = sb("ss", [P, 3 * NQ])
        ms = sb("ms", [P, 3 * NQ])
        rstd = sb("rstd", [P, 3 * NQ])
        row_inv = sb("row_inv", [P, 32])
        tok_now = sb("tok_now", [CAP, 1], I32)
        n_ovf = sb("n_ovf", [1, 1], I32)

        bank = [ctx.enter_context(nc.psum_tensor(f"bank{i}", [P, 512], F32)) for i in range(8)]

        x_loaded = [sem(f"x_loaded{n}") for n in range(NQ)]
        win_loaded = [sem(f"win_loaded{i}") for i in range(5)]
        wout_loaded = sem("wout_loaded")
        raw_piece = [sem(f"raw_piece{i}") for i in range(PIECES)]
        rows_loaded = sem("rows_loaded")
        bout_loaded = sem("bout_loaded")
        stage_loaded = sem("stage_loaded")
        router_loaded = sem("router_loaded")
        norm_rows_loaded = sem("norm_rows_loaded")
        rpb_tile_loaded = sem("rpb_tile_loaded")
        rpb_stored = sem("rpb_stored")
        raw_loaded = sem("raw_loaded")
        consts_ready = sem("consts_ready")
        iotas_ready = sem("iotas_ready")
        upad_zeroed = sem("upad_zeroed")
        rpb_zeroed = sem("rpb_zeroed")
        mask_step = sem("mask_step")
        ss_ready = sem("ss_ready")
        ms_ready = sem("ms_ready")
        rstd_ready = sem("rstd_ready")
        xn_ready = sem("xn_ready")
        xn_transposed = sem("xn_transposed")
        xnT_dve = sem("xnT_dve")
        xnT_act = sem("xnT_act")
        stage_transposed = sem("stage_transposed")
        cols_ready = sem("cols_ready")
        bq_ready = sem("bq_ready")
        xb_ready = sem("xb_ready")
        proj_done = sem("proj_done")
        act_evac = sem("act_evac")
        glu_ready = sem("glu_ready")
        conv_tap = sem("conv_tap")
        tables_ready = sem("tables_ready")
        mean_done = sem("mean_done")
        centred = sem("centred")
        squared = sem("squared")
        var_part = sem("var_part")
        std_ready = sem("std_ready")
        ln_rs_ready = sem("ln_rs_ready")
        ln_scaled = sem("ln_scaled")
        ln_affine = sem("ln_affine")
        silu_sig_ready = sem("silu_sig_ready")
        silu_ready = sem("silu_ready")
        qk_done = sem("qk_done")
        s_ready = sem("s_ready")
        neg_max_ready = sem("neg_max_ready")
        exp_ready = sem("exp_ready")
        p_transposed = sem("p_transposed")
        pT_dve = sem("pT_dve")
        pT_act = sem("pT_act")
        pv_done = sem("pv_done")
        inv_ready = sem("inv_ready")
        o_ready = sem("o_ready")
        o_transposed = sem("o_transposed")
        oT_ready = sem("oT_ready")
        wout_done = sem("wout_done")
        h_ready = sem("h_ready")
        ss2_ready = sem("ss2_ready")
        xn2_ready = sem("xn2_ready")
        xn2_stored = sem("xn2_stored")
        xn2_transposed = sem("xn2_transposed")
        xn2T_act = sem("xn2T_act")
        xn2T_dve = sem("xn2T_dve")
        logits_done = sem("logits_done")
        logits_ready = sem("logits_ready")
        top_ready = sem("top_ready")
        gate_exp = sem("gate_exp")
        gates_ready = sem("gates_ready")
        route_step = sem("route_step")
        chosen_ready = sem("chosen_ready")
        rank_done = sem("rank_done")
        onehots_ready = sem("onehots_ready")
        table_done = sem("table_done")
        table_ready = sem("table_ready")
        slot_ready = sem("slot_ready")
        zeros_ready = sem("zeros_ready")
        overflow_ready = sem("overflow_ready")
        xg_loaded = sem("xg_loaded")
        xg_transposed = sem("xg_transposed")
        high_ready = sem("high_ready")
        low_dve = sem("low_dve")
        low_pool = sem("low_pool")
        piece_used = sem("piece_used")
        selector_ready = sem("selector_ready")
        bias_rows_loaded = sem("bias_rows_loaded")
        bias_high = sem("bias_high")
        bias_split = sem("bias_split")
        xT_high_ready = sem("xT_high_ready")
        xT_low_ready = sem("xT_low_ready")
        g_limited = sem("g_limited")
        g_sig_ready = sem("g_sig_ready")
        g_silu_ready = sem("g_silu_ready")
        u_limited = sem("u_limited")
        h_tok_ready = sem("h_tok_ready")
        h_transposed = sem("h_transposed")
        hT_high_ready = sem("hT_high_ready")
        hT_low_ready = sem("hT_low_ready")
        y_ready = sem("y_ready")
        y_stored = sem("y_stored")
        y_back = [sem(f"y_back{n}") for n in range(NQ)]
        combined = sem("combined")
        ss3_ready = sem("ss3_ready")
        final_ready = sem("final_ready")
        out_stored = sem("out_stored")

        def row_bcast(ap, n, offset=0):
            return bass.AP(ap.tensor, ap.offset + offset, [[0, P], [1, n]])

        def by_block(ap):
            return ap[0].rearrange("(r n c) d -> n r c d", r=N_ROWS, c=QB)

        x_blocks, out_blocks = by_block(x), by_block(out)
        win_v = w_in[0].rearrange("(k p) f -> p k f", p=P)
        wout_v = w_out[0].rearrange("(k p) f -> p k f", p=P)
        wg_v, wu_v, wd_v = (w[0].rearrange("e (k p) f -> e p k f", p=P) for w in (w_gate, w_up, w_down))

        def piece_src(i, e):
            if i < 8:
                mat, half, ks = (wg_v, wu_v)[i // 2 % 2], i // 4, i % 2
                return mat[e, :, 4 * ks:4 * ks + 4, half * HALF:(half + 1) * HALF]
            return wd_v[e, :, 2 * (i - 8):2 * (i - 8) + 2, :]

        def wait_low(eng, b, i):
            if i in POOL_PIECES:
                eng.wait_ge(low_pool, len(POOL_PIECES) * b + POOL_PIECES.index(i) + 1)
            else:
                eng.wait_ge(low_dve, len(DVE_PIECES) * b + DVE_PIECES.index(i) + 1)

        def keys_of(n):
            return max(n - 1, 0), min(n + 2, NQ)

        def table_of(n, hd):
            if n == 0:
                return T_edge[:, hd, 0, :]
            if n == NQ - 1:
                return T_edge[:, hd, 1, :]
            return T_mid[:, hd, :]

        steps = [(n, hd) for n in range(NQ) for hd in range(HEADS)]
        NS = len(steps)

        block = ctx.enter_context(nc.Block())

        @block.sync
        def _(sp):
            for n in range(NQ):
                sp.dma_start(h[:, n, :], x_blocks[n]).then_inc(x_loaded[n], 16)
            for i, col in enumerate((1, 0, 2, 3, 4)):
                sp.dma_start(unit(1 + i), win_v[:, :, col * HALF:(col + 1) * HALF]).then_inc(win_loaded[i], 16)
            sp.wait_ge(rpb_tile_loaded, 16)
            for c in range(QB):
                sp.dma_start(rpb_pad[c], rpb_tile[:, :]).then_inc(rpb_stored, 16)
            sp.wait_ge(rpb_stored, 16 * QB)
            copy_size = (HEADS * RPB_H + 1) * RPB_PITCH
            for pair in range(HEADS // 2):
                if pair:
                    sp.wait_ge(tables_ready, 6 * pair)
                for r in range(N_ROWS):
                    start = (2 * pair * RPB_H + WIN_H - 1 - r) * RPB_PITCH + QB - 1
                    src = bass.AP(rpb_pad.tensor, rpb_pad.offset + start,
                                  [[copy_size - 1, QB], [RPB_H * RPB_PITCH, 2], [1, RUN]])
                    sp.dma_start(raw_bias[r * QB:(r + 1) * QB, :, :], src).then_inc(raw_loaded, 16)
            spare = y_rows[N_EXPERTS * CAP:, :].rearrange("(p i) (j f) -> p (i j) f", p=CAP, f=D_MODEL)
            sp.wait_ge(zeros_ready, 1)
            sp.dma_start(spare, zeros[0:CAP].unsqueeze(1).to_broadcast([CAP, spare.shape[1], spare.shape[2]])).then_inc(y_stored, 16)
            sp.wait_ge(y_stored, 16)
            sp.dma_start(unit(6), wout_v[:, :, 0:HALF]).then_inc(wout_loaded, 16)
            sp.wait_ge(proj_done, 8)
            sp.dma_start(unit(1), wout_v[:, :, HALF:]).then_inc(wout_loaded, 16)

            def load(i, e):
                src = piece_src(i, e)
                sp.dma_start(w_raw[i][:, :].rearrange("p (k f) -> p k f", f=src.shape[2]), src).then_inc(raw_piece[i], 16)

            load(0, 0)
            load(1, 0)
            for g, i in ((12, 2), (16, 4), (20, 6)):
                sp.wait_ge(proj_done, g)
                load(i, 0)
                load(i + 1, 0)
            sp.wait_ge(wout_done, 2 * NQ)
            load(8, 0)
            load(9, 0)
            sp.wait_ge(overflow_ready, 2)
            load(10, 0)
            sp.wait_ge(xn2_stored, 16 * NQ)
            sp.wait_ge(xn2_transposed, 2 * NQ)
            load(11, 0)

            def weights(b, e):
                for i in range(PIECES):
                    sp.wait_ge(piece_used, PIECES * (b - 1) + i + 1)
                    load(i, e)

            with sp.Fori(1, N_EXPERTS) as b:
                weights(b, b)
            trips = sp.value_load(n_ovf[0:1, 0:1], min_val=0, max_val=MAX_OVERFLOW)
            with sp.If(trips > 0):
                with sp.Fori(N_EXPERTS, trips + N_EXPERTS) as b:
                    e = sp.value_load(ovf_exp[0:1, bass.ds(b - N_EXPERTS, 1)], min_val=0, max_val=N_EXPERTS - 1)
                    weights(b, e)
            for n in range(NQ):
                sp.wait_ge(final_ready, n + 1)
                sp.dma_start(out_blocks[n], y_tok[:, n * TOP_K, :]).then_inc(out_stored, 16)
            sp.wait_ge(out_stored, 16 * NQ)

        @block.gpsimd
        def _(pool):
            g = nc.gpsimd
            g.memset(minus_half[:, :], -0.5).then_inc(consts_ready, 1)
            g.memset(ident[:, :], 0.0).then_inc(consts_ready, 1)
            g.memset(ones_b[:, :], 1.0).then_inc(consts_ready, 1)
            g.memset(before, 1.0).then_inc(consts_ready, 1)
            g.memset(mean_w[:, :], 1.0 / D_CONV).then_inc(consts_ready, 1)
            g.memset(eps_col[:, :], EPS).then_inc(consts_ready, 1)
            pool.wait_ge(consts_ready, 6)
            g.affine_select(out=ident[:, :], in_=ident[:, :], compare_op=ALU.not_equal, fill=1.0,
                            base=0, pattern=[[-1, P]], channel_multiplier=1).then_inc(consts_ready, 1)
            g.affine_select(out=before, in_=before, compare_op=ALU.is_gt, fill=0.0,
                            base=0, pattern=[[1, P]], channel_multiplier=-1).then_inc(consts_ready, 1)
            g.memset(zeros, 0.0).then_inc(zeros_ready, 1)
            g.memset(rpb_tile[:, :], 0.0).then_inc(rpb_zeroed, 1)
            g.iota(iota_i[:, :], [[QB, 3], [0, N_ROWS], [1, QB]], base=0, channel_multiplier=0).then_inc(iotas_ready, 1)
            pool.wait_ge(consts_ready, 8)
            g.tensor_copy(before_b[:, :], before).then_inc(consts_ready, 1)
            g.iota(p_int[:, 0:1], [[0, 1]], base=0, channel_multiplier=1).then_inc(iotas_ready, 1)
            g.iota(iota_f[:, :], [[1, 128]], base=0, channel_multiplier=0,
                   allow_small_or_imprecise_dtypes=True).then_inc(iotas_ready, 1)
            g.iota(tok_id[:, :], [[P, NQ]], base=0, channel_multiplier=1,
                   allow_small_or_imprecise_dtypes=True).then_inc(iotas_ready, 1)
            g.iota(thresholds[:, :], [[CAP, EXTRA]], base=CAP, channel_multiplier=0,
                   allow_small_or_imprecise_dtypes=True).then_inc(iotas_ready, 1)
            g.memset(area_u[:, :], 0.0).then_inc(upad_zeroed, 1)
            pool.wait_ge(rpb_zeroed, 1)
            pool.dma_start(rpb_tile[0:HEADS * RPB_H, QB:QB + RPB_W],
                           rpb[0].rearrange("h a b -> (h a) b")).then_inc(rpb_tile_loaded, 16)

            def rstd_of(i, ready):
                g.tensor_scalar(ms[:, i:i + 1], ss[:, i:i + 1], 1.0 / D_MODEL, EPS, ALU.mult, ALU.add).then_inc(ms_ready, 1)
                pool.wait_ge(ms_ready, i + 1)
                g.tensor_tensor(rstd[:, i:i + 1], ms[:, i:i + 1], minus_half[:, :], ALU.pow).then_inc(rstd_ready, 1)

            for n in range(NQ):
                pool.wait_ge(ss_ready, n + 1)
                rstd_of(n, ss_ready)
            pool.wait_ge(bout_loaded, 16)
            for n in range(NQ):
                pool.wait_ge(xn_ready, n + 1)
                g.tensor_tensor(h[:, n, :], h[:, n, :], bout_row, ALU.add).then_inc(xb_ready, 1)
            pool.wait_ge(mask_step, 13)

            for hd in range(HEADS):
                pool.wait_ge(raw_loaded, 16 * N_ROWS * (hd // 2 + 1))
                raw = raw_bias[:, hd % 2, :].rearrange("p (r w) -> p r w", r=N_ROWS)
                for kind, (dst, m0, m1, o) in enumerate(((T_mid[:, hd, :], 0, 3, 0), (T_edge[:, hd, 0, :], 1, 3, 384),
                                                         (T_edge[:, hd, 1, :], 0, 2, 640))):
                    w = (m1 - m0) * P
                    src = raw[:, :, m0 * QB:m1 * QB].rearrange("p r (m c) -> p m r c", c=QB)
                    g.tensor_tensor(dst.rearrange("p (m r c) -> p m r c", r=N_ROWS, c=QB), src,
                                    mask[:, o:o + w].rearrange("p (m r c) -> p m r c", r=N_ROWS, c=QB),
                                    ALU.add).then_inc(tables_ready, 1)
            for c in range(CC):
                pool.wait_ge(ln_rs_ready, 1)
                g.tensor_tensor(mixedT[:, c, :], mixedT[:, c, :], ln_rs, ALU.mult).then_inc(ln_scaled, 1)
            for c in range(CC):
                pool.wait_ge(silu_sig_ready, c + 1)
                g.tensor_scalar(mixedT[:, c, :], mixedT[:, c, :], colT[:, 24 + c:25 + c], colT[:, 28 + c:29 + c],
                                ALU.mult, ALU.add).then_inc(ln_affine, 1)
                pool.wait_ge(ln_affine, c + 1)
                natural = [a.rearrange("p (r n q) -> p n r q", n=NQ, q=QB) for a in (mixedT[:, c, :], silu_sig)]
                g.tensor_tensor(convT_out[c].rearrange("p (n r q) -> p n r q", n=NQ, q=QB), *natural, ALU.mult).then_inc(silu_ready, 1)
            for n in range(NQ):
                pool.wait_ge(ss2_ready, n + 1)
                rstd_of(NQ + n, ss2_ready)

            def gather(b):
                g.tensor_copy(tok_now[:, :], tok_tab[:, bass.ds(b, 1)])
                pool.drain()
                g.indirect_dma_start(out=xg[0:CAP, :], out_offset=None, in_=xn2_rows,
                                     in_offset=bass.IndirectOffsetOnAxis(ap=tok_now[:, 0:1], axis=0)).then_inc(xg_loaded, 16)

            pool.wait_ge(table_ready, 1)
            pool.wait_ge(xn2_stored, 16 * NQ)
            pool.wait_ge(wout_done, 2 * NQ)
            gather(0)

            def select(e):
                g.tensor_copy(selector[:, :], is_expert[:, bass.ds(e, 1)].to_broadcast([P, CAP])).then_inc(selector_ready, 1)

            def low_part(b, i):
                pool.wait_ge(high_ready, PIECES * b + i + 1)
                g.tensor_tensor(w_low[i][:, :], w_raw[i][:, :],
                                w_high[:, i % HIGH_RING, :].bitcast(F32), ALU.subtract).then_inc(low_pool, 1)

            def silu(b, half):
                pool.wait_ge(g_sig_ready, 2 * b + half + 1)
                g.tensor_tensor(g_silu[:, half], g_lim[:, half], g_silu[:, half], ALU.mult).then_inc(g_silu_ready, 1)

            def pool_block(b, next_e=None):
                pool.wait_ge(xg_loaded, 16 * (b + 1))
                pool.wait_ge(xg_transposed, b + 1)
                gather(b + 1)
                silu(b, 0)
                for i in POOL_PIECES:
                    if i < 7:
                        low_part(b, i)
                silu(b, 1)
                for i in POOL_PIECES:
                    if i >= 7:
                        low_part(b, i)
                if next_e is not None:
                    pool.wait_ge(piece_used, PIECES * b + 9)
                    select(next_e)

            select(0)
            pool_block(0, 1)
            with pool.Fori(1, N_EXPERTS - 1) as b:
                pool_block(b, b + 1)
            pool_block(N_EXPERTS - 1)
            pool.wait_ge(overflow_ready, 2)
            trips = pool.value_load(n_ovf[0:1, 0:1], min_val=0, max_val=MAX_OVERFLOW)
            with pool.If(trips > 0):
                with pool.Fori(N_EXPERTS, trips + N_EXPERTS) as b:
                    e = pool.value_load(ovf_exp[0:1, bass.ds(b - N_EXPERTS, 1)], min_val=0, max_val=N_EXPERTS - 1)
                    pool.wait_ge(piece_used, PIECES * b)
                    select(e)
                    pool_block(b)
            pool.wait_ge(slot_ready, 1)
            pool.wait_ge(y_stored, 16 * (trips + N_EXPERTS + 1))
            g.tensor_tensor(slot[:, :], first_slot[:, :], pos_i[:, :], ALU.add).then_inc(slot_ready, 1)
            pool.wait_ge(slot_ready, 2)
            for i in range(NJ):
                g.indirect_dma_start(out=y_tok[:, i, :], out_offset=None, in_=y_rows,
                                     in_offset=bass.IndirectOffsetOnAxis(ap=slot[:, i:i + 1], axis=0)).then_inc(y_back[i // TOP_K], 16)
            for n in range(NQ):
                pool.wait_ge(ss3_ready, n + 1)
                rstd_of(2 * NQ + n, ss3_ready)

        @block.scalar
        def _(act):
            s = nc.scalar
            act.dma_start(gmix_row, row_bcast(g_mix, D_MODEL)).then_inc(rows_loaded, 16)
            act.dma_start(stage[0:20, 0, :], b_in[0].rearrange("(c p) -> c p", p=P)).then_inc(stage_loaded, 16)
            for i, vec in enumerate((conv_b, ln_g, ln_b)):
                act.dma_start(stage[20 + CC * i:20 + CC * (i + 1), 0, :],
                              vec[0].rearrange("(c p) -> c p", p=P)).then_inc(stage_loaded, 16)
            act.dma_start(stage[0:CONV_K * CC, 1, :],
                          conv_w[0].rearrange("k (c p) -> (k c) p", p=P)).then_inc(stage_loaded, 16)
            act.dma_start(bout_row, row_bcast(b_out, D_MODEL)).then_inc(bout_loaded, 16)

            def xnT_half(n):
                act.wait_ge(xn_transposed, 2 * n + 2)
                s.copy(xnT[:, 4:8, n * P:(n + 1) * P],
                       bank[4 + (2 * n + 1) % 4][:, :].rearrange("p (k t) -> p k t", k=4)).then_inc(xnT_act, 1)

            def pT_out(j):
                m0, m1 = keys_of(steps[j][0])
                w = (m1 - m0) * P
                act.wait_ge(p_transposed, j + 1)
                s.copy(PT_sb[:, 1, 0:w], bank[6][:, 0:w]).then_inc(pT_act, 1)

            for n in range(NQ):
                act.wait_ge(x_loaded[n], 16)
                if n:
                    act.wait_ge(ss_ready, n)
                s.activation(junk_norm[n % 2], h[:, n, :], ACT.Square, accum_out=ss[:, n:n + 1]).then_inc(ss_ready, 1)
            for n in range(NQ):
                xnT_half(n)
            act.wait_ge(cols_ready, 1)
            for c in range(CC):
                act.wait_ge(proj_done, 2 * c + 1)
                if c >= 2:
                    act.wait_ge(glu_ready, 4 * (c - 1))
                s.activation(sg[:, c % 2, :], bank[2 * c % 4][:, :], ACT.Sigmoid, bias=colT[:, 4 + c:5 + c]).then_inc(act_evac, 1)
            act.wait_ge(bq_ready, 1)
            for i in range(4):
                act.wait_ge(proj_done, 8 + i + 1)
                s.activation(qT[:, i, :], bank[i][:, :], ACT.Identity, bias=bq[:, i:i + 1], scale=HEAD_DIM ** -0.5).then_inc(act_evac, 1)
            act.wait_ge(xb_ready, NQ)
            for i in range(4):
                act.wait_ge(proj_done, 12 + i + 1)
                s.activation(kT[:, i, :], bank[i][:, :], ACT.Identity, bias=colT[:, 12 + i:13 + i]).then_inc(act_evac, 1)
            act.wait_ge(glu_ready, 16)
            for n in range(NQ):
                act.wait_ge(proj_done, 16 + n + 1)
                s.copy(v_sb[:, n, :], bank[n][:, :]).then_inc(act_evac, 1)
            for c in range(CC):
                act.wait_ge(centred, c + 1)
                if c >= 2:
                    act.wait_ge(var_part, c - 1)
                s.activation(sq[:, c % 2, :], mixedT[:, c, :], ACT.Square).then_inc(squared, 1)
            act.wait_ge(var_part, CC)
            s.activation(ln_rs, bank[5][:, :], ACT.Sqrt, bias=eps_col[:, :]).then_inc(std_ready, 1)
            for i in range(NS):
                n, hd = steps[i]
                m0, m1 = keys_of(n)
                w = (m1 - m0) * P
                act.wait_ge(neg_max_ready, i + 1)
                if i >= 3:
                    act.wait_ge(p_transposed, i - 2)
                s.activation(P_sb[:, i % 3, 0:w], S_sb[:, i % 3, 0:w], ACT.Exp, bias=neg_max[:, i:i + 1],
                             accum_out=row_sum[:, i:i + 1]).then_inc(exp_ready, 1)
                j = i - 2
                if j >= 1 and j % 2:
                    pT_out(j)
                if i == 8:
                    for c in range(CC):
                        act.wait_ge(ln_scaled, c + 1)
                        if c >= 1:
                            act.wait_ge(silu_ready, c)
                        s.activation(silu_sig, mixedT[:, c, :], ACT.Sigmoid, bias=colT[:, 28 + c:29 + c],
                                     scale=colT[:, 24 + c:25 + c]).then_inc(silu_sig_ready, 1)
            pT_out(NS - 1)

            act.wait_ge(pv_done, NS)
            act.dma_start(br_row, row_bcast(b_router, N_EXPERTS)).then_inc(router_loaded, 16)
            act.dma_start(wr[:, :, :], w_router[0].rearrange("(k p) e -> p k e", p=P)).then_inc(router_loaded, 16)
            act.dma_start(gffn_row, row_bcast(g_ffn, D_MODEL)).then_inc(norm_rows_loaded, 16)
            act.dma_start(gfin_row, row_bcast(g_final, D_MODEL)).then_inc(norm_rows_loaded, 16)

            def square2(n):
                act.wait_ge(h_ready, 2 * n + 2)
                if n:
                    act.wait_ge(ss2_ready, n)
                s.activation(junk, h[:, n, :], ACT.Square, accum_out=ss[:, NQ + n:NQ + n + 1]).then_inc(ss2_ready, 1)

            def xn2T_half(n):
                act.wait_ge(xn2_ready, n + 1)
                act.dma_start(xn2_rows[n * P:(n + 1) * P, :], xn2[:, n, :]).then_inc(xn2_stored, 16)
                act.wait_ge(xn2_transposed, 2 * n + 2)
                s.copy(xn2T[n // 2][:, n % 2, 4:8, :],
                       bank[4 + (2 * n + 1) % 3][:, :].rearrange("p (k t) -> p k t", k=4)).then_inc(xn2T_act, 1)

            square2(0)
            square2(1)
            xn2T_half(0)
            square2(2)
            xn2T_half(1)
            square2(3)
            xn2T_half(2)
            xn2T_half(3)

            def high_part(b, i, first=False):
                act.wait_ge(raw_piece[i], 16 * (b + 1))
                if not (first and i <= AHEAD):
                    act.wait_ge(piece_used, PIECES * b + i - AHEAD)
                s.copy(w_high[:, i % HIGH_RING, :], w_raw[i][:, :]).then_inc(high_ready, 1)

            act.wait_ge(wout_done, 2 * NQ)
            for i in range(AHEAD):
                high_part(0, i, first=True)
            for n in range(NQ):
                act.wait_ge(top_ready, n + 1)
                s.mul(gate_neg[:, n:n + 1], top_val[:, n, 0:1], -1.0).then_inc(gate_exp, 1)
                act.wait_ge(gate_exp, 2 * n + 1)
                s.activation(gates[:, n, :], top_val[:, n, 0:TOP_K], ACT.Exp, bias=gate_neg[:, n:n + 1],
                             accum_out=gate_sum[:, n:n + 1]).then_inc(gate_exp, 1)
            act.wait_ge(xn2_transposed, 2 * NQ)
            act.wait_ge(xn2_stored, 16 * NQ)
            for i, mat in enumerate((b_gate, b_gate, b_up, b_up)):
                act.dma_start(bias_stage[32 * i:32 * i + 32, :], mat[0]).then_inc(bias_rows_loaded, 16)
            act.wait_ge(bias_rows_loaded, 64)
            s.copy(bias_gu[:, :], bias_stage).then_inc(bias_high, 1)
            act.wait_ge(bias_split, 2)
            for i in range(2):
                act.dma_start(bias_stage[32 * i:32 * i + 32, :], b_down[0]).then_inc(bias_rows_loaded, 16)
            act.wait_ge(bias_rows_loaded, 96)
            s.copy(bias_d[0:64, :], bias_stage[0:64, :]).then_inc(bias_high, 1)

            def rows_out(b):
                act.wait_ge(y_stored, 16 * (b + 1))
                act.wait_ge(piece_used, PIECES * (b + 1))
                for half in range(2):
                    s.copy(y_sb[0:CAP, half * HALF:(half + 1) * HALF], bank[4 + half][0:CAP, :]).then_inc(y_ready, 1)
                act.wait_ge(y_ready, 2 * b + 2)
                act.dma_start(y_rows[bass.ds(b * CAP, CAP), :], y_sb[0:CAP, :]).then_inc(y_stored, 16)

            def sigmoid(b, half):
                act.wait_ge(g_limited, 2 * b + half + 1)
                s.activation(g_silu[:, half], g_lim[:, half], ACT.Sigmoid, scale=SWIGLU_ALPHA).then_inc(g_sig_ready, 1)

            def four(ap, half):
                return ap[:, 4 * half:4 * half + 4, :]

            def out_of(i):
                return bank[i][:, 0:4 * CAP].rearrange("p (k t) -> p k t", k=4)

            def hT_high_part(b, half):
                act.wait_ge(h_transposed, 2 * b + half + 1)
                s.copy(four(hT_high, half), out_of(6 + half)).then_inc(hT_high_ready, 1)

            def xT_high_part(b, half):
                act.wait_ge(xg_transposed, b + 1)
                s.copy(four(xT_high, half), out_of(6 + half)).then_inc(xT_high_ready, 1)

            def act_block(b, first=False, has_next=True):
                for i in range(PIECES):
                    if i >= 10:
                        xT_high_part(b + 1, i - 10)
                    if i == 6:
                        hT_high_part(b, 0)
                    if i == 9:
                        hT_high_part(b, 1)
                    if i + AHEAD < PIECES:
                        high_part(b, i + AHEAD, first)
                    elif has_next:
                        high_part(b + 1, i + AHEAD - PIECES)
                    if i in (2, 6):
                        sigmoid(b, i // 4)
                    if i == 0 and not first:
                        rows_out(b - 1)

            for half in range(2):
                xT_high_part(0, half)
            act_block(0, first=True)
            with act.Fori(1, N_EXPERTS - 1) as b:
                act_block(b)
            act_block(N_EXPERTS - 1, has_next=False)
            act.wait_ge(overflow_ready, 2)
            trips = act.value_load(n_ovf[0:1, 0:1], min_val=0, max_val=MAX_OVERFLOW)
            with act.If(trips > 0):
                with act.Fori(N_EXPERTS, trips + N_EXPERTS) as b:
                    for i in range(AHEAD):
                        high_part(b, i)
                    act_block(b, has_next=False)
            rows_out(trips + N_EXPERTS - 1)
            for n in range(NQ):
                act.wait_ge(combined, TOP_K * (n + 1))
                if n:
                    act.wait_ge(ss3_ready, n)
                s.activation(junk, h[:, n, :], ACT.Square, accum_out=ss[:, 2 * NQ + n:2 * NQ + n + 1]).then_inc(ss3_ready, 1)

        @block.vector
        def _(dve):
            v = nc.vector
            dve.wait_ge(iotas_ready, 5)
            v.tensor_scalar(p_int[:, 1:2], p_int[:, 0:1], QB - 1, None, ALU.bitwise_and)
            v.tensor_scalar(p_int[:, 2:3], p_int[:, 0:1], N_EXPERTS - 1, None, ALU.bitwise_and).then_inc(mask_step, 1)
            v.tensor_copy(iota_u, iota_i[:, :]).then_inc(mask_step, 1)
            dve.wait_ge(mask_step, 2)
            v.tensor_copy(c_flt[:, :], p_int[:, 1:3]).then_inc(mask_step, 1)
            dve.wait_ge(mask_step, 3)
            v.tensor_scalar(win_lo[:, 0:1], c_flt[:, 0:1], WIN_W / 2, None, ALU.add)
            v.tensor_scalar(win_lo[:, 1:2], c_flt[:, 0:1], WIN_W / 2, float(QB), ALU.add, ALU.max)
            v.tensor_scalar(win_lo[:, 2:3], c_flt[:, 0:1], WIN_W / 2, float(QB), ALU.add, ALU.min).then_inc(mask_step, 3)
            dve.wait_ge(mask_step, 6)
            v.tensor_scalar(is_expert[:, :], iota_f[:, 0:N_EXPERTS], c_flt[:, 1:2], None, ALU.is_equal)
            v.tensor_scalar(win_hi[:, :], win_lo[:, :], WIN_W - 1.0, None, ALU.add)
            for kind, (o, a, w) in enumerate(((0, 0, 384), (384, 128, 256), (640, 0, 256))):
                v.tensor_scalar(mask[:, o:o + w], iota_u[:, a:a + w], win_lo[:, kind:kind + 1], None, ALU.is_ge).then_inc(mask_step, 1)
            dve.wait_ge(mask_step, 9)
            for kind, (o, a, w) in enumerate(((0, 0, 384), (384, 128, 256), (640, 0, 256))):
                v.scalar_tensor_tensor(mask[:, o:o + w], iota_u[:, a:a + w], win_hi[:, kind:kind + 1],
                                       mask[:, o:o + w], ALU.is_le, ALU.mult).then_inc(mask_step, 1)
            dve.wait_ge(mask_step, 12)
            v.tensor_scalar(mask, mask, -1.0, NEG, ALU.add, ALU.mult).then_inc(mask_step, 1)

            dve.wait_ge(rows_loaded, 16)
            for n in range(NQ + 1):
                if n < NQ:
                    dve.wait_ge(rstd_ready, n + 1)
                    if n >= 2:
                        dve.wait_ge(xn_transposed, 2 * (n - 1))
                    v.scalar_tensor_tensor(xn_tile[:, n % 2, :], h[:, n, :], rstd[:, n:n + 1], gmix_row,
                                           ALU.mult, ALU.mult).then_inc(xn_ready, 1)
                if n:
                    dve.wait_ge(xn_transposed, 2 * (n - 1) + 1)
                    v.tensor_copy(xnT[:, 0:4, (n - 1) * P:n * P],
                                  bank[4 + 2 * (n - 1) % 4][:, :].rearrange("p (k t) -> p k t", k=4)).then_inc(xnT_dve, 1)
            dve.wait_ge(stage_transposed, 1)
            v.tensor_copy(colT[:, :], bank[0][:, 0:32])
            v.tensor_copy(convT[:, 0:CONV_K * CC], bank[0][:, 32:32 + CONV_K * CC]).then_inc(cols_ready, 1)
            dve.wait_ge(cols_ready, 1)
            v.tensor_scalar(bq[:, :], colT[:, 8:12], HEAD_DIM ** -0.5, None, ALU.mult).then_inc(bq_ready, 1)
            dve.wait_ge(upad_zeroed, 1)
            for c in range(CC):
                dve.wait_ge(proj_done, 2 * c + 2)
                dve.wait_ge(act_evac, c + 1)
                dst = u_pad[:, c, PAD:PAD + SEQ].rearrange("p (r n q) -> p n r q", n=NQ, q=QB)
                for n in range(NQ):
                    v.scalar_tensor_tensor(dst[:, n], bank[(2 * c + 1) % 4][:, n * P:(n + 1) * P].rearrange("p (r q) -> p r q", q=QB),
                                           colT[:, c:c + 1],
                                           sg[:, c % 2, n * P:(n + 1) * P].rearrange("p (r q) -> p r q", q=QB),
                                           ALU.add, ALU.mult).then_inc(glu_ready, 1)
            dve.wait_ge(glu_ready, 16)
            for c in range(CC):
                v.tensor_scalar(mixedT[:, c, :], u_pad[:, c, 0:SEQ], convT[:, c:c + 1], colT[:, 20 + c:21 + c],
                                ALU.mult, ALU.add).then_inc(conv_tap, 1)
            with dve.Fori(1, CONV_K) as k:
                for c in range(CC):
                    dve.wait_ge(conv_tap, k * CC + c - (CC - 1))
                    v.scalar_tensor_tensor(mixedT[:, c, :], u_pad[:, c, bass.ds(k, SEQ)], convT[:, bass.ds(k * CC + c, 1)],
                                           mixedT[:, c, :], ALU.mult, ALU.add).then_inc(conv_tap, 1)
            dve.wait_ge(mean_done, 1)
            dve.wait_ge(conv_tap, CONV_K * CC)
            for c in range(CC):
                v.tensor_tensor(mixedT[:, c, :], mixedT[:, c, :], bank[4][:, :], ALU.subtract).then_inc(centred, 1)

            def scores(i):
                n, hd = steps[i]
                m0, m1 = keys_of(n)
                w = (m1 - m0) * P
                dve.wait_ge(qk_done, i + 1)
                if i >= 3:
                    dve.wait_ge(exp_ready, i - 2)
                v.tensor_tensor_reduce(out=S_sb[:, i % 3, 0:w], in0=bank[i % 3][:, 0:w], in1=table_of(n, hd),
                                       scale=1.0, scalar=-3.0e38, op0=ALU.add, op1=ALU.max,
                                       accum_out=row_max[:, i:i + 1]).then_inc(s_ready, 1)
                dve.wait_ge(s_ready, i + 1)
                v.tensor_scalar(neg_max[:, i:i + 1], row_max[:, i:i + 1], -1.0, None, ALU.mult).then_inc(neg_max_ready, 1)

            dve.wait_ge(tables_ready, 3 * HEADS)
            for i in range(NS + 4):
                if i < NS:
                    scores(i)
                if i == 1:
                    dve.wait_ge(std_ready, 1)
                    v.reciprocal(ln_rs, ln_rs).then_inc(ln_rs_ready, 1)
                j = i - 3
                if 0 <= j < NS and j % 2 == 0:
                    m0, m1 = keys_of(steps[j][0])
                    w = (m1 - m0) * P
                    dve.wait_ge(p_transposed, j + 1)
                    v.tensor_copy(PT_sb[:, 0, 0:w], bank[3][:, 0:w]).then_inc(pT_dve, 1)
                if i >= 11 and (i - 11) % HEADS == 0:
                    n = (i - 11) // HEADS
                    dve.wait_ge(exp_ready, HEADS * (n + 1))
                    v.reciprocal(row_inv[:, n * HEADS:(n + 1) * HEADS], row_sum[:, n * HEADS:(n + 1) * HEADS]).then_inc(inv_ready, 1)
                    dve.wait_ge(inv_ready, n + 1)
                    dve.wait_ge(pv_done, HEADS * (n + 1))
                    if n:
                        dve.wait_ge(o_transposed, n)
                    v.tensor_tensor(O_sb.rearrange("p (h d) -> p h d", d=HEAD_DIM),
                                    bank[7 if n % 2 == 0 else 4][:, :].rearrange("p (h d) -> p h d", d=HEAD_DIM),
                                    row_inv[:, n * HEADS:(n + 1) * HEADS].unsqueeze(2).to_broadcast([P, HEADS, HEAD_DIM]),
                                    ALU.mult).then_inc(o_ready, 1)
                    dve.wait_ge(o_transposed, n + 1)
                    v.tensor_tensor(mixedT[:, 4:8, n * P:(n + 1) * P], bank[5][:, :].rearrange("p (k t) -> p k t", k=4),
                                    colT[:, 16:20].unsqueeze(2).to_broadcast([P, 4, P]), ALU.add).then_inc(oT_ready, 1)

            def residual(n):
                for half in range(2):
                    dve.wait_ge(wout_done, 2 * n + half + 1)
                    v.tensor_tensor(h[:, n, half * HALF:(half + 1) * HALF], h[:, n, half * HALF:(half + 1) * HALF],
                                    bank[(2 * n + half) % 4][:, :], ALU.add).then_inc(h_ready, 1)

            def norm2(n):
                dve.wait_ge(rstd_ready, NQ + n + 1)
                v.scalar_tensor_tensor(xn2[:, n, :], h[:, n, :], rstd[:, NQ + n:NQ + n + 1], gffn_row,
                                       ALU.mult, ALU.mult).then_inc(xn2_ready, 1)
                dve.wait_ge(xn2_transposed, 2 * n + 1)
                v.tensor_copy(xn2T[n // 2][:, n % 2, 0:4, :],
                              bank[4 + 2 * n % 3][:, :].rearrange("p (k t) -> p k t", k=4)).then_inc(xn2T_dve, 1)

            def top(n):
                dve.wait_ge(logits_done, n + 1)
                v.tensor_tensor(logits[:, n, :], bank[7][:, n * 32:(n + 1) * 32], br_row, ALU.add).then_inc(logits_ready, 1)
                dve.wait_ge(logits_ready, n + 1)
                v.max(top_val[:, n, :], logits[:, n, :]).then_inc(top_ready, 1)
                dve.wait_ge(top_ready, n + 1)
                v.max_index(top_idx[:, n, :], top_val[:, n, :], logits[:, n, :]).then_inc(route_step, 1)

            dve.wait_ge(norm_rows_loaded, 32)
            dve.wait_ge(router_loaded, 32)
            residual(0)
            residual(1)
            norm2(0)
            residual(2)
            norm2(1)
            top(0)
            residual(3)
            norm2(2)
            top(1)
            norm2(3)
            top(2)
            top(3)

            def low_part(b, i):
                if i in DVE_PIECES:
                    dve.wait_ge(high_ready, PIECES * b + i + 1)
                    v.tensor_tensor(w_low[i][:, :], w_raw[i][:, :],
                                    w_high[:, i % HIGH_RING, :].bitcast(F32), ALU.subtract).then_inc(low_dve, 1)

            n_steps = [NQ]

            def then(ins):
                n_steps[0] += 1
                ins.then_inc(route_step, 1)
                dve.wait_ge(route_step, n_steps[0])

            def wide(ap, n):
                return ap.unsqueeze(2).to_broadcast([ap.shape[0], ap.shape[1], n])

            def across(ap, n):
                return ap.unsqueeze(1).to_broadcast([ap.shape[0], n, ap.shape[1]])

            dve.wait_ge(route_step, NQ)
            dve.wait_ge(ss2_ready, NQ)
            then(v.tensor_copy(e_idx[:, :].rearrange("p (n j) -> p n j", j=TOP_K), top_idx[:, :, 0:TOP_K]))
            then(v.tensor_tensor(exp_1h, across(iota_f[:, 0:N_EXPERTS], NJ), wide(e_idx[:, :], N_EXPERTS), ALU.is_equal))
            with nc.allow_low_precision(reason="zeros and ones"):
                v.tensor_reduce(chosen[:, :, :], exp_1h.rearrange("p (n j) e -> p n e j", j=TOP_K), AX.X, ALU.add).then_inc(chosen_ready, 1)
            for i in range(AHEAD):
                low_part(0, i)
            dve.wait_ge(rank_done, 1)
            then(v.tensor_copy(counts[:, :], bank[0][:, NQ * 32:NQ * 32 + 32]))
            then(v.tensor_tensor(picked.rearrange("p (n j) e -> p n j e", j=TOP_K),
                                 exp_1h.rearrange("p (n j) e -> p n j e", j=TOP_K),
                                 bank[0][:, 0:NQ * 32].rearrange("p (n e) -> p n e", n=NQ).unsqueeze(2).to_broadcast([P, NQ, TOP_K, N_EXPERTS]),
                                 ALU.mult))
            then(v.tensor_reduce(rank[:, :], picked, AX.X, ALU.add))
            over = cmp[:, 0:EXTRA * N_EXPERTS].rearrange("p (i e) -> p i e", i=EXTRA)
            then(v.tensor_tensor(over, across(counts[:, :], EXTRA), wide(thresholds[:, :], N_EXPERTS), ALU.is_gt))
            then(v.tensor_reduce(n_extra[:, :], over.rearrange("p i e -> p e i"), AX.X, ALU.add))
            v.memset(cum[:, :, 0:N_EXPERTS], 0.0)
            then(v.tensor_copy(cum[:, 0, N_EXPERTS:], n_extra[:, :]))
            cur, shift = 0, 1
            while shift < N_EXPERTS:
                then(v.tensor_tensor(cum[:, 1 - cur, N_EXPERTS:], cum[:, cur, N_EXPERTS:],
                                     cum[:, cur, N_EXPERTS - shift:2 * N_EXPERTS - shift], ALU.add))
                cur, shift = 1 - cur, 2 * shift
            upto = cum[:, cur, N_EXPERTS:]
            then(v.tensor_tensor(first_extra[:, :], upto, n_extra[:, :], ALU.subtract))
            then(v.tensor_tensor(picked, exp_1h, across(first_extra[:, :], NJ), ALU.mult))
            then(v.tensor_reduce(first_j[:, :], picked, AX.X, ALU.add))
            past = cmp[:, 0:NJ * EXTRA].rearrange("p (i t) -> p i t", i=NJ)
            then(v.tensor_tensor(past, wide(rank[:, :], EXTRA), across(thresholds[:, :], NJ), ALU.is_ge))
            then(v.tensor_reduce(extra_j[:, :], past, AX.X, ALU.add))
            then(v.scalar_tensor_tensor(pos[:, :], extra_j[:, :], -float(CAP), rank[:, :], ALU.mult, ALU.add))
            v.tensor_tensor(pos_1h[:, :, :], across(iota_f[:, 0:CAP], NJ), wide(pos[:, :], CAP), ALU.is_equal).then_inc(onehots_ready, 1)
            then(v.tensor_scalar(is_extra[:, :], extra_j[:, :], 1.0, None, ALU.min))
            then(v.tensor_tensor(tmp_j[:, :], first_j[:, :], extra_j[:, :], ALU.add))
            then(v.scalar_tensor_tensor(tmp_j[:, :], tmp_j[:, :], N_EXPERTS - 1.0, e_idx[:, :], ALU.add, ALU.subtract))
            then(v.tensor_tensor(tmp_j[:, :], tmp_j[:, :], is_extra[:, :], ALU.mult))
            then(v.tensor_tensor(blk[:, :], tmp_j[:, :], e_idx[:, :], ALU.add))
            then(v.tensor_tensor(blk_1h[:, :, :], across(iota_f[:, 0:COLS], NJ), wide(blk[:, :], COLS), ALU.is_equal))
            v.tensor_tensor(blk_1h[:, :, :].rearrange("p (n j) c -> p n (j c)", j=TOP_K),
                            blk_1h[:, :, :].bitcast(F32).rearrange("p (n j) c -> p n (j c)", j=TOP_K),
                            wide(tok_id[:, :], TOP_K * COLS), ALU.mult).then_inc(onehots_ready, 1)
            dve.wait_ge(table_done, 1)
            v.tensor_copy(tok_tab[:, :], bank[1][0:CAP, 0:COLS]).then_inc(table_ready, 1)
            v.tensor_scalar(first_slot[:, :], blk[:, :], float(CAP), None, ALU.mult)
            v.tensor_copy(pos_i[:, :], pos[:, :]).then_inc(slot_ready, 1)
            v.tensor_copy(n_ovf[:, :], cum[0:1, cur, 2 * N_EXPERTS - 1:]).then_inc(overflow_ready, 1)
            seen = cmp[0:1, :].rearrange("p (b e) -> p b e", e=N_EXPERTS)
            then(v.tensor_tensor(seen, wide(iota_f[0:1, 0:MAX_OVERFLOW], N_EXPERTS), across(cum[0:1, cur, N_EXPERTS:], MAX_OVERFLOW), ALU.is_ge))
            then(v.tensor_reduce(ovf_exp_f[:, :], seen, AX.X, ALU.add))
            v.tensor_scalar(ovf_exp[:, :], ovf_exp_f[:, :], N_EXPERTS - 1.0, None, ALU.min).then_inc(overflow_ready, 1)
            dve.wait_ge(gate_exp, 2 * NQ)
            then(v.reciprocal(gate_sum[:, :], gate_sum[:, :]))
            v.tensor_tensor(gates[:, :, :], gates[:, :, :], wide(gate_sum[:, :], TOP_K), ALU.mult).then_inc(gates_ready, 1)

            dve.wait_ge(bias_high, 1)
            for p in (32, 96):
                v.tensor_tensor(bias_gu[p:p + 32, :], bias_stage[p:p + 32, :], bias_gu[p:p + 32, :].bitcast(F32),
                                ALU.subtract).then_inc(bias_split, 1)

            def four(ap, half):
                return ap[:, 4 * half:4 * half + 4, :]

            def out_of(i):
                return bank[i][:, 0:4 * CAP].rearrange("p (k t) -> p k t", k=4)

            def xT_low_part(b, half):
                dve.wait_ge(xT_high_ready, 2 * b + half + 1)
                v.tensor_tensor(four(xT_low, half), out_of(6 + half), four(xT_high, half).bitcast(F32), ALU.subtract).then_inc(xT_low_ready, 1)

            def hT_low_part(b, half):
                dve.wait_ge(hT_high_ready, 2 * b + half + 1)
                v.tensor_tensor(four(hT_low, half), out_of(6 + half), four(hT_high, half).bitcast(F32), ALU.subtract).then_inc(hT_low_ready, 1)

            def limit_gate(b, half):
                dve.wait_ge(piece_used, PIECES * b + 4 * half + 2)
                v.tensor_scalar(g_lim[:, half], bank[2 * half][0:CAP, :], SWIGLU_LIMIT, None, ALU.min).then_inc(g_limited, 1)

            def hidden(b, half):
                dve.wait_ge(piece_used, PIECES * b + 4 * half + 4)
                v.tensor_scalar(u_lim[:, half], bank[2 * half + 1][0:CAP, :], SWIGLU_LIMIT, -SWIGLU_LIMIT,
                                ALU.min, ALU.max).then_inc(u_limited, 1)
                dve.wait_ge(u_limited, 2 * b + half + 1)
                dve.wait_ge(g_silu_ready, 2 * b + half + 1)
                v.scalar_tensor_tensor(h_tok[:, half], u_lim[:, half], 1.0, g_silu[:, half], ALU.add, ALU.mult).then_inc(h_tok_ready, 1)

            def dve_block(b, has_next=True):
                for i in range(PIECES):
                    if i in (2, 6):
                        limit_gate(b, i // 4)
                    if i in (4, 8):
                        hidden(b, i // 4 - 1)
                    if i == 9:
                        hT_low_part(b, 1)
                    if i >= 10:
                        xT_low_part(b + 1, i - 10)
                    if i + AHEAD < PIECES:
                        low_part(b, i + AHEAD)
                    elif has_next:
                        low_part(b + 1, i + AHEAD - PIECES)
                    if i == 6:
                        hT_low_part(b, 0)

            for half in range(2):
                xT_low_part(0, half)
            dve.wait_ge(bias_high, 2)
            v.tensor_tensor(bias_d[32:64, :], bias_stage[32:64, :], bias_d[32:64, :].bitcast(F32), ALU.subtract).then_inc(bias_split, 1)
            dve_block(0)
            with dve.Fori(1, N_EXPERTS - 1) as b:
                dve_block(b)
            dve_block(N_EXPERTS - 1, has_next=False)
            trips = dve.value_load(n_ovf[0:1, 0:1], min_val=0, max_val=MAX_OVERFLOW)
            with dve.If(trips > 0):
                with dve.Fori(N_EXPERTS, trips + N_EXPERTS) as b:
                    for i in range(AHEAD):
                        low_part(b, i)
                    dve_block(b, has_next=False)
            dve.wait_ge(gates_ready, 1)
            for n in range(NQ + 1):
                if n < NQ:
                    dve.wait_ge(y_back[n], 16 * TOP_K)
                    for j in range(TOP_K):
                        if j:
                            dve.wait_ge(combined, TOP_K * n + j)
                        v.scalar_tensor_tensor(h[:, n, :], y_tok[:, n * TOP_K + j, :], gates[:, n, j:j + 1], h[:, n, :],
                                               ALU.mult, ALU.add).then_inc(combined, 1)
                if n:
                    m = n - 1
                    dve.wait_ge(rstd_ready, 2 * NQ + m + 1)
                    v.scalar_tensor_tensor(y_tok[:, m * TOP_K, :], h[:, m, :], rstd[:, 2 * NQ + m:2 * NQ + m + 1], gfin_row,
                                           ALU.mult, ALU.mult).then_inc(final_ready, 1)

        @block.tensor
        def _(pe):
            t = nc.tensor
            pe.wait_ge(consts_ready, 9)
            for n in range(NQ):
                pe.wait_ge(xn_ready, n + 1)
                for half in range(2):
                    i = 2 * n + half
                    if i >= 4:
                        pe.wait_ge(xnT_act if half else xnT_dve, n - 1)
                    for c in range(4):
                        k = 4 * half + c
                        last = t.transpose(bank[4 + i % 4][:, c * P:(c + 1) * P], xn_tile[:, n % 2, k * P:(k + 1) * P], ident[:, :])
                    last.then_inc(xn_transposed, 1)
                if n == 0:
                    pe.wait_ge(stage_loaded, 16 * 5)
                    t.transpose(bank[0][:, 0:32], stage[0:32, 0, :], ident[0:32, 0:32])
                    rows = CONV_K * CC
                    last = t.transpose(bank[0][:, 32:32 + rows], stage[0:rows, 1, :], ident[0:rows, 0:rows])
                    last.then_inc(stage_transposed, 1)
            pe.wait_ge(xnT_dve, NQ)
            pe.wait_ge(xnT_act, NQ)
            pe.wait_ge(cols_ready, 1)

            groups = [(1 + i % 2, i // 2) for i in range(8)] + [(3, c) for c in range(4)] + [(4, c) for c in range(4)]
            for g, (s, c) in enumerate(groups):
                pe.wait_ge(win_loaded[s - 1], 16)
                if 4 <= g < 12 and g % 2:
                    pe.wait_ge(glu_ready, 4 * ((g - 4) // 2 + 1))
                elif 4 <= g < 12:
                    pe.wait_ge(act_evac, (g - 4) // 2 + 1)
                elif g >= 12:
                    pe.wait_ge(act_evac, 4 + g - 12 + 1)
                for k in range(KD):
                    last = t.matmul(bank[g % 4][:, :], unit(s)[:, k, c * P:(c + 1) * P], xnT[:, k, :],
                                    start=(k == 0), stop=(k == KD - 1))
                last.then_inc(proj_done, 1)
            pe.wait_ge(win_loaded[4], 16)
            for n in range(NQ):
                pe.wait_ge(act_evac, 8 + n + 1)
                for k in range(KD):
                    last = t.matmul(bank[n][:, :], xnT[:, k, n * P:(n + 1) * P], unit(5)[:, k, :],
                                    start=(k == 0), stop=(k == KD - 1))
                last.then_inc(proj_done, 1)
            pe.wait_ge(conv_tap, CONV_K * CC)
            for c in range(CC):
                last = t.matmul(bank[4][:, :], mean_w[:, :], mixedT[:, c, :], start=(c == 0), stop=(c == CC - 1))
            last.then_inc(mean_done, 1)

            def qk(i):
                n, hd = steps[i]
                m0, m1 = keys_of(n)
                p0 = (hd % 2) * HEAD_DIM
                if i >= 3:
                    pe.wait_ge(s_ready, i - 2)
                t.matmul(bank[i % 3][:, 0:(m1 - m0) * P], qT[p0:p0 + HEAD_DIM, hd // 2, n * P:(n + 1) * P],
                         kT[p0:p0 + HEAD_DIM, hd // 2, m0 * P:m1 * P], start=True, stop=True).then_inc(qk_done, 1)

            def transpose_p(i):
                m0, m1 = keys_of(steps[i][0])
                pe.wait_ge(exp_ready, i + 1)
                if i >= 2:
                    pe.wait_ge(pT_act if i % 2 else pT_dve, i // 2)
                for m in range(m1 - m0):
                    last = t.transpose(bank[6 if i % 2 else 3][:, m * P:(m + 1) * P], P_sb[:, i % 3, m * P:(m + 1) * P], ident[:, :])
                last.then_inc(p_transposed, 1)

            def pv(i):
                n, hd = steps[i]
                m0, m1 = keys_of(n)
                pe.wait_ge(pT_act if i % 2 else pT_dve, i // 2 + 1)
                if hd == 0 and n >= 2:
                    pe.wait_ge(o_ready, n - 1)
                for m in range(m0, m1):
                    last = t.matmul(bank[7 if n % 2 == 0 else 4][:, hd * HEAD_DIM:(hd + 1) * HEAD_DIM],
                                    PT_sb[:, i % 2, (m - m0) * P:(m - m0 + 1) * P],
                                    v_sb[:, m, hd * HEAD_DIM:(hd + 1) * HEAD_DIM], start=(m == m0), stop=(m == m1 - 1))
                last.then_inc(pv_done, 1)

            def transpose_o(n):
                pe.wait_ge(o_ready, n + 1)
                if n:
                    pe.wait_ge(oT_ready, n)
                for c in range(4):
                    last = t.transpose(bank[5][:, c * P:(c + 1) * P], O_sb[:, c * P:(c + 1) * P], ident[:, :])
                last.then_inc(o_transposed, 1)

            pe.wait_ge(act_evac, 16)
            for i in range(NS + 4):
                if i < NS:
                    qk(i)
                if i == 1:
                    for c in range(CC):
                        pe.wait_ge(squared, c + 1)
                        t.matmul(bank[5][:, :], mean_w[:, :], sq[:, c % 2, :], start=(c == 0),
                                 stop=(c == CC - 1)).then_inc(var_part, 1)
                if 0 <= i - 2 < NS:
                    transpose_p(i - 2)
                if 0 <= i - 3 < NS:
                    pv(i - 3)
                if i >= 11 and (i - 11) % HEADS == 0:
                    transpose_o((i - 11) // HEADS)

            def project_out(n):
                for half in range(2):
                    i = 2 * n + half
                    if i >= 4:
                        pe.wait_ge(h_ready, i - 3)
                    for k in range(KD):
                        if k < 4:
                            lhsT = convT_out[k][:, n * P:(n + 1) * P]
                        else:
                            lhsT = mixedT[:, k, n * P:(n + 1) * P]
                        last = t.matmul(bank[i % 4][:, :], lhsT, unit((6, 1)[half])[:, k, :], start=(k == 0), stop=(k == KD - 1))
                    last.then_inc(wout_done, 1)

            def route(n):
                pe.wait_ge(xn2_ready, n + 1)
                for half in range(2):
                    i = 2 * n + half
                    if i >= 3:
                        j = i - 3
                        pe.wait_ge(xn2T_act if j % 2 else xn2T_dve, j // 2 + 1)
                    for c in range(4):
                        k = 4 * half + c
                        last = t.transpose(bank[4 + i % 3][:, c * P:(c + 1) * P], xn2[:, n, k * P:(k + 1) * P], ident[:, :])
                    last.then_inc(xn2_transposed, 1)
                if n:
                    pe.wait_ge(logits_ready, n)
                pe.wait_ge(xn2T_act, n + 1)
                pe.wait_ge(xn2T_dve, n + 1)
                for k in range(KD):
                    last = t.matmul(bank[7][:, n * 32:(n + 1) * 32], xn2T[n // 2][:, n % 2, k, :], wr[:, k, :],
                                    start=(k == 0), stop=(k == KD - 1))
                last.then_inc(logits_done, 1)

            pe.wait_ge(silu_ready, CC)
            pe.wait_ge(oT_ready, NQ)
            pe.wait_ge(wout_loaded, 32)
            pe.wait_ge(router_loaded, 32)
            project_out(0)
            project_out(1)
            route(0)
            project_out(2)
            route(1)
            project_out(3)
            route(2)
            route(3)
            pe.wait_ge(chosen_ready, 1)
            for n in range(NQ):
                for m in range(n + 1):
                    last = t.matmul(bank[0][:, n * 32:(n + 1) * 32], (before_b if m == n else ones_b)[:, :], chosen[:, m, :],
                                    start=(m == 0), stop=(m == n))
            for m in range(NQ):
                last = t.matmul(bank[0][:, NQ * 32:NQ * 32 + 32], ones_b[:, :], chosen[:, m, :], start=(m == 0), stop=(m == NQ - 1))
            last.then_inc(rank_done, 1)
            pe.wait_ge(onehots_ready, 2)
            for i in range(NJ):
                last = t.matmul(bank[1][0:CAP, 0:COLS], pos_1h[:, i, :], blk_1h[:, i, :], start=(i == 0), stop=(i == NJ - 1))
            last.then_inc(table_done, 1)

            def transpose_x(b):
                pe.wait_ge(xg_loaded, 16 * (b + 1))
                for k in range(KD):
                    last = t.transpose(bank[6 + k // 4][:, (k % 4) * CAP:(k % 4 + 1) * CAP], xg[0:CAP, k * P:(k + 1) * P],
                                       ident[0:CAP, 0:CAP])
                last.then_inc(xg_transposed, 1)

            def transpose_h(b, half):
                pe.wait_ge(h_tok_ready, 2 * b + half + 1)
                for c in range(4):
                    last = t.transpose(bank[6 + half][:, c * CAP:(c + 1) * CAP], h_tok[:, half, c * P:(c + 1) * P],
                                       ident[0:CAP, 0:CAP])
                last.then_inc(h_transposed, 1)

            def three(to, high, low, i, at, k, stop):
                hi, lo = w_high[:, i % HIGH_RING, at:at + HALF], w_low[i][:, at:at + HALF]
                t.matmul(to, high[:, k, :], hi, start=False, stop=False)
                t.matmul(to, high[:, k, :], lo, start=False, stop=False)
                return t.matmul(to, low[:, k, :], hi, start=False, stop=stop)

            def pe_block(b):
                pe.wait_ge(xT_low_ready, 2 * (b + 1))
                pe.wait_ge(selector_ready, b + 1)
                for i in range(PIECES):
                    if i < 8:
                        to = bank[i // 2][0:CAP, :]
                        if i % 2 == 0:
                            rows, cols = 64 * (i // 2 % 2), HALF * (i // 4)
                            t.matmul(to, selector[rows:rows + 64, :], bias_gu[rows:rows + 64, cols:cols + HALF],
                                     start=True, stop=False)
                        wait_low(pe, b, i)
                        for k in range(4):
                            last = three(to, xT_high, xT_low, i, k * HALF, 4 * (i % 2) + k, i % 2 == 1 and k == 3)
                    else:
                        if i == 8:
                            for half in range(2):
                                t.matmul(bank[4 + half][0:CAP, :], selector[0:64, :], bias_d[0:64, half * HALF:(half + 1) * HALF],
                                         start=True, stop=False)
                        wait_low(pe, b, i)
                        if i % 2 == 0:
                            pe.wait_ge(hT_low_ready, 2 * b + (i - 8) // 2 + 1)
                        for k in range(2):
                            for half in range(2):
                                last = three(bank[4 + half][0:CAP, :], hT_high, hT_low, i, k * D_MODEL + half * HALF,
                                             2 * (i - 8) + k, i == PIECES - 1 and k == 1)
                    last.then_inc(piece_used, 1)
                    if i == 5:
                        transpose_h(b, 0)
                    if i == 8:
                        transpose_h(b, 1)
                    if i == 9:
                        pe.wait_ge(hT_low_ready, 2 * b + 2)
                        transpose_x(b + 1)

            transpose_x(0)
            pe.wait_ge(bias_split, 3)
            pe_block(0)
            with pe.Fori(1, N_EXPERTS) as b:
                pe_block(b)
            pe.wait_ge(overflow_ready, 2)
            trips = pe.value_load(n_ovf[0:1, 0:1], min_val=0, max_val=MAX_OVERFLOW)
            with pe.If(trips > 0):
                with pe.Fori(N_EXPERTS, trips + N_EXPERTS) as b:
                    pe_block(b)


_INS = ['x', 'g_mix', 'w_in', 'b_in', 'conv_w', 'conv_b', 'ln_g', 'ln_b', 'rpb', 'w_out', 'b_out', 'g_ffn',
        'w_router', 'b_router', 'w_gate', 'b_gate', 'w_up', 'b_up', 'w_down', 'b_down', 'g_final']


def kernel(**inputs):
    import numpy as _np
    import concourse.bacc as _bacc
    from concourse import mybir as _mybir
    from concourse.bass_utils import run_bass_kernel_spmd as _run

    nc = _bacc.Bacc("TRN2", target_bir_lowering=False, num_devices=1)
    arrays, args = {}, []
    for name in _INS:
        a = _np.ascontiguousarray(inputs[name])
        arrays[f"in_{name}"] = a
        args.append(nc.dram_tensor(f"in_{name}", a.shape, _mybir.dt.from_np(a.dtype), kind="ExternalInput").ap())
    args.append(nc.dram_tensor("out_0", (1, SEQ, D_MODEL), F32, kind="ExternalOutput").ap())
    encoder_kernel(nc, *args)
    r = _run(nc, [arrays], core_ids=[0])
    return r.results[0]["out_0"]
```

```python
import numpy as np
import concourse.bass as bass
from concourse import mybir
from contextlib import ExitStack

F32 = mybir.dt.float32
F32R = mybir.dt.float32r
BF16 = mybir.dt.bfloat16
I32 = mybir.dt.int32
U32 = mybir.dt.uint32
ALU = mybir.AluOpType
ACT = mybir.ActivationFunctionType
AX = mybir.AxisListType

P = 128
SEQ, D_MODEL = 512, 1024
GRID_W, N_ROWS = 64, 8
QB = 16
NQ = GRID_W // QB
D_CONV, CONV_K = 512, 31
PAD = CONV_K // 2
HEADS, HEAD_DIM = 8, 64
WIN_H, WIN_W = 8, 16
N_EXPERTS, TOP_K, D_FF = 32, 4, 1024
EPS = 1e-5
SWIGLU_LIMIT, SWIGLU_ALPHA = 7.0, 1.702
NEG = 1e30

KD = D_MODEL // P
CC = D_CONV // P
HALF = D_MODEL // 2
RPB_H, RPB_W = 2 * WIN_H - 1, 2 * WIN_W - 1
RPB_PITCH = 64
RUN = WIN_H * RPB_PITCH

CAP = 112
EXTRA = (SEQ - 1) // CAP
MAX_OVERFLOW = (SEQ * TOP_K - 1) // CAP
N_BLOCKS = N_EXPERTS + MAX_OVERFLOW
COLS = N_BLOCKS + 2 - N_BLOCKS % 2
NJ = NQ * TOP_K
UNITS = 7
PIECES, PIECE = 12, 2048
HIGH_RING = 4
AHEAD = HIGH_RING - 1
POOL_PIECES = (11,)
DVE_PIECES = [i for i in range(PIECES) if i not in POOL_PIECES]


def encoder_kernel(nc, x, g_mix, w_in, b_in, conv_w, conv_b, ln_g, ln_b, rpb, w_out, b_out,
                   g_ffn, w_router, b_router, w_gate, b_gate, w_up, b_up, w_down, b_down,
                   g_final, out):
    ctx = ExitStack()
    with ctx:
        def sem(name):
            return ctx.enter_context(nc.semaphore(name))

        rpb_pad = nc.dram_tensor("rpb_pad", [QB, HEADS * RPB_H + 1, RPB_PITCH], F32, kind="Internal").ap()
        xn2_rows = nc.dram_tensor("xn2_rows", [SEQ, D_MODEL], F32, kind="Internal").ap()
        y_rows = nc.dram_tensor("y_rows", [N_BLOCKS * CAP, D_MODEL], F32, kind="Internal").ap()

        free = [-(-nc.sbuf_base // 64) * 64]

        def area(name, shape, dt=F32):
            at = free[0]
            size = int(np.prod(shape[1:])) * (2 if dt == BF16 else 4)
            free[0] = at + -(-size // 32) * 32
            return nc.alloc_sbuf_tensor_at(name, shape, dt, offset=at), at

        def sb(name, shape, dt=F32):
            return area(name, shape, dt)[0]

        def over(name, at, word, shape, dt=F32R):
            return nc.alloc_sbuf_tensor_at(name, shape, dt, offset=at + 4 * word)

        h = sb("h", [P, NQ, D_MODEL])
        ring, ring_at = area("ring", [P, UNITS, KD * HALF])
        area_a, a_at = area("area_a", [P, 4096])
        area_q, q_at = area("area_q", [P, 2048])
        area_k, k_at = area("area_k", [P, 2048])
        area_v, v_at = area("area_v", [P, 2048])
        area_u, u_at = area("area_u", [P, CC * (SEQ + 2 * PAD)])
        area_m, m_at = area("area_m", [P, 4096])
        area_t, t_at = area("area_t", [P, HEADS * 384])
        w_high = over("w_high", ring_at, 0, [P, HIGH_RING, PIECE])
        piece_at = [(ring_at, i * PIECE) for i in (10, 11, 9, 8, 4, 5, 6, 7, 12, 13)] + [(u_at, 0), (a_at, 2048)]
        w_raw = [over(f"w_raw{i}", *piece_at[i], [P, PIECE], F32) for i in range(PIECES)]
        w_low = [over(f"w_low{i}", *piece_at[i], [P, PIECE]) for i in range(PIECES)]
        bias_gu = over("bias_gu", a_at, 0, [P, D_MODEL])
        bias_d = over("bias_d", a_at, 1024, [P, D_MODEL])
        xT_high = over("xT_high", k_at, 0, [P, KD, CAP])
        xT_low = over("xT_low", k_at, 1024, [P, KD, CAP])
        hT_high = over("hT_high", m_at, 2048, [P, KD, CAP])
        hT_low = over("hT_low", m_at, 3072, [P, KD, CAP])
        pos_1h = over("pos_1h", t_at, 0, [P, NJ, CAP])
        blk_1h = over("blk_1h", t_at, NJ * CAP, [P, NJ, COLS])

        iota_i = over("iota_i", m_at, 1024, [P, 384], I32)
        iota_u = area_m[:, 1408:1792]
        before = area_m[:, 1792:1920]

        def unit(s):
            return ring[:, s, :].rearrange("p (k f) -> p k f", k=KD)

        xnT_high = over("xnT_high", a_at, 0, [P, KD, SEQ])
        xnT_low = over("xnT_low", ring_at, 6 * 4096, [P, KD, SEQ])
        glu_high = over("glu_high", ring_at, 0, [P, 4, KD, P])
        q0_high = over("q0_high", v_at, 1024, [P, KD, P])
        q_high = over("q_high", ring_at, 1 * 4096, [P, 4, KD, P])
        k_high = over("k_high", ring_at, 2 * 4096, [P, 4, KD, P])
        v_high = over("v_high", ring_at, 3 * 4096, [P, KD, HALF])
        win_low = [over(f"win_low{i}", ring_at, i * 4096, [P, KD, HALF]) for i in range(1, 6)]
        wout_low = [over(f"wout_low{i}", ring_at, p * 4096, [P, KD, HALF]) for i, p in enumerate((6, 1))]
        wout_high = [over(f"wout_high{i}", ring_at, p * 4096, [P, KD, HALF]) for i, p in enumerate((2, 3))]
        conv_high = over("conv_high", m_at, 0, [P, CC, SEQ])
        conv_low = [over(f"conv_low{i}", *at, [P, SEQ]) for i, at in enumerate(((u_at, 0), (u_at, 512), (u_at, 1536), (a_at, 3584)))]
        attn_high = over("attn_high", ring_at, 4 * 4096, [P, 4, SEQ])
        attn_low = over("attn_low", m_at, 2048, [P, 4, SEQ])
        groups = [(1 + i % 2, i // 2) for i in range(8)] + [(3, c) for c in range(4)] + [(4, c) for c in range(4)]

        def split_parts(g):
            if g >= 16:
                ks = slice(2 * (g - 16), 2 * (g - 16) + 2)
                return unit(5)[:, ks, :], v_high[:, ks, :], win_low[4][:, ks, :]
            place, c = groups[g]
            cols = slice(c * P, (c + 1) * P)
            high = glu_high[:, g % 4] if g < 8 else q0_high[:, :, :] if g == 8 else (q_high, k_high)[place - 3][:, c]
            return unit(place)[:, :, cols], high, win_low[place - 1][:, :, cols]

        qT = area_q[:, :].rearrange("p (k t) -> p k t", k=4)
        kT = area_k[:, :].rearrange("p (k t) -> p k t", k=4)
        v_sb = area_v[:, :].rearrange("p (n f) -> p n f", n=NQ)
        u_pad = area_u[:, :].rearrange("p (c t) -> p c t", c=CC)
        mixedT = area_m[:, :].rearrange("p (k t) -> p k t", k=KD)
        xn_tile = area_q[:, :].rearrange("p (b d) -> p b d", b=2)
        gmix_row = area_k[:, 0:1024]
        bout_row = area_k[:, 1024:2048]
        zeros = area_t[:, 2112:2112 + HALF]
        sg = area_v[:, 0:1024].rearrange("p (b t) -> p b t", b=2)
        stage = area_m[:, 0:1024].rearrange("p (s q) -> p s q", s=8)
        raw_bias = area_m[:, 2048:3072].rearrange("p (b t) -> p b t", b=2)
        mask = area_m[:, 3072:3072 + 896]
        sq = area_u[:, 0:1024].rearrange("p (b t) -> p b t", b=2)
        ln_rs = area_u[:, 1024:1536]
        convT_out = [area_u[:, 0:512], area_u[:, 512:1024], area_u[:, 1536:2048], area_a[:, 3584:4096]]
        T_mid = area_t[:, :].rearrange("p (h t) -> p h t", h=HEADS)
        T_edge = ring[:, 0, :].rearrange("p (h e t) -> p h e t", h=HEADS, e=2)
        S_sb = area_a[:, 0:1152].rearrange("p (b t) -> p b t", b=3)
        P_sb = area_a[:, 1152:2304].rearrange("p (b t) -> p b t", b=3)
        PT_sb = area_a[:, 2304:3072].rearrange("p (b t) -> p b t", b=2)
        O_sb = area_a[:, 3072:3584]
        wr = area_t[:, 2048:2304].rearrange("p (k e) -> p k e", k=KD)
        br_row = area_t[:, 2304:2336]
        xn2 = area_a[:, :].rearrange("p (n d) -> p n d", n=NQ)
        xn2T = [a[:, :].rearrange("p (b k t) -> p b k t", b=2, k=KD) for a in (area_q, area_k)]
        gffn_row = area_v[:, 0:1024]
        gfin_row = area_v[:, 1024:2048]
        xg = area_m[:, 0:1024]
        y_sb = area_m[:, 1024:2048]
        bias_stage = area_v[:, 0:1024]
        down_stage = area_q[:, 1024:2048]
        g_lim = area_t[0:CAP, 0:1024].rearrange("p (b f) -> p b f", b=2)
        g_silu = area_t[0:CAP, 1024:2048].rearrange("p (b f) -> p b f", b=2)
        u_lim = area_q[0:CAP, 0:1024].rearrange("p (b f) -> p b f", b=2)
        h_tok = area_q[0:CAP, 1024:2048].rearrange("p (b f) -> p b f", b=2)
        exp_1h = area_u[:, 0:512].rearrange("p (i e) -> p i e", i=NJ)
        picked = area_u[:, 512:1024].rearrange("p (i e) -> p i e", i=NJ)
        cmp = area_u[:, 1024:1024 + MAX_OVERFLOW * N_EXPERTS]
        junk_norm = [area_t[:, 0:1024], area_t[:, 1024:2048]]
        junk = area_t[:, 0:1024]
        y_tok = ring[:, :, :].rearrange("p s f -> p (s f)").rearrange("p (i d) -> p i d", d=D_MODEL)

        rpb_tile = area_t[0:HEADS * RPB_H + 1, 2048:2048 + RPB_PITCH]
        neg_max, row_max, row_sum = (area_u[:, 2048 + 32 * i:2080 + 32 * i] for i in range(3))
        late_at = NJ * (CAP + COLS)
        top_val = area_t[:, late_at:late_at + 32].rearrange("p (n j) -> p n j", n=NQ)
        top_idx = over("top_idx", t_at, late_at + 32, [P, NQ, 8], U32)
        chosen = over("chosen", t_at, late_at + 64, [P, NQ, N_EXPERTS], BF16)
        tok_tab = over("tok_tab", t_at, late_at + 128, [CAP, COLS], I32)
        gates = area_t[:, late_at + 128 + COLS:late_at + 144 + COLS].rearrange("p (n j) -> p n j", n=NQ)
        gate_neg, gate_sum = (area_t[:, late_at + 144 + COLS + NQ * i:late_at + 148 + COLS + NQ * i] for i in range(2))
        first_slot, pos_i, slot = (over(name, t_at, 2048 + NJ * i, [P, NJ], I32)
                                   for i, name in enumerate(("first_slot", "pos_i", "slot")))
        ovf_exp = over("ovf_exp", t_at, 2048 + 3 * NJ, [1, MAX_OVERFLOW], I32)
        e_idx, rank, first_j, extra_j, is_extra, blk, pos, tmp_j = (area_q[:, NJ * i:NJ * (i + 1)] for i in range(8))
        counts, n_extra, first_extra, ovf_exp_f = (area_q[:, 128 + 32 * i:160 + 32 * i] for i in range(4))
        ovf_exp_f = ovf_exp_f[0:1, 0:MAX_OVERFLOW]
        cum = area_q[:, 256:256 + 4 * N_EXPERTS].rearrange("p (b e) -> p b e", b=2)

        ident = sb("ident", [P, P])
        mean_w, mean_at = area("mean_w", [P, P])
        selector = over("selector", mean_at, 0, [P, CAP])
        is_expert = sb("is_expert", [P, N_EXPERTS])
        ones_b = sb("ones_b", [P, P], BF16)
        before_b = sb("before_b", [P, P], BF16)
        colT = sb("colT", [P, 32])
        convT = sb("convT", [P, P])
        logits = convT[:, :].rearrange("p (n e) -> p n e", n=NQ)
        bq = sb("bq", [P, 4])
        p_int = sb("p_int", [P, 3], I32)
        c_flt = sb("c_flt", [P, 2])
        win_lo = sb("win_lo", [P, 3])
        win_hi = sb("win_hi", [P, 3])
        iota_f = sb("iota_f", [P, 128])
        thresholds = sb("thresholds", [P, EXTRA])
        tok_id = sb("tok_id", [P, NQ])
        minus_half = sb("minus_half", [P, 1])
        eps_col = sb("eps_col", [P, 1])
        ss = sb("ss", [P, 3 * NQ])
        ms = sb("ms", [P, 3 * NQ])
        rstd = sb("rstd", [P, 3 * NQ])
        row_inv = sb("row_inv", [P, 32])
        tok_now = sb("tok_now", [CAP, 1], I32)
        n_ovf = sb("n_ovf", [1, 1], I32)

        bank = [ctx.enter_context(nc.psum_tensor(f"bank{i}", [P, 512], F32)) for i in range(8)]

        x_loaded = [sem(f"x_loaded{n}") for n in range(NQ)]
        win_loaded = [sem(f"win_loaded{i}") for i in range(5)]
        wout_loaded = [sem(f"wout_loaded{i}") for i in range(2)]
        raw_piece = [sem(f"raw_piece{i}") for i in range(PIECES)]
        rows_loaded = sem("rows_loaded")
        bout_loaded = sem("bout_loaded")
        stage_loaded = sem("stage_loaded")
        router_loaded = sem("router_loaded")
        norm_rows_loaded = sem("norm_rows_loaded")
        rpb_tile_loaded = sem("rpb_tile_loaded")
        rpb_stored = sem("rpb_stored")
        raw_loaded = sem("raw_loaded")
        consts_ready = sem("consts_ready")
        iotas_ready = sem("iotas_ready")
        upad_zeroed = sem("upad_zeroed")
        rpb_zeroed = sem("rpb_zeroed")
        mask_step = sem("mask_step")
        ss_ready = sem("ss_ready")
        ms_ready = sem("ms_ready")
        rstd_ready = sem("rstd_ready")
        xn_ready = sem("xn_ready")
        xn_transposed = sem("xn_transposed")
        xnT_dve = sem("xnT_dve")
        xnT_act = sem("xnT_act")
        xnT_low_ready = sem("xnT_low_ready")
        win_high_ready = sem("win_high_ready")
        win_low_dve = sem("win_low_dve")
        win_low_pool = sem("win_low_pool")
        stage_transposed = sem("stage_transposed")
        cols_ready = sem("cols_ready")
        bq_ready = sem("bq_ready")
        xb_ready = sem("xb_ready")
        proj_done = sem("proj_done")
        act_evac = sem("act_evac")
        glu_ready = sem("glu_ready")
        conv_tap = sem("conv_tap")
        tables_ready = sem("tables_ready")
        mean_done = sem("mean_done")
        centred = sem("centred")
        squared = sem("squared")
        var_part = sem("var_part")
        std_ready = sem("std_ready")
        ln_rs_ready = sem("ln_rs_ready")
        ln_scaled = sem("ln_scaled")
        ln_affine = sem("ln_affine")
        silu_sig_ready = sem("silu_sig_ready")
        silu_ready = sem("silu_ready")
        qk_done = sem("qk_done")
        s_ready = sem("s_ready")
        neg_max_ready = sem("neg_max_ready")
        exp_ready = sem("exp_ready")
        p_transposed = sem("p_transposed")
        pT_dve = sem("pT_dve")
        pT_act = sem("pT_act")
        pv_done = sem("pv_done")
        inv_ready = sem("inv_ready")
        o_ready = sem("o_ready")
        o_transposed = sem("o_transposed")
        oT_ready = sem("oT_ready")
        wout_done = sem("wout_done")
        wout_high_ready = sem("wout_high_ready")
        wout_low_dve = sem("wout_low_dve")
        wout_low_pool = sem("wout_low_pool")
        conv_high_ready = sem("conv_high_ready")
        conv_low_ready = sem("conv_low_ready")
        attn_high_ready = sem("attn_high_ready")
        attn_low_ready = sem("attn_low_ready")
        h_ready = sem("h_ready")
        ss2_ready = sem("ss2_ready")
        xn2_ready = sem("xn2_ready")
        xn2_stored = sem("xn2_stored")
        xn2_transposed = sem("xn2_transposed")
        xn2T_act = sem("xn2T_act")
        xn2T_dve = sem("xn2T_dve")
        logits_done = sem("logits_done")
        logits_ready = sem("logits_ready")
        top_ready = sem("top_ready")
        gate_exp = sem("gate_exp")
        gates_ready = sem("gates_ready")
        route_step = sem("route_step")
        chosen_ready = sem("chosen_ready")
        rank_done = sem("rank_done")
        onehots_ready = sem("onehots_ready")
        table_done = sem("table_done")
        table_ready = sem("table_ready")
        slot_ready = sem("slot_ready")
        zeros_ready = sem("zeros_ready")
        overflow_ready = sem("overflow_ready")
        xg_loaded = sem("xg_loaded")
        xg_transposed = sem("xg_transposed")
        high_ready = sem("high_ready")
        low_ready = sem("low_ready")
        low_last = sem("low_last")
        piece_used = sem("piece_used")
        selector_ready = sem("selector_ready")
        bias_rows_loaded = sem("bias_rows_loaded")
        bias_high = sem("bias_high")
        bias_split = sem("bias_split")
        xT_high_ready = sem("xT_high_ready")
        xT_low_ready = sem("xT_low_ready")
        g_limited = sem("g_limited")
        g_sig_ready = sem("g_sig_ready")
        g_silu_ready = sem("g_silu_ready")
        u_limited = sem("u_limited")
        h_tok_ready = sem("h_tok_ready")
        h_transposed = sem("h_transposed")
        hT_high_ready = sem("hT_high_ready")
        hT_low_ready = sem("hT_low_ready")
        y_ready = sem("y_ready")
        y_stored = sem("y_stored")
        y_back = [sem(f"y_back{n}") for n in range(NQ)]
        combined = sem("combined")
        ss3_ready = sem("ss3_ready")
        final_ready = sem("final_ready")
        out_stored = sem("out_stored")

        def row_bcast(ap, n, offset=0):
            return bass.AP(ap.tensor, ap.offset + offset, [[0, P], [1, n]])

        def by_block(ap):
            return ap[0].rearrange("(r n c) d -> n r c d", r=N_ROWS, c=QB)

        x_blocks, out_blocks = by_block(x), by_block(out)
        win_v = w_in[0].rearrange("(k p) f -> p k f", p=P)
        wout_v = w_out[0].rearrange("(k p) f -> p k f", p=P)
        wg_v, wu_v, wd_v = (w[0].rearrange("e (k p) f -> e p k f", p=P) for w in (w_gate, w_up, w_down))

        def piece_src(i, e):
            if i < 8:
                mat, half, ks = (wg_v, wu_v)[i // 2 % 2], i // 4, i % 2
                return mat[e, :, 4 * ks:4 * ks + 4, half * HALF:(half + 1) * HALF]
            return wd_v[e, :, 2 * (i - 8):2 * (i - 8) + 2, :]

        def wait_low(eng, b, i):
            if i in POOL_PIECES:
                eng.wait_ge(low_last, len(POOL_PIECES) * b + POOL_PIECES.index(i) + 1)
            else:
                eng.wait_ge(low_ready, len(DVE_PIECES) * b + DVE_PIECES.index(i) + 1)

        def keys_of(n):
            return max(n - 1, 0), min(n + 2, NQ)

        def table_of(n, hd):
            if n == 0:
                return T_edge[:, hd, 0, :]
            if n == NQ - 1:
                return T_edge[:, hd, 1, :]
            return T_mid[:, hd, :]

        OUT_BANKS, T_BANKS = (2, 4), (0, 1, 3)
        PROJECT_AT = {10: (0, 0), 11: (1, 0), 14: (0, 1), 16: (1, 1)}
        RESIDUAL_AT = (15, 17)
        steps = [(n, hd) for n in range(NQ) for hd in range(HEADS)]
        NS = len(steps)

        block = ctx.enter_context(nc.Block())

        @block.sync
        def _(sp):
            for n in range(NQ):
                sp.dma_start(h[:, n, :], x_blocks[n]).then_inc(x_loaded[n], 16)
            sp.dma_start(stage[0:20, 0, :], b_in[0].rearrange("(c p) -> c p", p=P)).then_inc(stage_loaded, 16)
            sp.dma_start(stage[0:CONV_K * CC, 1, :],
                         conv_w[0].rearrange("k (c p) -> (k c) p", p=P)).then_inc(stage_loaded, 16)
            for i, col in enumerate((1, 0, 2, 3, 4)):
                sp.dma_start(unit(1 + i), win_v[:, :, col * HALF:(col + 1) * HALF]).then_inc(win_loaded[i], 16)
            spare = y_rows[N_EXPERTS * CAP:, :].rearrange("(p i) (j f) -> p (i j) f", p=CAP, f=HALF)
            sp.wait_ge(zeros_ready, 1)
            sp.dma_start(spare, zeros[0:CAP].unsqueeze(1).to_broadcast([CAP, spare.shape[1], spare.shape[2]])).then_inc(y_stored, 16)
            sp.wait_ge(rpb_tile_loaded, 16)
            for c in range(QB):
                sp.dma_start(rpb_pad[c], rpb_tile[:, :]).then_inc(rpb_stored, 16)
            sp.wait_ge(rpb_stored, 16 * QB)
            copy_size = (HEADS * RPB_H + 1) * RPB_PITCH
            for pair in range(HEADS // 2):
                if pair:
                    sp.wait_ge(tables_ready, 6 * pair)
                for r in range(N_ROWS):
                    start = (2 * pair * RPB_H + WIN_H - 1 - r) * RPB_PITCH + QB - 1
                    src = bass.AP(rpb_pad.tensor, rpb_pad.offset + start,
                                  [[copy_size - 1, QB], [RPB_H * RPB_PITCH, 2], [1, RUN]])
                    sp.dma_start(raw_bias[r * QB:(r + 1) * QB, :, :], src).then_inc(raw_loaded, 16)
            def load(i, e):
                src = piece_src(i, e)
                sp.dma_start(w_raw[i][:, :].rearrange("p (k f) -> p k f", f=src.shape[2]), src).then_inc(raw_piece[i], 16)

            sp.wait_ge(proj_done, 12)
            sp.dma_start(unit(1), wout_v[:, :, HALF:]).then_inc(wout_loaded[1], 16)
            sp.wait_ge(proj_done, 20)
            sp.dma_start(unit(6), wout_v[:, :, 0:HALF]).then_inc(wout_loaded[0], 16)
            for i in range(3):
                load(i, 0)
            sp.wait_ge(wout_done, 2 * NQ)
            for i in (3, 4):
                load(i, 0)
            sp.wait_ge(xn2_stored, 16 * NQ)
            load(5, 0)
            load(6, 0)
            sp.wait_ge(bias_rows_loaded, 96)
            for i in range(7, 10):
                load(i, 0)
            sp.wait_ge(overflow_ready, 2)
            sp.wait_ge(xg_loaded, 16)
            load(10, 0)
            sp.wait_ge(xn2_transposed, 2 * NQ)
            load(11, 0)

            def weights(b, e):
                for i in range(PIECES):
                    sp.wait_ge(piece_used, PIECES * (b - 1) + i + 1)
                    load(i, e)

            with sp.Fori(1, N_EXPERTS) as b:
                weights(b, b)
            trips = sp.value_load(n_ovf[0:1, 0:1], min_val=0, max_val=MAX_OVERFLOW)
            with sp.If(trips > 0):
                with sp.Fori(N_EXPERTS, trips + N_EXPERTS) as b:
                    e = sp.value_load(ovf_exp[0:1, bass.ds(b - N_EXPERTS, 1)], min_val=0, max_val=N_EXPERTS - 1)
                    weights(b, e)
            for n in range(NQ):
                sp.wait_ge(final_ready, n + 1)
                sp.dma_start(out_blocks[n], y_tok[:, n * TOP_K, :]).then_inc(out_stored, 16)
            sp.wait_ge(out_stored, 16 * NQ)

        @block.gpsimd
        def _(pool):
            g = nc.gpsimd
            g.memset(minus_half[:, :], -0.5).then_inc(consts_ready, 1)
            g.memset(ident[:, :], 0.0).then_inc(consts_ready, 1)
            g.memset(ones_b[:, :], 1.0).then_inc(consts_ready, 1)
            g.memset(before, 1.0).then_inc(consts_ready, 1)
            g.memset(mean_w[:, :], 1.0 / D_CONV).then_inc(consts_ready, 1)
            g.memset(eps_col[:, :], EPS).then_inc(consts_ready, 1)
            pool.wait_ge(consts_ready, 6)
            g.affine_select(out=ident[:, :], in_=ident[:, :], compare_op=ALU.not_equal, fill=1.0,
                            base=0, pattern=[[-1, P]], channel_multiplier=1).then_inc(consts_ready, 1)
            g.affine_select(out=before, in_=before, compare_op=ALU.is_gt, fill=0.0,
                            base=0, pattern=[[1, P]], channel_multiplier=-1).then_inc(consts_ready, 1)
            g.memset(zeros, 0.0).then_inc(zeros_ready, 1)
            g.memset(rpb_tile[:, :], 0.0).then_inc(rpb_zeroed, 1)
            g.iota(iota_i[:, :], [[QB, 3], [0, N_ROWS], [1, QB]], base=0, channel_multiplier=0).then_inc(iotas_ready, 1)
            pool.wait_ge(consts_ready, 8)
            g.tensor_copy(before_b[:, :], before).then_inc(consts_ready, 1)
            g.iota(p_int[:, 0:1], [[0, 1]], base=0, channel_multiplier=1).then_inc(iotas_ready, 1)
            g.iota(iota_f[:, :], [[1, 128]], base=0, channel_multiplier=0,
                   allow_small_or_imprecise_dtypes=True).then_inc(iotas_ready, 1)
            g.iota(tok_id[:, :], [[P, NQ]], base=0, channel_multiplier=1,
                   allow_small_or_imprecise_dtypes=True).then_inc(iotas_ready, 1)
            g.iota(thresholds[:, :], [[CAP, EXTRA]], base=CAP, channel_multiplier=0,
                   allow_small_or_imprecise_dtypes=True).then_inc(iotas_ready, 1)
            g.memset(area_u[:, :], 0.0).then_inc(upad_zeroed, 1)
            pool.wait_ge(rpb_zeroed, 1)
            pool.dma_start(rpb_tile[0:HEADS * RPB_H, QB:QB + RPB_W],
                           rpb[0].rearrange("h a b -> (h a) b")).then_inc(rpb_tile_loaded, 16)

            def rstd_of(i, ready):
                g.tensor_scalar(ms[:, i:i + 1], ss[:, i:i + 1], 1.0 / D_MODEL, EPS, ALU.mult, ALU.add).then_inc(ms_ready, 1)
                pool.wait_ge(ms_ready, i + 1)
                g.tensor_tensor(rstd[:, i:i + 1], ms[:, i:i + 1], minus_half[:, :], ALU.pow).then_inc(rstd_ready, 1)

            for n in range(NQ):
                pool.wait_ge(ss_ready, n + 1)
                rstd_of(n, ss_ready)
            pool.wait_ge(bout_loaded, 16)
            for n in range(NQ):
                pool.wait_ge(xn_ready, n + 1)
                g.tensor_tensor(h[:, n, :], h[:, n, :], bout_row, ALU.add).then_inc(xb_ready, 1)
            for g_i in range(8, 20):
                loaded, high, low = split_parts(g_i)
                pool.wait_ge(win_high_ready, g_i + 1)
                g.tensor_tensor(low, loaded, high.bitcast(F32), ALU.subtract).then_inc(win_low_pool, 1)
            pool.wait_ge(mask_step, 13)
            pool.wait_ge(y_stored, 16)
            pool.wait_ge(proj_done, 8)

            for hd in range(HEADS):
                pool.wait_ge(raw_loaded, 16 * N_ROWS * (hd // 2 + 1))
                raw = raw_bias[:, hd % 2, :].rearrange("p (r w) -> p r w", r=N_ROWS)
                for kind, (dst, m0, m1, o) in enumerate(((T_mid[:, hd, :], 0, 3, 0), (T_edge[:, hd, 0, :], 1, 3, 384),
                                                         (T_edge[:, hd, 1, :], 0, 2, 640))):
                    w = (m1 - m0) * P
                    src = raw[:, :, m0 * QB:m1 * QB].rearrange("p r (m c) -> p m r c", c=QB)
                    g.tensor_tensor(dst.rearrange("p (m r c) -> p m r c", r=N_ROWS, c=QB), src,
                                    mask[:, o:o + w].rearrange("p (m r c) -> p m r c", r=N_ROWS, c=QB),
                                    ALU.add).then_inc(tables_ready, 1)
            for c in range(4):
                ks = slice(2 * c, 2 * c + 2)
                pool.wait_ge(wout_high_ready, c + 1)
                g.tensor_tensor(wout_low[1][:, ks, :], unit(1)[:, ks, :], wout_high[1][:, ks, :].bitcast(F32),
                                ALU.subtract).then_inc(wout_low_pool, 1)
            for c in range(CC):
                pool.wait_ge(ln_rs_ready, 4)
                g.tensor_tensor(mixedT[:, c, :], mixedT[:, c, :], ln_rs, ALU.mult).then_inc(ln_scaled, 1)
            for c in range(CC):
                pool.wait_ge(silu_sig_ready, c + 1)
                g.tensor_scalar(mixedT[:, c, :], mixedT[:, c, :], colT[:, 24 + c:25 + c], colT[:, 28 + c:29 + c],
                                ALU.mult, ALU.add).then_inc(ln_affine, 1)
                pool.wait_ge(ln_affine, c + 1)
                by_blocks = convT_out[c].rearrange("p (n r q) -> p n r q", n=NQ, q=QB)
                g.tensor_tensor(by_blocks, mixedT[:, c, :].rearrange("p (r n q) -> p n r q", n=NQ, q=QB),
                                by_blocks, ALU.mult).then_inc(silu_ready, 1)
            for n in range(NQ):
                pool.wait_ge(ss2_ready, n + 1)
                rstd_of(NQ + n, ss2_ready)

            def gather(b):
                g.tensor_copy(tok_now[:, :], tok_tab[:, bass.ds(b, 1)])
                pool.drain()
                g.indirect_dma_start(out=xg[0:CAP, :], out_offset=None, in_=xn2_rows,
                                     in_offset=bass.IndirectOffsetOnAxis(ap=tok_now[:, 0:1], axis=0)).then_inc(xg_loaded, 16)

            for i in range(AHEAD):
                pool.wait_ge(high_ready, i + 1)
                g.tensor_tensor(w_low[i][:, :], w_raw[i][:, :], w_high[:, i, :].bitcast(F32), ALU.subtract).then_inc(low_ready, 1)
            pool.wait_ge(bias_high, 2)
            pool.wait_ge(low_ready, AHEAD)
            g.tensor_tensor(bias_gu[32:64, :], bias_stage[32:64, :], bias_gu[32:64, :].bitcast(F32),
                            ALU.subtract).then_inc(bias_split, 1)
            pool.wait_ge(bias_split, 1)
            pool.wait_ge(table_ready, 1)
            pool.wait_ge(xn2_stored, 16 * NQ)
            pool.wait_ge(wout_done, 2 * NQ)
            gather(0)

            def select(e):
                g.tensor_copy(selector[:, :], is_expert[:, bass.ds(e, 1)].to_broadcast([P, CAP])).then_inc(selector_ready, 1)

            def low_part(b, i):
                pool.wait_ge(high_ready, PIECES * b + i + 1)
                g.tensor_tensor(w_low[i][:, :], w_raw[i][:, :],
                                w_high[:, i % HIGH_RING, :].bitcast(F32), ALU.subtract).then_inc(low_last, 1)

            def silu(b, half):
                pool.wait_ge(g_sig_ready, 2 * b + half + 1)
                g.tensor_tensor(g_silu[:, half], g_lim[:, half], g_silu[:, half], ALU.mult).then_inc(g_silu_ready, 1)

            def pool_block(b, next_e=None):
                pool.wait_ge(xg_loaded, 16 * (b + 1))
                pool.wait_ge(xg_transposed, b + 1)
                gather(b + 1)
                silu(b, 0)
                for i in POOL_PIECES:
                    if i < 7:
                        low_part(b, i)
                silu(b, 1)
                for i in POOL_PIECES:
                    if i >= 7:
                        low_part(b, i)
                if next_e is not None:
                    pool.wait_ge(piece_used, PIECES * b + 9)
                    select(next_e)

            select(0)
            pool_block(0, 1)
            with pool.Fori(1, N_EXPERTS - 1) as b:
                pool_block(b, b + 1)
            pool_block(N_EXPERTS - 1)
            pool.wait_ge(overflow_ready, 2)
            trips = pool.value_load(n_ovf[0:1, 0:1], min_val=0, max_val=MAX_OVERFLOW)
            with pool.If(trips > 0):
                with pool.Fori(N_EXPERTS, trips + N_EXPERTS) as b:
                    e = pool.value_load(ovf_exp[0:1, bass.ds(b - N_EXPERTS, 1)], min_val=0, max_val=N_EXPERTS - 1)
                    pool.wait_ge(piece_used, PIECES * b)
                    select(e)
                    pool_block(b)
            pool.wait_ge(slot_ready, 1)
            pool.wait_ge(y_stored, 16 * (trips + N_EXPERTS + 1))
            g.tensor_tensor(slot[:, :], first_slot[:, :], pos_i[:, :], ALU.add).then_inc(slot_ready, 1)
            pool.wait_ge(slot_ready, 2)
            for i in range(NJ):
                g.indirect_dma_start(out=y_tok[:, i, :], out_offset=None, in_=y_rows,
                                     in_offset=bass.IndirectOffsetOnAxis(ap=slot[:, i:i + 1], axis=0)).then_inc(y_back[i // TOP_K], 16)
            for n in range(NQ):
                pool.wait_ge(ss3_ready, n + 1)
                rstd_of(2 * NQ + n, ss3_ready)

        @block.scalar
        def _(act):
            s = nc.scalar
            act.dma_start(gmix_row, row_bcast(g_mix, D_MODEL)).then_inc(rows_loaded, 16)
            for i, vec in enumerate((conv_b, ln_g, ln_b)):
                act.dma_start(stage[20 + CC * i:20 + CC * (i + 1), 0, :],
                              vec[0].rearrange("(c p) -> c p", p=P)).then_inc(stage_loaded, 16)
            act.dma_start(bout_row, row_bcast(b_out, D_MODEL)).then_inc(bout_loaded, 16)

            def xnT_half(n):
                act.wait_ge(xn_transposed, 2 * n + 2)
                s.copy(xnT_high[:, 4:8, n * P:(n + 1) * P],
                       bank[4 + (2 * n + 1) % 4][:, :].rearrange("p (k t) -> p k t", k=4)).then_inc(xnT_act, 1)

            def pT_out(j):
                m0, m1 = keys_of(steps[j][0])
                w = (m1 - m0) * P
                act.wait_ge(p_transposed, j + 1)
                s.copy(PT_sb[:, 1, 0:w], bank[6][:, 0:w]).then_inc(pT_act, 1)

            for n in range(NQ):
                act.wait_ge(x_loaded[n], 16)
                if n:
                    act.wait_ge(ss_ready, n)
                s.activation(junk_norm[n % 2], h[:, n, :], ACT.Square, accum_out=ss[:, n:n + 1]).then_inc(ss_ready, 1)
            for n in range(NQ):
                xnT_half(n)
            def win_high_part(g):
                loaded, high, _ = split_parts(g)
                act.wait_ge(win_loaded[4 if g >= 16 else groups[g][0] - 1], 16)
                if 4 <= g < 8:
                    act.wait_ge(proj_done, g - 3)
                elif 9 <= g < 16:
                    act.wait_ge(proj_done, 8)
                elif g >= 16:
                    act.wait_ge(proj_done, 12)
                s.copy(high, loaded).then_inc(win_high_ready, 1)

            for g in range(4):
                win_high_part(g)
            act.wait_ge(cols_ready, 1)
            for c in range(CC):
                act.wait_ge(proj_done, 2 * c + 1)
                if c >= 2:
                    act.wait_ge(glu_ready, 4 * (c - 1))
                s.activation(sg[:, c % 2, :], bank[2 * c % 4][:, :], ACT.Sigmoid, bias=colT[:, 4 + c:5 + c]).then_inc(act_evac, 1)
                for g in {0: (4, 5), 1: (6, 7, 8)}.get(c, ()):
                    win_high_part(g)
            act.wait_ge(bq_ready, 1)
            for g in (9, 10):
                win_high_part(g)
            for i in range(4):
                act.wait_ge(proj_done, 8 + i + 1)
                s.activation(qT[:, i, :], bank[i][:, :], ACT.Identity, bias=bq[:, i:i + 1], scale=HEAD_DIM ** -0.5).then_inc(act_evac, 1)
                if i < 3:
                    for g in {0: (11, 12), 1: (13, 14), 2: (15,)}[i]:
                        win_high_part(g)
            for g in range(16, 20):
                win_high_part(g)
            act.wait_ge(xb_ready, NQ)
            for i in range(4):
                act.wait_ge(proj_done, 12 + i + 1)
                s.activation(kT[:, i, :], bank[i][:, :], ACT.Identity, bias=colT[:, 12 + i:13 + i]).then_inc(act_evac, 1)
            act.wait_ge(glu_ready, 16)
            for n in range(NQ):
                act.wait_ge(proj_done, 16 + n + 1)
                s.copy(v_sb[:, n, :], bank[n][:, :]).then_inc(act_evac, 1)
            def wout_high_part(half, c):
                act.wait_ge(wout_loaded[half], 16)
                ks = slice(2 * c, 2 * c + 2)
                s.copy(wout_high[half][:, ks, :], unit((6, 1)[half])[:, ks, :]).then_inc(wout_high_ready, 1)

            act.wait_ge(proj_done, 20)
            for c in range(4):
                wout_high_part(1, c)
            for c in range(CC):
                act.wait_ge(centred, c + 1)
                if c >= 2:
                    act.wait_ge(var_part, c - 1)
                s.activation(sq[:, c % 2, :], mixedT[:, c, :], ACT.Square).then_inc(squared, 1)
            act.wait_ge(var_part, CC)
            s.activation(ln_rs, bank[5][:, :], ACT.Sqrt, bias=eps_col[:, :]).then_inc(std_ready, 1)
            def attn_high_part(n):
                act.wait_ge(oT_ready, n + 1)
                s.copy(attn_high[:, :, n * P:(n + 1) * P], mixedT[:, 4:8, n * P:(n + 1) * P]).then_inc(attn_high_ready, 1)

            for i in range(NS):
                n, hd = steps[i]
                m0, m1 = keys_of(n)
                w = (m1 - m0) * P
                act.wait_ge(neg_max_ready, i + 1)
                if i >= 3:
                    act.wait_ge(p_transposed, i - 2)
                s.activation(P_sb[:, i % 3, 0:w], S_sb[:, i % 3, 0:w], ACT.Exp, bias=neg_max[:, i:i + 1],
                             accum_out=row_sum[:, i:i + 1]).then_inc(exp_ready, 1)
                j = i - 2
                if j >= 1 and j % 2:
                    pT_out(j)
                if 2 <= i <= 5:
                    wout_high_part(0, i - 2)
                if i == 9:
                    for c in range(CC):
                        act.wait_ge(silu_ready, CC)
                        s.copy(conv_high[:, c, :], convT_out[c]).then_inc(conv_high_ready, 1)
                if i >= 12 and (i - 12) % HEADS == 0:
                    attn_high_part((i - 12) // HEADS)
                if i == 6:
                    for c in range(CC):
                        act.wait_ge(ln_scaled, c + 1)
                        s.activation(convT_out[c].rearrange("p (n r q) -> p n r q", n=NQ, q=QB),
                                     mixedT[:, c, :].rearrange("p (r n q) -> p n r q", n=NQ, q=QB), ACT.Sigmoid, bias=colT[:, 28 + c:29 + c],
                                     scale=colT[:, 24 + c:25 + c]).then_inc(silu_sig_ready, 1)
            pT_out(NS - 1)
            attn_high_part(NQ - 1)

            act.wait_ge(pv_done, NS)
            act.dma_start(br_row, row_bcast(b_router, N_EXPERTS)).then_inc(router_loaded, 16)
            act.dma_start(wr[:, :, :], w_router[0].rearrange("(k p) e -> p k e", p=P)).then_inc(router_loaded, 16)
            act.dma_start(gffn_row, row_bcast(g_ffn, D_MODEL)).then_inc(norm_rows_loaded, 16)
            act.dma_start(gfin_row, row_bcast(g_final, D_MODEL)).then_inc(norm_rows_loaded, 16)

            def square2(n):
                act.wait_ge(h_ready, 2 * n + 2)
                if n:
                    act.wait_ge(ss2_ready, n)
                s.activation(junk, h[:, n, :], ACT.Square, accum_out=ss[:, NQ + n:NQ + n + 1]).then_inc(ss2_ready, 1)

            def xn2T_half(n):
                act.wait_ge(xn2_ready, n + 1)
                act.dma_start(xn2_rows[n * P:(n + 1) * P, :], xn2[:, n, :]).then_inc(xn2_stored, 16)
                act.wait_ge(xn2_transposed, 2 * n + 2)
                s.copy(xn2T[n // 2][:, n % 2, 4:8, :],
                       bank[T_BANKS[(2 * n + 1) % 3]][:, :].rearrange("p (k t) -> p k t", k=4)).then_inc(xn2T_act, 1)

            square2(0)
            square2(1)
            xn2T_half(0)
            square2(2)
            xn2T_half(1)
            square2(3)
            xn2T_half(2)
            xn2T_half(3)

            def high_part(b, i, first=False):
                act.wait_ge(raw_piece[i], 16 * (b + 1))
                if not (first and i <= AHEAD):
                    act.wait_ge(piece_used, PIECES * b + i - AHEAD)
                s.copy(w_high[:, i % HIGH_RING, :], w_raw[i][:, :]).then_inc(high_ready, 1)

            act.wait_ge(wout_done, 2 * NQ)
            for i in range(AHEAD):
                high_part(0, i, first=True)
            act.wait_ge(xn2_transposed, 2 * NQ)
            act.wait_ge(xn2_stored, 16 * NQ)
            for i, mat in enumerate((b_gate, b_gate, b_up, b_up)):
                act.dma_start(bias_stage[32 * i:32 * i + 32, :], mat[0]).then_inc(bias_rows_loaded, 16)
            for n in range(NQ):
                act.wait_ge(top_ready, n + 1)
                s.mul(gate_neg[:, n:n + 1], top_val[:, n, 0:1], -1.0).then_inc(gate_exp, 1)
                act.wait_ge(gate_exp, 2 * n + 1)
                s.activation(gates[:, n, :], top_val[:, n, 0:TOP_K], ACT.Exp, bias=gate_neg[:, n:n + 1],
                             accum_out=gate_sum[:, n:n + 1]).then_inc(gate_exp, 1)
            act.wait_ge(logits_done, NQ)
            for i in range(2):
                act.dma_start(down_stage[32 * i:32 * i + 32, :], b_down[0]).then_inc(bias_rows_loaded, 16)
            act.wait_ge(bias_rows_loaded, 96)
            s.copy(bias_gu[:, :], bias_stage).then_inc(bias_high, 1)
            s.copy(bias_d[0:64, :], down_stage[0:64, :]).then_inc(bias_high, 1)

            def rows_out(b):
                act.wait_ge(y_stored, 16 * (b + 1))
                act.wait_ge(piece_used, PIECES * (b + 1))
                for half in range(2):
                    s.copy(y_sb[0:CAP, half * HALF:(half + 1) * HALF], bank[4 + half][0:CAP, :]).then_inc(y_ready, 1)
                act.wait_ge(y_ready, 2 * b + 2)
                act.dma_start(y_rows[bass.ds(b * CAP, CAP), :], y_sb[0:CAP, :]).then_inc(y_stored, 16)

            def sigmoid(b, half):
                act.wait_ge(g_limited, 2 * b + half + 1)
                s.activation(g_silu[:, half], g_lim[:, half], ACT.Sigmoid, scale=SWIGLU_ALPHA).then_inc(g_sig_ready, 1)

            def four(ap, half):
                return ap[:, 4 * half:4 * half + 4, :]

            def out_of(i):
                return bank[i][:, 0:4 * CAP].rearrange("p (k t) -> p k t", k=4)

            def hT_high_part(b, half):
                act.wait_ge(h_transposed, 2 * b + half + 1)
                s.copy(four(hT_high, half), out_of(6 + half)).then_inc(hT_high_ready, 1)

            def xT_high_part(b, half):
                act.wait_ge(xg_transposed, b + 1)
                s.copy(four(xT_high, half), out_of(6 + half)).then_inc(xT_high_ready, 1)

            def act_block(b, first=False, has_next=True):
                for i in range(PIECES):
                    if i >= 10:
                        xT_high_part(b + 1, i - 10)
                    if i == 6:
                        hT_high_part(b, 0)
                    if i == 9:
                        hT_high_part(b, 1)
                    if i + AHEAD < PIECES:
                        high_part(b, i + AHEAD, first)
                    elif has_next:
                        high_part(b + 1, i + AHEAD - PIECES)
                    if i in (2, 6):
                        sigmoid(b, i // 4)
                    if i == 0 and not first:
                        rows_out(b - 1)

            for half in range(2):
                xT_high_part(0, half)
            act_block(0, first=True)
            with act.Fori(1, N_EXPERTS - 1) as b:
                act_block(b)
            act_block(N_EXPERTS - 1, has_next=False)
            act.wait_ge(overflow_ready, 2)
            trips = act.value_load(n_ovf[0:1, 0:1], min_val=0, max_val=MAX_OVERFLOW)
            with act.If(trips > 0):
                with act.Fori(N_EXPERTS, trips + N_EXPERTS) as b:
                    for i in range(AHEAD):
                        high_part(b, i)
                    act_block(b, has_next=False)
            rows_out(trips + N_EXPERTS - 1)
            for n in range(NQ):
                act.wait_ge(combined, TOP_K * (n + 1))
                if n:
                    act.wait_ge(ss3_ready, n)
                s.activation(junk, h[:, n, :], ACT.Square, accum_out=ss[:, 2 * NQ + n:2 * NQ + n + 1]).then_inc(ss3_ready, 1)

        @block.vector
        def _(dve):
            v = nc.vector
            dve.wait_ge(iotas_ready, 5)
            v.tensor_scalar(p_int[:, 1:2], p_int[:, 0:1], QB - 1, None, ALU.bitwise_and)
            v.tensor_scalar(p_int[:, 2:3], p_int[:, 0:1], N_EXPERTS - 1, None, ALU.bitwise_and).then_inc(mask_step, 1)
            v.tensor_copy(iota_u, iota_i[:, :]).then_inc(mask_step, 1)
            dve.wait_ge(mask_step, 2)
            v.tensor_copy(c_flt[:, :], p_int[:, 1:3]).then_inc(mask_step, 1)
            dve.wait_ge(mask_step, 3)
            v.tensor_scalar(win_lo[:, 0:1], c_flt[:, 0:1], WIN_W / 2, None, ALU.add)
            v.tensor_scalar(win_lo[:, 1:2], c_flt[:, 0:1], WIN_W / 2, float(QB), ALU.add, ALU.max)
            v.tensor_scalar(win_lo[:, 2:3], c_flt[:, 0:1], WIN_W / 2, float(QB), ALU.add, ALU.min).then_inc(mask_step, 3)
            dve.wait_ge(mask_step, 6)
            v.tensor_scalar(is_expert[:, :], iota_f[:, 0:N_EXPERTS], c_flt[:, 1:2], None, ALU.is_equal)
            v.tensor_scalar(win_hi[:, :], win_lo[:, :], WIN_W - 1.0, None, ALU.add)
            for kind, (o, a, w) in enumerate(((0, 0, 384), (384, 128, 256), (640, 0, 256))):
                v.tensor_scalar(mask[:, o:o + w], iota_u[:, a:a + w], win_lo[:, kind:kind + 1], None, ALU.is_ge).then_inc(mask_step, 1)
            dve.wait_ge(mask_step, 9)
            for kind, (o, a, w) in enumerate(((0, 0, 384), (384, 128, 256), (640, 0, 256))):
                v.scalar_tensor_tensor(mask[:, o:o + w], iota_u[:, a:a + w], win_hi[:, kind:kind + 1],
                                       mask[:, o:o + w], ALU.is_le, ALU.mult).then_inc(mask_step, 1)
            dve.wait_ge(mask_step, 12)
            v.tensor_scalar(mask, mask, -1.0, NEG, ALU.add, ALU.mult).then_inc(mask_step, 1)

            dve.wait_ge(rows_loaded, 16)
            for n in range(NQ + 1):
                if n < NQ:
                    dve.wait_ge(rstd_ready, n + 1)
                    if n >= 2:
                        dve.wait_ge(xn_transposed, 2 * (n - 1))
                    v.scalar_tensor_tensor(xn_tile[:, n % 2, :], h[:, n, :], rstd[:, n:n + 1], gmix_row,
                                           ALU.mult, ALU.mult).then_inc(xn_ready, 1)
                if n:
                    dve.wait_ge(xn_transposed, 2 * (n - 1) + 1)
                    tokens = slice((n - 1) * P, n * P)
                    v.tensor_copy(xnT_high[:, 0:4, tokens],
                                  bank[4 + 2 * (n - 1) % 4][:, :].rearrange("p (k t) -> p k t", k=4)).then_inc(xnT_dve, 1)
                    for half, high_done in enumerate((xnT_dve, xnT_act)):
                        dve.wait_ge(high_done, n)
                        ks = slice(4 * half, 4 * half + 4)
                        v.tensor_tensor(xnT_low[:, ks, tokens],
                                        bank[4 + (2 * (n - 1) + half) % 4][:, :].rearrange("p (k t) -> p k t", k=4),
                                        xnT_high[:, ks, tokens].bitcast(F32), ALU.subtract).then_inc(xnT_low_ready, 1)
            dve.wait_ge(stage_transposed, 1)
            v.tensor_copy(colT[:, :], bank[0][:, 0:32])
            v.tensor_copy(convT[:, 0:CONV_K * CC], bank[0][:, 32:32 + CONV_K * CC]).then_inc(cols_ready, 1)
            dve.wait_ge(cols_ready, 1)
            v.tensor_scalar(bq[:, :], colT[:, 8:12], HEAD_DIM ** -0.5, None, ALU.mult).then_inc(bq_ready, 1)
            def win_low_part(g):
                loaded, high, low = split_parts(g)
                dve.wait_ge(win_high_ready, g + 1)
                v.tensor_tensor(low, loaded, high.bitcast(F32), ALU.subtract).then_inc(win_low_dve, 1)

            def glu(c):
                dve.wait_ge(proj_done, 2 * c + 2)
                dve.wait_ge(act_evac, c + 1)
                dst = u_pad[:, c, PAD:PAD + SEQ].rearrange("p (r n q) -> p n r q", n=NQ, q=QB)
                for n in range(NQ):
                    v.scalar_tensor_tensor(dst[:, n], bank[(2 * c + 1) % 4][:, n * P:(n + 1) * P].rearrange("p (r q) -> p r q", q=QB),
                                           colT[:, c:c + 1],
                                           sg[:, c % 2, n * P:(n + 1) * P].rearrange("p (r q) -> p r q", q=QB),
                                           ALU.add, ALU.mult).then_inc(glu_ready, 1)

            def conv_start(c0):
                dve.wait_ge(glu_ready, 4 * (c0 + 2))
                for c in (c0, c0 + 1):
                    v.tensor_scalar(mixedT[:, c, :], u_pad[:, c, 0:SEQ], convT[:, c:c + 1], colT[:, 20 + c:21 + c],
                                    ALU.mult, ALU.add).then_inc(conv_tap, 1)

            def conv_taps(c0, first, end):
                with dve.Fori(first, end) as k:
                    for c in (c0, c0 + 1):
                        dve.wait_ge(conv_tap, k * 2 + (CONV_K * c0 + c - c0 - 1))
                        v.scalar_tensor_tensor(mixedT[:, c, :], u_pad[:, c, bass.ds(k, SEQ)], convT[:, bass.ds(k * CC + c, 1)],
                                               mixedT[:, c, :], ALU.mult, ALU.add).then_inc(conv_tap, 1)

            for g in range(4):
                win_low_part(g)
            dve.wait_ge(upad_zeroed, 1)
            glu(0)
            win_low_part(4)
            win_low_part(5)
            glu(1)
            win_low_part(6)
            win_low_part(7)
            conv_start(0)
            conv_taps(0, 1, 6)
            glu(2)
            conv_taps(0, 6, 13)
            glu(3)
            conv_taps(0, 13, CONV_K)
            conv_start(2)
            conv_taps(2, 1, CONV_K)
            dve.wait_ge(mean_done, 1)
            dve.wait_ge(conv_tap, CONV_K * CC)
            for c in range(CC):
                v.tensor_tensor(mixedT[:, c, :], mixedT[:, c, :], bank[4][:, :], ALU.subtract).then_inc(centred, 1)

            def scores(i):
                n, hd = steps[i]
                m0, m1 = keys_of(n)
                w = (m1 - m0) * P
                dve.wait_ge(qk_done, i + 1)
                if i >= 3:
                    dve.wait_ge(exp_ready, i - 2)
                v.tensor_tensor_reduce(out=S_sb[:, i % 3, 0:w], in0=bank[i % 2][:, 0:w], in1=table_of(n, hd),
                                       scale=1.0, scalar=-3.0e38, op0=ALU.add, op1=ALU.max,
                                       accum_out=row_max[:, i:i + 1]).then_inc(s_ready, 1)
                dve.wait_ge(s_ready, i + 1)
                v.tensor_scalar(neg_max[:, i:i + 1], row_max[:, i:i + 1], -1.0, None, ALU.mult).then_inc(neg_max_ready, 1)

            def residual(n, half):
                dve.wait_ge(wout_done, 2 * n + half + 1)
                v.tensor_tensor(h[:, n, half * HALF:(half + 1) * HALF], h[:, n, half * HALF:(half + 1) * HALF],
                                bank[OUT_BANKS[half]][:, :], ALU.add).then_inc(h_ready, 1)

            dve.wait_ge(tables_ready, 3 * HEADS)
            dve.wait_ge(xb_ready, NQ)
            def attn_low_part(n):
                tokens = slice(n * P, (n + 1) * P)
                dve.wait_ge(attn_high_ready, n + 1)
                v.tensor_tensor(attn_low[:, :, tokens], mixedT[:, 4:8, tokens], attn_high[:, :, tokens].bitcast(F32),
                                ALU.subtract).then_inc(attn_low_ready, 1)

            def normalise(n):
                dve.wait_ge(exp_ready, HEADS * (n + 1))
                v.reciprocal(row_inv[:, n * HEADS:(n + 1) * HEADS], row_sum[:, n * HEADS:(n + 1) * HEADS]).then_inc(inv_ready, 1)
                dve.wait_ge(inv_ready, n + 1)
                dve.wait_ge(pv_done, HEADS * (n + 1))
                if n:
                    dve.wait_ge(o_transposed, n)
                v.tensor_tensor(O_sb.rearrange("p (h d) -> p h d", d=HEAD_DIM),
                                bank[7][:, :].rearrange("p (h d) -> p h d", d=HEAD_DIM),
                                row_inv[:, n * HEADS:(n + 1) * HEADS].unsqueeze(2).to_broadcast([P, HEADS, HEAD_DIM]),
                                ALU.mult).then_inc(o_ready, 1)

            for i in range(NS + 5):
                if i >= 11 and (i - 11) % HEADS == 0:
                    normalise((i - 11) // HEADS)
                if i < NS:
                    scores(i)
                for half, at in enumerate(RESIDUAL_AT):
                    n = (i - at) // HEADS
                    if i >= at and (i - at) % HEADS == 0 and n < NQ - 1:
                        residual(n, half)
                if 4 <= i <= 7:
                    ks = slice(2 * (i - 4), 2 * (i - 4) + 2)
                    dve.wait_ge(wout_high_ready, 4 + i - 3)
                    v.tensor_tensor(wout_low[0][:, ks, :], unit(6)[:, ks, :], wout_high[0][:, ks, :].bitcast(F32),
                                    ALU.subtract).then_inc(wout_low_dve, 1)
                if i == 9:
                    for c in range(CC):
                        dve.wait_ge(conv_high_ready, c + 1)
                        v.tensor_tensor(conv_low[c][:, :], convT_out[c], conv_high[:, c, :].bitcast(F32),
                                        ALU.subtract).then_inc(conv_low_ready, 1)
                if i >= 13 and (i - 13) % HEADS == 0:
                    attn_low_part((i - 13) // HEADS)
                if 1 <= i <= 4:
                    dve.wait_ge(std_ready, 1)
                    v.reciprocal(ln_rs[:, (i - 1) * P:i * P], ln_rs[:, (i - 1) * P:i * P]).then_inc(ln_rs_ready, 1)
                j = i - 2
                if 0 <= j < NS and j % 2 == 0:
                    m0, m1 = keys_of(steps[j][0])
                    w = (m1 - m0) * P
                    dve.wait_ge(p_transposed, j + 1)
                    v.tensor_copy(PT_sb[:, 0, 0:w], bank[3][:, 0:w]).then_inc(pT_dve, 1)
                if i >= 12 and (i - 12) % HEADS == 0:
                    n = (i - 12) // HEADS
                    dve.wait_ge(o_transposed, n + 1)
                    v.tensor_tensor(mixedT[:, 4:8, n * P:(n + 1) * P], bank[5][:, :].rearrange("p (k t) -> p k t", k=4),
                                    colT[:, 16:20].unsqueeze(2).to_broadcast([P, 4, P]), ALU.add).then_inc(oT_ready, 1)

            attn_low_part(NQ - 1)
            def norm2(n):
                dve.wait_ge(rstd_ready, NQ + n + 1)
                v.scalar_tensor_tensor(xn2[:, n, :], h[:, n, :], rstd[:, NQ + n:NQ + n + 1], gffn_row,
                                       ALU.mult, ALU.mult).then_inc(xn2_ready, 1)
                dve.wait_ge(xn2_transposed, 2 * n + 1)
                v.tensor_copy(xn2T[n // 2][:, n % 2, 0:4, :],
                              bank[T_BANKS[2 * n % 3]][:, :].rearrange("p (k t) -> p k t", k=4)).then_inc(xn2T_dve, 1)

            def top(n):
                dve.wait_ge(logits_done, n + 1)
                v.tensor_tensor(logits[:, n, :], bank[7][:, n * 32:(n + 1) * 32], br_row, ALU.add).then_inc(logits_ready, 1)
                dve.wait_ge(logits_ready, n + 1)
                v.max(top_val[:, n, :], logits[:, n, :]).then_inc(top_ready, 1)
                dve.wait_ge(top_ready, n + 1)
                v.max_index(top_idx[:, n, :], top_val[:, n, :], logits[:, n, :]).then_inc(route_step, 1)

            dve.wait_ge(norm_rows_loaded, 32)
            dve.wait_ge(router_loaded, 32)
            residual(NQ - 1, 0)
            norm2(0)
            residual(NQ - 1, 1)
            norm2(1)
            top(0)
            norm2(2)
            top(1)
            norm2(3)
            top(2)
            top(3)

            def low_part(b, i):
                if i in DVE_PIECES:
                    dve.wait_ge(high_ready, PIECES * b + i + 1)
                    v.tensor_tensor(w_low[i][:, :], w_raw[i][:, :],
                                    w_high[:, i % HIGH_RING, :].bitcast(F32), ALU.subtract).then_inc(low_ready, 1)

            n_steps = [NQ]

            def then(ins):
                n_steps[0] += 1
                ins.then_inc(route_step, 1)
                dve.wait_ge(route_step, n_steps[0])

            def wide(ap, n):
                return ap.unsqueeze(2).to_broadcast([ap.shape[0], ap.shape[1], n])

            def across(ap, n):
                return ap.unsqueeze(1).to_broadcast([ap.shape[0], n, ap.shape[1]])

            dve.wait_ge(route_step, NQ)
            dve.wait_ge(ss2_ready, NQ)
            then(v.tensor_copy(e_idx[:, :].rearrange("p (n j) -> p n j", j=TOP_K), top_idx[:, :, 0:TOP_K]))
            then(v.tensor_tensor(exp_1h, across(iota_f[:, 0:N_EXPERTS], NJ), wide(e_idx[:, :], N_EXPERTS), ALU.is_equal))
            with nc.allow_low_precision(reason="zeros and ones"):
                v.tensor_reduce(chosen[:, :, :], exp_1h.rearrange("p (n j) e -> p n e j", j=TOP_K), AX.X, ALU.add).then_inc(chosen_ready, 1)
            dve.wait_ge(rank_done, 1)
            then(v.tensor_copy(counts[:, :], bank[0][:, NQ * 32:NQ * 32 + 32]))
            then(v.tensor_tensor(picked.rearrange("p (n j) e -> p n j e", j=TOP_K),
                                 exp_1h.rearrange("p (n j) e -> p n j e", j=TOP_K),
                                 bank[0][:, 0:NQ * 32].rearrange("p (n e) -> p n e", n=NQ).unsqueeze(2).to_broadcast([P, NQ, TOP_K, N_EXPERTS]),
                                 ALU.mult))
            then(v.tensor_reduce(rank[:, :], picked, AX.X, ALU.add))
            over = cmp[:, 0:EXTRA * N_EXPERTS].rearrange("p (i e) -> p i e", i=EXTRA)
            then(v.tensor_tensor(over, across(counts[:, :], EXTRA), wide(thresholds[:, :], N_EXPERTS), ALU.is_gt))
            then(v.tensor_reduce(n_extra[:, :], over.rearrange("p i e -> p e i"), AX.X, ALU.add))
            v.memset(cum[:, :, 0:N_EXPERTS], 0.0)
            then(v.tensor_copy(cum[:, 0, N_EXPERTS:], n_extra[:, :]))
            cur, shift = 0, 1
            while shift < N_EXPERTS:
                then(v.tensor_tensor(cum[:, 1 - cur, N_EXPERTS:], cum[:, cur, N_EXPERTS:],
                                     cum[:, cur, N_EXPERTS - shift:2 * N_EXPERTS - shift], ALU.add))
                cur, shift = 1 - cur, 2 * shift
            upto = cum[:, cur, N_EXPERTS:]
            then(v.tensor_tensor(first_extra[:, :], upto, n_extra[:, :], ALU.subtract))
            then(v.tensor_tensor(picked, exp_1h, across(first_extra[:, :], NJ), ALU.mult))
            then(v.tensor_reduce(first_j[:, :], picked, AX.X, ALU.add))
            past = cmp[:, 0:NJ * EXTRA].rearrange("p (i t) -> p i t", i=NJ)
            then(v.tensor_tensor(past, wide(rank[:, :], EXTRA), across(thresholds[:, :], NJ), ALU.is_ge))
            then(v.tensor_reduce(extra_j[:, :], past, AX.X, ALU.add))
            then(v.scalar_tensor_tensor(pos[:, :], extra_j[:, :], -float(CAP), rank[:, :], ALU.mult, ALU.add))
            v.tensor_tensor(pos_1h[:, :, :], across(iota_f[:, 0:CAP], NJ), wide(pos[:, :], CAP), ALU.is_equal).then_inc(onehots_ready, 1)
            then(v.tensor_scalar(is_extra[:, :], extra_j[:, :], 1.0, None, ALU.min))
            then(v.tensor_tensor(tmp_j[:, :], first_j[:, :], extra_j[:, :], ALU.add))
            then(v.scalar_tensor_tensor(tmp_j[:, :], tmp_j[:, :], N_EXPERTS - 1.0, e_idx[:, :], ALU.add, ALU.subtract))
            then(v.tensor_tensor(tmp_j[:, :], tmp_j[:, :], is_extra[:, :], ALU.mult))
            then(v.tensor_tensor(blk[:, :], tmp_j[:, :], e_idx[:, :], ALU.add))
            then(v.tensor_tensor(blk_1h[:, :, :], across(iota_f[:, 0:COLS], NJ), wide(blk[:, :], COLS), ALU.is_equal))
            v.tensor_tensor(blk_1h[:, :, :].rearrange("p (n j) c -> p n (j c)", j=TOP_K),
                            blk_1h[:, :, :].bitcast(F32).rearrange("p (n j) c -> p n (j c)", j=TOP_K),
                            wide(tok_id[:, :], TOP_K * COLS), ALU.mult).then_inc(onehots_ready, 1)
            dve.wait_ge(table_done, 1)
            v.tensor_copy(tok_tab[:, :], bank[1][0:CAP, 0:COLS]).then_inc(table_ready, 1)
            v.tensor_scalar(first_slot[:, :], blk[:, :], float(CAP), None, ALU.mult)
            v.tensor_copy(pos_i[:, :], pos[:, :]).then_inc(slot_ready, 1)
            v.tensor_copy(n_ovf[:, :], cum[0:1, cur, 2 * N_EXPERTS - 1:]).then_inc(overflow_ready, 1)
            seen = cmp[0:1, :].rearrange("p (b e) -> p b e", e=N_EXPERTS)
            then(v.tensor_tensor(seen, wide(iota_f[0:1, 0:MAX_OVERFLOW], N_EXPERTS), across(cum[0:1, cur, N_EXPERTS:], MAX_OVERFLOW), ALU.is_ge))
            then(v.tensor_reduce(ovf_exp_f[:, :], seen, AX.X, ALU.add))
            v.tensor_scalar(ovf_exp[:, :], ovf_exp_f[:, :], N_EXPERTS - 1.0, None, ALU.min).then_inc(overflow_ready, 1)
            dve.wait_ge(gate_exp, 2 * NQ)
            then(v.reciprocal(gate_sum[:, :], gate_sum[:, :]))
            v.tensor_tensor(gates[:, :, :], gates[:, :, :], wide(gate_sum[:, :], TOP_K), ALU.mult).then_inc(gates_ready, 1)

            dve.wait_ge(bias_high, 2)
            dve.wait_ge(bias_split, 1)
            for low, rows, p in ((bias_gu, bias_stage, 96), (bias_d, down_stage, 32)):
                v.tensor_tensor(low[p:p + 32, :], rows[p:p + 32, :], low[p:p + 32, :].bitcast(F32),
                                ALU.subtract).then_inc(bias_split, 1)

            def four(ap, half):
                return ap[:, 4 * half:4 * half + 4, :]

            def out_of(i):
                return bank[i][:, 0:4 * CAP].rearrange("p (k t) -> p k t", k=4)

            def xT_low_part(b, half):
                dve.wait_ge(xT_high_ready, 2 * b + half + 1)
                v.tensor_tensor(four(xT_low, half), out_of(6 + half), four(xT_high, half).bitcast(F32), ALU.subtract).then_inc(xT_low_ready, 1)

            def hT_low_part(b, half):
                dve.wait_ge(hT_high_ready, 2 * b + half + 1)
                v.tensor_tensor(four(hT_low, half), out_of(6 + half), four(hT_high, half).bitcast(F32), ALU.subtract).then_inc(hT_low_ready, 1)

            def limit_gate(b, half):
                dve.wait_ge(piece_used, PIECES * b + 4 * half + 2)
                v.tensor_scalar(g_lim[:, half], bank[2 * half][0:CAP, :], SWIGLU_LIMIT, None, ALU.min).then_inc(g_limited, 1)

            def hidden(b, half):
                dve.wait_ge(piece_used, PIECES * b + 4 * half + 4)
                v.tensor_scalar(u_lim[:, half], bank[2 * half + 1][0:CAP, :], SWIGLU_LIMIT, -SWIGLU_LIMIT,
                                ALU.min, ALU.max).then_inc(u_limited, 1)
                dve.wait_ge(u_limited, 2 * b + half + 1)
                dve.wait_ge(g_silu_ready, 2 * b + half + 1)
                v.scalar_tensor_tensor(h_tok[:, half], u_lim[:, half], 1.0, g_silu[:, half], ALU.add, ALU.mult).then_inc(h_tok_ready, 1)

            def dve_block(b, has_next=True):
                for i in range(PIECES):
                    if i in (2, 6):
                        limit_gate(b, i // 4)
                    if i in (4, 8):
                        hidden(b, i // 4 - 1)
                    if i == 9:
                        hT_low_part(b, 1)
                    if i >= 10:
                        xT_low_part(b + 1, i - 10)
                    if i + AHEAD < PIECES:
                        low_part(b, i + AHEAD)
                    elif has_next:
                        low_part(b + 1, i + AHEAD - PIECES)
                    if i == 6:
                        hT_low_part(b, 0)

            for half in range(2):
                xT_low_part(0, half)
            dve.wait_ge(low_ready, AHEAD)
            dve_block(0)
            with dve.Fori(1, N_EXPERTS - 1) as b:
                dve_block(b)
            dve_block(N_EXPERTS - 1, has_next=False)
            trips = dve.value_load(n_ovf[0:1, 0:1], min_val=0, max_val=MAX_OVERFLOW)
            with dve.If(trips > 0):
                with dve.Fori(N_EXPERTS, trips + N_EXPERTS) as b:
                    for i in range(AHEAD):
                        low_part(b, i)
                    dve_block(b, has_next=False)
            dve.wait_ge(gates_ready, 1)
            for n in range(NQ + 1):
                if n < NQ:
                    dve.wait_ge(y_back[n], 16 * TOP_K)
                    for j in range(TOP_K):
                        if j:
                            dve.wait_ge(combined, TOP_K * n + j)
                        v.scalar_tensor_tensor(h[:, n, :], y_tok[:, n * TOP_K + j, :], gates[:, n, j:j + 1], h[:, n, :],
                                               ALU.mult, ALU.add).then_inc(combined, 1)
                if n:
                    m = n - 1
                    dve.wait_ge(rstd_ready, 2 * NQ + m + 1)
                    v.scalar_tensor_tensor(y_tok[:, m * TOP_K, :], h[:, m, :], rstd[:, 2 * NQ + m:2 * NQ + m + 1], gfin_row,
                                           ALU.mult, ALU.mult).then_inc(final_ready, 1)

        @block.tensor
        def _(pe):
            t = nc.tensor
            pe.wait_ge(consts_ready, 9)
            for n in range(NQ):
                pe.wait_ge(xn_ready, n + 1)
                for half in range(2):
                    i = 2 * n + half
                    if i >= 4:
                        pe.wait_ge(xnT_low_ready, i - 3)
                    for c in range(4):
                        k = 4 * half + c
                        last = t.transpose(bank[4 + i % 4][:, c * P:(c + 1) * P], xn_tile[:, n % 2, k * P:(k + 1) * P], ident[:, :])
                    last.then_inc(xn_transposed, 1)
                if n == 0:
                    pe.wait_ge(stage_loaded, 16 * 5)
                    t.transpose(bank[0][:, 0:32], stage[0:32, 0, :], ident[0:32, 0:32])
                    rows = CONV_K * CC
                    last = t.transpose(bank[0][:, 32:32 + rows], stage[0:rows, 1, :], ident[0:rows, 0:rows])
                    last.then_inc(stage_transposed, 1)
            pe.wait_ge(xnT_low_ready, 2 * NQ)
            pe.wait_ge(cols_ready, 1)

            def three_products(to, a_high, a_low, b_high, b_low, k):
                t.matmul(to, a_high, b_high, start=(k == 0), stop=False)
                t.matmul(to, a_high, b_low, start=False, stop=False)
                return t.matmul(to, a_low, b_high, start=False, stop=(k == KD - 1))

            for g in range(16):
                if g < 8:
                    pe.wait_ge(win_low_dve, g + 1)
                else:
                    pe.wait_ge(win_low_pool, g - 7)
                if 4 <= g < 12 and g % 2:
                    pe.wait_ge(glu_ready, 4 * ((g - 4) // 2 + 1))
                elif 4 <= g < 12:
                    pe.wait_ge(act_evac, (g - 4) // 2 + 1)
                elif g >= 12:
                    pe.wait_ge(act_evac, 4 + g - 12 + 1)
                _, high, low = split_parts(g)
                for k in range(KD):
                    last = three_products(bank[g % 4][:, :], high[:, k, :], low[:, k, :], xnT_high[:, k, :], xnT_low[:, k, :], k)
                last.then_inc(proj_done, 1)
            pe.wait_ge(win_low_pool, 12)
            for n in range(NQ):
                pe.wait_ge(act_evac, 8 + n + 1)
                tokens = slice(n * P, (n + 1) * P)
                for k in range(KD):
                    last = three_products(bank[n][:, :], xnT_high[:, k, tokens], xnT_low[:, k, tokens], v_high[:, k, :],
                                          win_low[4][:, k, :], k)
                last.then_inc(proj_done, 1)
            pe.wait_ge(conv_tap, CONV_K * CC)
            for c in range(CC):
                last = t.matmul(bank[4][:, :], mean_w[:, :], mixedT[:, c, :], start=(c == 0), stop=(c == CC - 1))
            last.then_inc(mean_done, 1)

            def qk(i):
                n, hd = steps[i]
                m0, m1 = keys_of(n)
                p0 = (hd % 2) * HEAD_DIM
                if i >= 2:
                    pe.wait_ge(s_ready, i - 1)
                t.matmul(bank[i % 2][:, 0:(m1 - m0) * P], qT[p0:p0 + HEAD_DIM, hd // 2, n * P:(n + 1) * P],
                         kT[p0:p0 + HEAD_DIM, hd // 2, m0 * P:m1 * P], start=True, stop=True).then_inc(qk_done, 1)

            def transpose_p(i):
                m0, m1 = keys_of(steps[i][0])
                pe.wait_ge(exp_ready, i + 1)
                if i >= 2:
                    pe.wait_ge(pT_act if i % 2 else pT_dve, i // 2)
                for m in range(m1 - m0):
                    last = t.transpose(bank[6 if i % 2 else 3][:, m * P:(m + 1) * P], P_sb[:, i % 3, m * P:(m + 1) * P], ident[:, :])
                last.then_inc(p_transposed, 1)

            def pv(i):
                n, hd = steps[i]
                m0, m1 = keys_of(n)
                pe.wait_ge(pT_act if i % 2 else pT_dve, i // 2 + 1)
                if hd == 0 and n >= 1:
                    pe.wait_ge(o_ready, n)
                for m in range(m0, m1):
                    last = t.matmul(bank[7][:, hd * HEAD_DIM:(hd + 1) * HEAD_DIM],
                                    PT_sb[:, i % 2, (m - m0) * P:(m - m0 + 1) * P],
                                    v_sb[:, m, hd * HEAD_DIM:(hd + 1) * HEAD_DIM], start=(m == m0), stop=(m == m1 - 1))
                last.then_inc(pv_done, 1)

            def transpose_o(n):
                pe.wait_ge(o_ready, n + 1)
                if n:
                    pe.wait_ge(oT_ready, n)
                for c in range(4):
                    last = t.transpose(bank[5][:, c * P:(c + 1) * P], O_sb[:, c * P:(c + 1) * P], ident[:, :])
                last.then_inc(o_transposed, 1)

            def project_out(n, half, attn):
                if attn:
                    pe.wait_ge(attn_low_ready, n + 1)
                elif n:
                    pe.wait_ge(h_ready, 2 * n - 1 + half)
                else:
                    pe.wait_ge(conv_low_ready, CC)
                    pe.wait_ge(wout_low_pool if half else wout_low_dve, 4)
                tokens = slice(n * P, (n + 1) * P)
                for k in range(4 * attn, 4 * attn + 4):
                    if attn:
                        high, low = attn_high[:, k - 4, tokens], attn_low[:, k - 4, tokens]
                    else:
                        high, low = conv_high[:, k, tokens], conv_low[k][:, tokens]
                    last = three_products(bank[OUT_BANKS[half]][:, :], high, low, wout_high[half][:, k, :], wout_low[half][:, k, :], k)
                if attn:
                    last.then_inc(wout_done, 1)

            pe.wait_ge(act_evac, 16)
            for i in range(NS + 5):
                if i < NS:
                    qk(i)
                if i == 1:
                    for c in range(CC):
                        pe.wait_ge(squared, c + 1)
                        t.matmul(bank[5][:, :], mean_w[:, :], sq[:, c % 2, :], start=(c == 0),
                                 stop=(c == CC - 1)).then_inc(var_part, 1)
                if 0 <= i - 2 < NS:
                    transpose_p(i - 2)
                if 0 <= i - 3 < NS:
                    pv(i - 3)
                if i >= 12 and (i - 12) % HEADS == 0:
                    transpose_o((i - 12) // HEADS)
                if (i - 10) % HEADS + 10 in PROJECT_AT and 10 <= i:
                    project_out((i - 10) // HEADS, *PROJECT_AT[(i - 10) % HEADS + 10])
            project_out(NQ - 1, 0, 1)
            project_out(NQ - 1, 1, 1)

            def route(n):
                pe.wait_ge(xn2_ready, n + 1)
                for half in range(2):
                    i = 2 * n + half
                    if i >= 3:
                        j = i - 3
                        pe.wait_ge(xn2T_act if j % 2 else xn2T_dve, j // 2 + 1)
                    for c in range(4):
                        k = 4 * half + c
                        last = t.transpose(bank[T_BANKS[i % 3]][:, c * P:(c + 1) * P], xn2[:, n, k * P:(k + 1) * P], ident[:, :])
                    last.then_inc(xn2_transposed, 1)
                if n:
                    pe.wait_ge(logits_ready, n)
                pe.wait_ge(xn2T_act, n + 1)
                pe.wait_ge(xn2T_dve, n + 1)
                for k in range(KD):
                    last = t.matmul(bank[7][:, n * 32:(n + 1) * 32], xn2T[n // 2][:, n % 2, k, :], wr[:, k, :],
                                    start=(k == 0), stop=(k == KD - 1))
                last.then_inc(logits_done, 1)

            pe.wait_ge(router_loaded, 32)
            for n in range(NQ):
                route(n)
            pe.wait_ge(chosen_ready, 1)
            for n in range(NQ):
                for m in range(n + 1):
                    last = t.matmul(bank[0][:, n * 32:(n + 1) * 32], (before_b if m == n else ones_b)[:, :], chosen[:, m, :],
                                    start=(m == 0), stop=(m == n))
            for m in range(NQ):
                last = t.matmul(bank[0][:, NQ * 32:NQ * 32 + 32], ones_b[:, :], chosen[:, m, :], start=(m == 0), stop=(m == NQ - 1))
            last.then_inc(rank_done, 1)
            pe.wait_ge(onehots_ready, 2)
            for i in range(NJ):
                last = t.matmul(bank[1][0:CAP, 0:COLS], pos_1h[:, i, :], blk_1h[:, i, :], start=(i == 0), stop=(i == NJ - 1))
            last.then_inc(table_done, 1)

            def transpose_x(b):
                pe.wait_ge(xg_loaded, 16 * (b + 1))
                for k in range(KD):
                    last = t.transpose(bank[6 + k // 4][:, (k % 4) * CAP:(k % 4 + 1) * CAP], xg[0:CAP, k * P:(k + 1) * P],
                                       ident[0:CAP, 0:CAP])
                last.then_inc(xg_transposed, 1)

            def transpose_h(b, half):
                pe.wait_ge(h_tok_ready, 2 * b + half + 1)
                for c in range(4):
                    last = t.transpose(bank[6 + half][:, c * CAP:(c + 1) * CAP], h_tok[:, half, c * P:(c + 1) * P],
                                       ident[0:CAP, 0:CAP])
                last.then_inc(h_transposed, 1)

            def three(to, high, low, i, at, k, stop):
                hi, lo = w_high[:, i % HIGH_RING, at:at + HALF], w_low[i][:, at:at + HALF]
                t.matmul(to, high[:, k, :], hi, start=False, stop=False)
                t.matmul(to, high[:, k, :], lo, start=False, stop=False)
                return t.matmul(to, low[:, k, :], hi, start=False, stop=stop)

            def pe_block(b):
                pe.wait_ge(xT_low_ready, 2 * (b + 1))
                pe.wait_ge(selector_ready, b + 1)
                for i in range(PIECES):
                    if i < 8:
                        to = bank[i // 2][0:CAP, :]
                        if i % 2 == 0:
                            rows, cols = 64 * (i // 2 % 2), HALF * (i // 4)
                            t.matmul(to, selector[rows:rows + 64, :], bias_gu[rows:rows + 64, cols:cols + HALF],
                                     start=True, stop=False)
                        wait_low(pe, b, i)
                        for k in range(4):
                            last = three(to, xT_high, xT_low, i, k * HALF, 4 * (i % 2) + k, i % 2 == 1 and k == 3)
                    else:
                        if i == 8:
                            for half in range(2):
                                t.matmul(bank[4 + half][0:CAP, :], selector[0:64, :], bias_d[0:64, half * HALF:(half + 1) * HALF],
                                         start=True, stop=False)
                        wait_low(pe, b, i)
                        if i % 2 == 0:
                            pe.wait_ge(hT_low_ready, 2 * b + (i - 8) // 2 + 1)
                        for k in range(2):
                            for half in range(2):
                                last = three(bank[4 + half][0:CAP, :], hT_high, hT_low, i, k * D_MODEL + half * HALF,
                                             2 * (i - 8) + k, i == PIECES - 1 and k == 1)
                    last.then_inc(piece_used, 1)
                    if i == 5:
                        transpose_h(b, 0)
                    if i == 8:
                        transpose_h(b, 1)
                    if i == 9:
                        pe.wait_ge(hT_low_ready, 2 * b + 2)
                        transpose_x(b + 1)

            transpose_x(0)
            pe.wait_ge(bias_split, 3)
            pe_block(0)
            with pe.Fori(1, N_EXPERTS) as b:
                pe_block(b)
            pe.wait_ge(overflow_ready, 2)
            trips = pe.value_load(n_ovf[0:1, 0:1], min_val=0, max_val=MAX_OVERFLOW)
            with pe.If(trips > 0):
                with pe.Fori(N_EXPERTS, trips + N_EXPERTS) as b:
                    pe_block(b)


_INS = ['x', 'g_mix', 'w_in', 'b_in', 'conv_w', 'conv_b', 'ln_g', 'ln_b', 'rpb', 'w_out', 'b_out', 'g_ffn',
        'w_router', 'b_router', 'w_gate', 'b_gate', 'w_up', 'b_up', 'w_down', 'b_down', 'g_final']


def kernel(**inputs):
    import numpy as _np
    import concourse.bacc as _bacc
    from concourse import mybir as _mybir
    from concourse.bass_utils import run_bass_kernel_spmd as _run

    nc = _bacc.Bacc("TRN2", target_bir_lowering=False, num_devices=1)
    arrays, args = {}, []
    for name in _INS:
        a = _np.ascontiguousarray(inputs[name])
        arrays[f"in_{name}"] = a
        args.append(nc.dram_tensor(f"in_{name}", a.shape, _mybir.dt.from_np(a.dtype), kind="ExternalInput").ap())
    args.append(nc.dram_tensor("out_0", (1, SEQ, D_MODEL), F32, kind="ExternalOutput").ap())
    encoder_kernel(nc, *args)
    r = _run(nc, [arrays], core_ids=[0])
    return r.results[0]["out_0"]
```
